# Optimizing a Trainium2 kernel written in Bass

```python
import math
import jax, jax.numpy as jnp
from jax import lax
import numpy as np

D_MODEL = 1024
BATCH = 1
SEQ = 256
DEPTH = 1

CHUNK = 64
Q_BLOCK = 128
EPS = 1e-6

MLSTM_HEADS = 4
MLSTM_HD = D_MODEL // MLSTM_HEADS
MLSTM_W = MLSTM_HEADS * MLSTM_HD
CONV_K = 4

DIFF_HEADS = 8
DIFF_HD = D_MODEL // (2 * DIFF_HEADS)
DIFF_W = DIFF_HEADS * 2 * DIFF_HD

RET_HEADS = 4
RET_HD = D_MODEL // RET_HEADS
RET_W = RET_HEADS * RET_HD

FFN_HIDDEN = -(-8 * D_MODEL // (3 * 256)) * 256

IN_SIZES = (MLSTM_W, MLSTM_W, MLSTM_W, MLSTM_W, MLSTM_HEADS, MLSTM_HEADS,
            DIFF_W, DIFF_W, DIFF_W,
            RET_W, RET_W, RET_W, RET_W,
            3 * D_MODEL)
N_IN = sum(IN_SIZES)


def rmsnorm(x, g):
    x32 = x.astype(jnp.float32)
    y = x32 * lax.rsqrt(jnp.mean(x32 * x32, axis=-1, keepdims=True) + EPS)
    return (y * g.astype(jnp.float32)).astype(x.dtype)

def head_rms(x):
    x32 = x.astype(jnp.float32)
    return x32 * lax.rsqrt(jnp.mean(x32 * x32, axis=-1, keepdims=True) + EPS)

def causal_dwconv(x, w):
    K = w.shape[0]
    S = x.shape[1]
    xp = jnp.pad(x, ((0, 0), (K - 1, 0), (0, 0)))
    out = xp[:, 0:S] * w[0]
    for j in range(1, K):
        out = out + xp[:, j:j + S] * w[j]
    return out

def to_chunks(a):
    B, S = a.shape[0], a.shape[1]
    return jnp.moveaxis(a.reshape(B, S // CHUNK, CHUNK, *a.shape[2:]), 1, 0)

def from_chunks(a):
    a = jnp.moveaxis(a, 0, 1)
    return a.reshape(a.shape[0], a.shape[1] * a.shape[2], *a.shape[3:])

def mlstm(q, k, v, i_pre, f_pre):
    B, S, H, dh = q.shape
    f32 = jnp.float32
    q = q.astype(f32)
    k = k.astype(f32) * (dh ** -0.5)
    v = v.astype(f32)
    logf = jax.nn.log_sigmoid(f_pre.astype(f32))
    ig = i_pre.astype(f32)
    causal = jnp.tril(jnp.ones((CHUNK, CHUNK), dtype=bool))

    def step(carry, inp):
        C, n, m = carry
        qj, kj, vj, lf, igj = inp
        b = jnp.cumsum(lf, axis=1).transpose(0, 2, 1)
        igT = igj.transpose(0, 2, 1)
        g = b[..., -1]
        d_intra = b[..., :, None] - b[..., None, :] + igT[..., None, :]
        d_intra = jnp.where(causal, d_intra, -jnp.inf)
        d_inter = b + m[..., None]
        m_row = jnp.maximum(jnp.max(d_intra, axis=-1), d_inter)
        w_intra = jnp.exp(d_intra - m_row[..., None])
        w_inter = jnp.exp(d_inter - m_row)
        s = jnp.einsum('blhd,bshd->bhls', qj, kj) * w_intra
        w_int_t = w_inter.transpose(0, 2, 1)[..., None]
        num = (jnp.einsum('bhls,bshe->blhe', s, vj)
               + jnp.einsum('blhd,bhde->blhe', qj, C) * w_int_t)
        den = jnp.sum(s, axis=-1) + jnp.einsum('blhd,bhd->bhl', qj, n) * w_inter
        den = jnp.maximum(jnp.abs(den), jnp.exp(-m_row))
        h = num / den.transpose(0, 2, 1)[..., None]
        a = g[..., None] - b + igT
        m_new = jnp.maximum(g + m, jnp.max(a, axis=-1))
        w_old = jnp.exp(g + m - m_new)
        w_k = jnp.exp(a - m_new[..., None])
        C_new = w_old[..., None, None] * C + jnp.einsum('bhs,bshd,bshe->bhde', w_k, kj, vj)
        n_new = w_old[..., None] * n + jnp.einsum('bhs,bshd->bhd', w_k, kj)
        return (C_new, n_new, m_new), h

    init = (jnp.zeros((B, H, dh, dh), f32), jnp.zeros((B, H, dh), f32), jnp.zeros((B, H), f32))
    xs = (to_chunks(q), to_chunks(k), to_chunks(v), to_chunks(logf), to_chunks(ig))
    _, hs = lax.scan(step, init, xs)
    return from_chunks(hs)

def retention(q, k, v):
    B, S, H, dh = q.shape
    f32 = jnp.float32
    q = q.astype(f32)
    k = k.astype(f32) * (dh ** -0.5)
    v = v.astype(f32)
    log_gamma = jnp.log(1.0 - 2.0 ** (-5.0 - jnp.arange(H, dtype=f32)))
    pos = jnp.arange(CHUNK, dtype=f32)
    rel = pos[:, None] - pos[None, :]
    dmask = jnp.where(rel[None] >= 0, jnp.exp(log_gamma[:, None, None] * jnp.maximum(rel, 0.0)[None]), 0.0)
    xi = jnp.exp(log_gamma[None, :] * (pos[:, None] + 1.0))
    zeta = jnp.exp(log_gamma[:, None] * (CHUNK - 1.0 - pos[None, :]))
    chunk_decay = jnp.exp(log_gamma * CHUNK)

    def step(R, inp):
        qj, kj, vj = inp
        s = jnp.einsum('blhd,bshd->bhls', qj, kj) * dmask[None]
        o = (jnp.einsum('bhls,bshe->blhe', s, vj)
             + jnp.einsum('blhd,bhde->blhe', qj, R) * xi[None, :, :, None])
        R_new = chunk_decay[None, :, None, None] * R + jnp.einsum('hs,bshd,bshe->bhde', zeta, kj, vj)
        return R_new, o

    R0 = jnp.zeros((B, H, dh, dh), f32)
    _, os_ = lax.scan(step, R0, (to_chunks(q), to_chunks(k), to_chunks(v)))
    return from_chunks(os_)

def diff_attention(q, k, v, lam):
    B, S, H, _, dh = q.shape
    f32 = jnp.float32
    q = q.astype(f32) * (dh ** -0.5)
    k = k.astype(f32)
    v = v.astype(f32)
    slopes = 2.0 ** (-8.0 * (jnp.arange(H, dtype=f32) + 1.0) / H)
    outs = []
    for blk in range(S // Q_BLOCK):
        q0 = blk * Q_BLOCK
        kend = q0 + Q_BLOCK
        qb = q[:, q0:kend]
        kb = k[:, :kend]
        vb = v[:, :kend]
        s = jnp.einsum('bqhcd,bkhcd->bhcqk', qb, kb)
        tq = jnp.arange(q0, kend)
        tk = jnp.arange(kend)
        dist = jnp.abs(tq[:, None] - tk[None, :]).astype(f32)
        allowed = (tk // CHUNK)[None, :] <= (tq // CHUNK)[:, None]
        bias = -slopes[:, None, None] * dist[None]
        s = jnp.where(allowed, s + bias[None, :, None], -jnp.inf)
        p = jax.nn.softmax(s, axis=-1)
        a = p[:, :, 0] - lam * p[:, :, 1]
        outs.append(jnp.einsum('bhqk,bkhe->bqhe', a, vb))
    return jnp.concatenate(outs, axis=1)

def split_in(proj):
    idx = np.cumsum(np.array(IN_SIZES))[:-1].tolist()
    return jnp.split(proj, idx, axis=-1)

def first_inputs(seed: int = 0) -> dict:
    key = jax.random.key(seed)
    ks = jax.random.split(key, 16)
    f32 = jnp.float32

    def nrm(kk, shape, scale):
        return jax.random.normal(kk, shape, f32) * scale

    x = nrm(ks[0], (BATCH, SEQ, D_MODEL), 1.0)
    norm_gains = 1.0 + nrm(ks[1], (DEPTH, 4, D_MODEL), 0.05)
    w_in = nrm(ks[2], (DEPTH, D_MODEL, N_IN), D_MODEL ** -0.5)
    mlstm_conv = nrm(ks[3], (DEPTH, CONV_K, 2 * MLSTM_W), CONV_K ** -0.5)
    f_bias = jnp.broadcast_to(jnp.linspace(3.0, 6.0, MLSTM_HEADS, dtype=f32), (DEPTH, MLSTM_HEADS))
    i_bias = jnp.zeros((DEPTH, MLSTM_HEADS), f32)
    mlstm_gate_bias = jnp.stack([i_bias, f_bias], axis=1) + nrm(ks[4], (DEPTH, 2, MLSTM_HEADS), 0.1)
    diff_lambda = nrm(ks[5], (DEPTH, 4, DIFF_HD), 0.1)
    diff_subln = 1.0 + nrm(ks[6], (DEPTH, 2 * DIFF_HD), 0.05)
    w_mlstm_out = nrm(ks[7], (DEPTH, MLSTM_W, D_MODEL), MLSTM_W ** -0.5)
    w_diff_out = nrm(ks[8], (DEPTH, DIFF_W, D_MODEL), DIFF_W ** -0.5)
    w_ret_out = nrm(ks[9], (DEPTH, RET_W, D_MODEL), RET_W ** -0.5)
    w_out = nrm(ks[10], (DEPTH, D_MODEL, D_MODEL), D_MODEL ** -0.5)
    w_ffn_in = nrm(ks[11], (DEPTH, D_MODEL, 2 * FFN_HIDDEN), D_MODEL ** -0.5)
    w_ffn_out = nrm(ks[12], (DEPTH, FFN_HIDDEN, D_MODEL), FFN_HIDDEN ** -0.5)
    return {"x": x, "norm_gains": norm_gains, "w_in": w_in, "mlstm_conv": mlstm_conv,
            "mlstm_gate_bias": mlstm_gate_bias, "diff_lambda": diff_lambda,
            "diff_subln": diff_subln, "w_mlstm_out": w_mlstm_out, "w_diff_out": w_diff_out,
            "w_ret_out": w_ret_out, "w_out": w_out, "w_ffn_in": w_ffn_in,
            "w_ffn_out": w_ffn_out}

def first_block(x, norm_gains, w_in, mlstm_conv, mlstm_gate_bias, diff_lambda, diff_subln,
              w_mlstm_out, w_diff_out, w_ret_out, w_out, w_ffn_in, w_ffn_out):
    B, S, _ = x.shape
    f32 = jnp.float32
    for l in range(DEPTH):
        g = norm_gains[l]
        h = rmsnorm(x, g[0])
        proj = h @ w_in[l]
        (mq, mk, mv, mo, mi, mf, dq, dk, dv, rq, rk, rv, rg, gates) = split_in(proj)

        qk = jax.nn.silu(causal_dwconv(jnp.concatenate([mq, mk], axis=-1), mlstm_conv[l]))
        mq_c, mk_c = jnp.split(qk, 2, axis=-1)
        hm = mlstm(mq_c.reshape(B, S, MLSTM_HEADS, MLSTM_HD),
                   mk_c.reshape(B, S, MLSTM_HEADS, MLSTM_HD),
                   mv.reshape(B, S, MLSTM_HEADS, MLSTM_HD),
                   mi + mlstm_gate_bias[l, 0],
                   mf + mlstm_gate_bias[l, 1])
        hm = jax.nn.sigmoid(mo.astype(f32)) * head_rms(hm).reshape(B, S, MLSTM_W)

        lam_init = 0.8 - 0.6 * math.exp(-0.3 * l)
        lmb = diff_lambda[l].astype(f32)
        lam = jnp.exp(jnp.sum(lmb[0] * lmb[1])) - jnp.exp(jnp.sum(lmb[2] * lmb[3])) + lam_init
        hd = diff_attention(dq.reshape(B, S, DIFF_HEADS, 2, DIFF_HD),
                            dk.reshape(B, S, DIFF_HEADS, 2, DIFF_HD),
                            dv.reshape(B, S, DIFF_HEADS, 2 * DIFF_HD), lam)
        hd = (rmsnorm(hd, diff_subln[l]) * (1.0 - lam_init)).reshape(B, S, DIFF_W)

        hr = retention(rq.reshape(B, S, RET_HEADS, RET_HD),
                       rk.reshape(B, S, RET_HEADS, RET_HD),
                       rv.reshape(B, S, RET_HEADS, RET_HD))
        hr = jax.nn.silu(rg.astype(f32)) * head_rms(hr).reshape(B, S, RET_W)

        gm, gd, gr = jnp.split(jax.nn.sigmoid(gates), 3, axis=-1)
        y = (gm * (hm.astype(x.dtype) @ w_mlstm_out[l])
             + gd * (hd.astype(x.dtype) @ w_diff_out[l])
             + gr * (hr.astype(x.dtype) @ w_ret_out[l]))
        y = y @ w_out[l]
        x = x + rmsnorm(y, g[1])

        h2 = rmsnorm(x, g[2])
        a, u = jnp.split(h2 @ w_ffn_in[l], 2, axis=-1)
        f = (jax.nn.silu(a) * u) @ w_ffn_out[l]
        x = x + rmsnorm(f, g[3])
    return x


DEPTH_2 = 2

GRID_W = 64
CTX_LEN = 256
N_MIXERS = 2
N_A = (DEPTH_2 + 1) // 2
N_B = DEPTH_2 // 2
D_MIX = D_MODEL
CHUNK_2 = 128
CM_GROUPS = 8
CM_GROUP_DIM = D_MIX // CM_GROUPS
SSM_GROUP = 16
SSM_GROUPS = D_MIX // SSM_GROUP
SSM_STATE = 64
PEER_HEADS = 8
PEER_KEYS = 128
PEER_EXPERTS = PEER_KEYS * PEER_KEYS
PEER_TOPK = 16
PEER_DKEY = 512
PEER_DHALF = PEER_DKEY // 2
PEER_BLOCK = 128
N_MOD = 6


def _rmsnorm(x, g):
    x32 = x.astype(jnp.float32)
    y = x32 * lax.rsqrt(jnp.mean(x32 * x32, axis=-1, keepdims=True) + EPS)
    return (y * g.astype(jnp.float32)).astype(x.dtype)

def _layernorm(x, g, b):
    x32 = x.astype(jnp.float32)
    mu = jnp.mean(x32, axis=-1, keepdims=True)
    xc = x32 - mu
    y = xc * lax.rsqrt(jnp.mean(xc * xc, axis=-1, keepdims=True) + EPS)
    return (y * g.astype(jnp.float32) + b.astype(jnp.float32)).astype(x.dtype)

def _modulate(h, shift, scale):
    return h * (1.0 + scale) + shift

def _sincos_1d(pos, dim):
    omega = 1.0 / (10000.0 ** (jnp.arange(dim // 2, dtype=jnp.float32) / (dim // 2)))
    ang = pos[:, None] * omega[None, :]
    return jnp.concatenate([jnp.sin(ang), jnp.cos(ang)], axis=-1)

def _pos_embed_2d(rows, dim):
    r = jnp.repeat(jnp.arange(rows, dtype=jnp.float32), GRID_W)
    col = jnp.tile(jnp.arange(GRID_W, dtype=jnp.float32), rows)
    return jnp.concatenate([_sincos_1d(r, dim // 2), _sincos_1d(col, dim // 2)], axis=-1)

def _chunk_mixer(h, w_in, ln_g, ln_b, w_s, b_s, w_out):
    bsz, length, _ = h.shape
    z = jax.nn.gelu(h @ w_in)
    u, v = jnp.split(z, 2, axis=-1)
    v = _layernorm(v, ln_g, ln_b)
    v = v.reshape(bsz, length // CHUNK_2, CHUNK_2, CM_GROUPS, CM_GROUP_DIM)
    v = jnp.einsum("hpq,bnqhd->bnphd", w_s, v) + b_s.T[:, :, None]
    return (u * v.reshape(bsz, length, D_MIX)) @ w_out

def _cmul(ar, ai, br, bi):
    return ar * br - ai * bi, ar * bi + ai * br

def _scan_combine(e1, e2):
    a1r, a1i, b1r, b1i = e1
    a2r, a2i, b2r, b2i = e2
    ar, ai = _cmul(a2r, a2i, a1r, a1i)
    br, bi = _cmul(a2r, a2i, b1r, b1i)
    return ar, ai, br + b2r, bi + b2i

def _diag_scan(a_r, a_i, bu_r, bu_i, h0=None):
    if h0 is not None:
        inj_r, inj_i = _cmul(a_r, a_i, h0[0], h0[1])
        bu_r = bu_r.at[0].add(inj_r)
        bu_i = bu_i.at[0].add(inj_i)
    a_full_r = jnp.broadcast_to(a_r, bu_r.shape)
    a_full_i = jnp.broadcast_to(a_i, bu_i.shape)
    _, _, h_r, h_i = lax.associative_scan(_scan_combine, (a_full_r, a_full_i, bu_r, bu_i), axis=0)
    return h_r, h_i

def _ssm_direction(u_lat, u_ctx, a_r, a_i, bb_r, bb_i, c_r, c_i, need_ctx_out):
    def inject(u):
        return (jnp.einsum("lgc,gpc->lgp", u, bb_r), jnp.einsum("lgc,gpc->lgp", u, bb_i))

    def readout(h_r, h_i):
        return jnp.einsum("lgp,gcp->lgc", h_r, c_r) - jnp.einsum("lgp,gcp->lgc", h_i, c_i)

    hc_r, hc_i = _diag_scan(a_r, a_i, *inject(u_ctx))
    hx_r, hx_i = _diag_scan(a_r, a_i, *inject(u_lat), h0=(hc_r[-1], hc_i[-1]))
    if need_ctx_out:
        return readout(hx_r, hx_i), readout(hc_r, hc_i)
    return readout(hx_r, hx_i), None

def _ssm_mixer(xn, cn, w_in, lam_re, lam_im, log_step, b_re, b_im, c_re, c_im, d_skip, w_out,
               need_ctx_out):
    u_x = xn @ w_in
    u_c = cn @ w_in
    lr = lam_re.astype(jnp.float32)
    li = lam_im.astype(jnp.float32)
    step = jnp.exp(log_step.astype(jnp.float32))[..., None]
    mag = jnp.exp(lr * step)
    a_r = mag * jnp.cos(li * step)
    a_i = mag * jnp.sin(li * step)
    den = lr * lr + li * li
    coef_r = ((a_r - 1.0) * lr + a_i * li) / den
    coef_i = (a_i * lr - (a_r - 1.0) * li) / den
    bb_r, bb_i = _cmul(coef_r[..., None], coef_i[..., None],
                       b_re.astype(jnp.float32), b_im.astype(jnp.float32))
    c_r = c_re.astype(jnp.float32)
    c_i = c_im.astype(jnp.float32)

    def per_sample(args):
        ux, uc = args
        ux = ux.astype(jnp.float32).reshape(-1, SSM_GROUPS, SSM_GROUP)
        uc = uc.astype(jnp.float32).reshape(-1, SSM_GROUPS, SSM_GROUP)
        yf_x, yf_c = _ssm_direction(ux, uc, a_r[0], a_i[0], bb_r[0], bb_i[0], c_r[0], c_i[0],
                                    need_ctx_out)
        yb_x, yb_c = _ssm_direction(ux[::-1], uc[::-1], a_r[1], a_i[1], bb_r[1], bb_i[1],
                                    c_r[1], c_i[1], need_ctx_out)
        y_lat = yf_x + yb_x[::-1]
        if need_ctx_out:
            return y_lat, yf_c + yb_c[::-1]
        return y_lat

    out = lax.map(per_sample, (u_x, u_c))

    def finish(y, u):
        y = y.reshape(u.shape).astype(u.dtype) + d_skip * u
        val, gate = jnp.split(jax.nn.gelu(y) @ w_out, 2, axis=-1)
        return val * jax.nn.sigmoid(gate)

    if need_ctx_out:
        return finish(out[0], u_x), finish(out[1], u_c)
    return finish(out, u_x), None

def _peer(h, w_q, sub_keys, u_tab, v_tab):
    shape = h.shape
    blocks = h.reshape(-1, PEER_BLOCK, D_MODEL)

    def block(hb):
        q = (hb @ w_q).reshape(PEER_BLOCK, PEER_HEADS, 2, PEER_DHALF)
        s = jnp.einsum("nhkd,hkmd->nhkm", q.astype(jnp.float32), sub_keys.astype(jnp.float32))
        s_half, i_half = lax.top_k(s, PEER_TOPK)
        cand = s_half[:, :, 0, :, None] + s_half[:, :, 1, None, :]
        top_s, top_c = lax.top_k(cand.reshape(PEER_BLOCK, PEER_HEADS, PEER_TOPK * PEER_TOPK),
                                 PEER_TOPK)
        k1 = jnp.take_along_axis(i_half[:, :, 0], top_c // PEER_TOPK, axis=-1)
        k2 = jnp.take_along_axis(i_half[:, :, 1], top_c % PEER_TOPK, axis=-1)
        ids = k1 * PEER_KEYS + k2
        g = jax.nn.softmax(top_s, axis=-1)
        ue = jnp.take(u_tab, ids, axis=0)
        ve = jnp.take(v_tab, ids, axis=0)
        act = jax.nn.gelu(jnp.einsum("nd,nhkd->nhk", hb, ue).astype(jnp.float32))
        return jnp.einsum("nhk,nhkd->nd", (g * act).astype(hb.dtype), ve)

    return lax.map(block, blocks).reshape(shape)

def second_inputs(seed: int = 0) -> dict:
    key = jax.random.key(seed)
    ks = jax.random.split(key, 32)
    f32 = jnp.float32
    nrm = lambda k, s, std: jax.random.normal(k, s, f32) * std
    G, P = SSM_GROUPS, SSM_STATE
    lam_im0 = jnp.broadcast_to(jnp.pi * jnp.arange(P, dtype=f32), (N_B, 2, G, P))
    return {
        "x": nrm(ks[0], (BATCH, SEQ, D_MODEL), 1.0),
        "c": nrm(ks[1], (BATCH, D_MODEL), 1.0),
        "ctx": nrm(ks[2], (BATCH, CTX_LEN, D_MODEL), 1.0),
        "c_ctx": nrm(ks[3], (D_MODEL,), 1.0),
        "ada_w": nrm(ks[4], (DEPTH_2, D_MODEL, N_MOD * D_MODEL), 0.5 * D_MODEL ** -0.5),
        "ada_b": nrm(ks[5], (DEPTH_2, N_MOD * D_MODEL), 0.02),
        "norm1_g": 1.0 + nrm(ks[6], (DEPTH_2, D_MODEL), 0.02),
        "norm2_g": 1.0 + nrm(ks[7], (DEPTH_2, D_MODEL), 0.02),
        "final_g": 1.0 + nrm(ks[8], (D_MODEL,), 0.02),
        "cm_w_in": nrm(ks[9], (N_A, D_MODEL, 2 * D_MIX), D_MODEL ** -0.5),
        "cm_ln_g": 1.0 + nrm(ks[10], (N_A, D_MIX), 0.02),
        "cm_ln_b": nrm(ks[11], (N_A, D_MIX), 0.02),
        "cm_w_s": nrm(ks[12], (N_A, CM_GROUPS, CHUNK_2, CHUNK_2), CHUNK_2 ** -0.5),
        "cm_b_s": 1.0 + nrm(ks[13], (N_A, CM_GROUPS, CHUNK_2), 0.02),
        "cm_w_out": nrm(ks[14], (N_A, D_MIX, D_MODEL), D_MIX ** -0.5),
        "ssm_w_in": nrm(ks[15], (N_B, D_MODEL, D_MIX), D_MODEL ** -0.5),
        "ssm_lam_re": -0.5 + nrm(ks[16], (N_B, 2, G, P), 0.01),
        "ssm_lam_im": lam_im0 + nrm(ks[17], (N_B, 2, G, P), 0.01),
        "ssm_log_step": jax.random.uniform(ks[18], (N_B, 2, G), f32,
                                           minval=math.log(1e-3), maxval=math.log(1e-1)),
        "ssm_b_re": nrm(ks[19], (N_B, 2, G, P, SSM_GROUP), (2 * SSM_GROUP) ** -0.5),
        "ssm_b_im": nrm(ks[20], (N_B, 2, G, P, SSM_GROUP), (2 * SSM_GROUP) ** -0.5),
        "ssm_c_re": nrm(ks[21], (N_B, 2, G, SSM_GROUP, P), P ** -0.5),
        "ssm_c_im": nrm(ks[22], (N_B, 2, G, SSM_GROUP, P), P ** -0.5),
        "ssm_d": nrm(ks[23], (N_B, D_MIX), 1.0),
        "ssm_w_out": nrm(ks[24], (N_B, D_MIX, 2 * D_MODEL), D_MIX ** -0.5),
        "peer_w_q": nrm(ks[25], (DEPTH_2, D_MODEL, PEER_HEADS * PEER_DKEY), D_MODEL ** -0.5),
        "peer_keys": nrm(ks[26], (DEPTH_2, PEER_HEADS, 2, PEER_KEYS, PEER_DHALF), PEER_DHALF ** -0.5),
        "peer_u": nrm(ks[27], (DEPTH_2, PEER_EXPERTS, D_MODEL), D_MODEL ** -0.5),
        "peer_v": nrm(ks[28], (DEPTH_2, PEER_EXPERTS, D_MODEL), (PEER_HEADS * PEER_TOPK) ** -0.5),
    }

def second_block(x, c, ctx, c_ctx, ada_w, ada_b, norm1_g, norm2_g, final_g,
              cm_w_in, cm_ln_g, cm_ln_b, cm_w_s, cm_b_s, cm_w_out,
              ssm_w_in, ssm_lam_re, ssm_lam_im, ssm_log_step, ssm_b_re, ssm_b_im,
              ssm_c_re, ssm_c_im, ssm_d, ssm_w_out,
              peer_w_q, peer_keys, peer_u, peer_v):
    rows = x.shape[1] // GRID_W
    x = x + _pos_embed_2d(rows, D_MODEL).astype(x.dtype)[None]
    h_ctx = ctx
    silu_c = jax.nn.silu(c)
    silu_cc = jax.nn.silu(c_ctx)
    for i in range(DEPTH_2):
        last = i == DEPTH_2 - 1
        k = i // N_MIXERS
        use_chunk = (i % N_MIXERS) == 0
        need_ctx_mix = (not last) or (not use_chunk)
        mod_x = (silu_c @ ada_w[i] + ada_b[i])[:, None, :]
        mod_c = (silu_cc @ ada_w[i] + ada_b[i])[None, None, :]
        sh1, sc1, g1, sh2, sc2, g2 = jnp.split(mod_x, N_MOD, axis=-1)
        csh1, csc1, cg1, csh2, csc2, cg2 = jnp.split(mod_c, N_MOD, axis=-1)

        xn = _modulate(_rmsnorm(x, norm1_g[i]), sh1, sc1)
        cn = _modulate(_rmsnorm(h_ctx, norm1_g[i]), csh1, csc1) if need_ctx_mix else None
        if use_chunk:
            y_x = _chunk_mixer(xn, cm_w_in[k], cm_ln_g[k], cm_ln_b[k], cm_w_s[k], cm_b_s[k],
                               cm_w_out[k])
            y_c = None if last else _chunk_mixer(cn, cm_w_in[k], cm_ln_g[k], cm_ln_b[k],
                                                 cm_w_s[k], cm_b_s[k], cm_w_out[k])
        else:
            y_x, y_c = _ssm_mixer(xn, cn, ssm_w_in[k], ssm_lam_re[k], ssm_lam_im[k],
                                  ssm_log_step[k], ssm_b_re[k], ssm_b_im[k], ssm_c_re[k],
                                  ssm_c_im[k], ssm_d[k], ssm_w_out[k], not last)
        x = x + g1 * y_x
        x = x + g2 * _peer(_modulate(_rmsnorm(x, norm2_g[i]), sh2, sc2),
                           peer_w_q[i], peer_keys[i], peer_u[i], peer_v[i])
        if not last:
            h_ctx = h_ctx + cg1 * y_c
            h_ctx = h_ctx + cg2 * _peer(_modulate(_rmsnorm(h_ctx, norm2_g[i]), csh2, csc2),
                                        peer_w_q[i], peer_keys[i], peer_u[i], peer_v[i])
    return _rmsnorm(x, final_g)


def setup_inputs(seed=0):
    out = dict(first_inputs(seed))
    for name, value in second_inputs(seed + 1).items():
        if name != "x":
            out[name + "_2"] = value
    return out


def reference(
    x, norm_gains, w_in, mlstm_conv, mlstm_gate_bias, diff_lambda, diff_subln, w_mlstm_out,
    w_diff_out, w_ret_out, w_out, w_ffn_in, w_ffn_out, c_2, ctx_2, c_ctx_2, ada_w_2, ada_b_2,
    norm1_g_2, norm2_g_2, final_g_2, cm_w_in_2, cm_ln_g_2, cm_ln_b_2, cm_w_s_2, cm_b_s_2,
    cm_w_out_2, ssm_w_in_2, ssm_lam_re_2, ssm_lam_im_2, ssm_log_step_2, ssm_b_re_2, ssm_b_im_2,
    ssm_c_re_2, ssm_c_im_2, ssm_d_2, ssm_w_out_2, peer_w_q_2, peer_keys_2, peer_u_2, peer_v_2,
):
    x = first_block(
        x, norm_gains, w_in, mlstm_conv, mlstm_gate_bias, diff_lambda, diff_subln, w_mlstm_out,
        w_diff_out, w_ret_out, w_out, w_ffn_in, w_ffn_out,
    )
    return second_block(
        x, c_2, ctx_2, c_ctx_2, ada_w_2, ada_b_2, norm1_g_2, norm2_g_2, final_g_2, cm_w_in_2,
        cm_ln_g_2, cm_ln_b_2, cm_w_s_2, cm_b_s_2, cm_w_out_2, ssm_w_in_2, ssm_lam_re_2,
        ssm_lam_im_2, ssm_log_step_2, ssm_b_re_2, ssm_b_im_2, ssm_c_re_2, ssm_c_im_2, ssm_d_2,
        ssm_w_out_2, peer_w_q_2, peer_keys_2, peer_u_2, peer_v_2,
    )


_drawn_inputs = setup_inputs


def setup_inputs(seed=0):
    import zlib

    import numpy as np

    out = dict(_drawn_inputs(seed))
    spreads = {}
    factors = {'ctx_2': 64.0,
     'c_ctx_2': 64.0,
     'ada_b_2': 4.336,
     'norm1_g_2': 8.0,
     'norm2_g_2': 8.0,
     'final_g_2': 7.388,
     'cm_ln_g_2': 8.0,
     'cm_ln_b_2': 8.0,
     'cm_b_s_2': 8.0,
     'ssm_lam_re_2': 64.0,
     'ssm_lam_im_2': 44.328,
     'ssm_log_step_2': 56.384,
     'ssm_b_re_2': 64.0,
     'ssm_b_im_2': 64.0,
     'ssm_c_re_2': 64.0,
     'ssm_c_im_2': 64.0,
     'peer_w_q_2': 5.151,
     'peer_keys_2': 5.132,
     'peer_u_2': 5.716,
     'peer_v_2': 5.097}
    for name, (base, spread) in spreads.items():
        noise = np.random.default_rng([zlib.crc32(name.encode()), seed]).standard_normal(out[name].shape)
        drawn = base * np.exp(spread * noise) if base else spread * noise
        out[name] = __import__('jax').numpy.asarray(drawn.astype(out[name].dtype))
    for name, factor in factors.items():
        out[name] = (out[name] * factor).astype(out[name].dtype)
    return out
```

```python
from contextlib import ExitStack

import numpy as np

import concourse.bass as bass
from concourse import mybir

F32 = mybir.dt.float32
F32R = mybir.dt.float32r
BF16 = mybir.dt.bfloat16
U32 = mybir.dt.uint32
ALU = mybir.AluOpType
ACT = mybir.ActivationFunctionType
AX_X = mybir.AxisListType.X

P = 128
D = 1024
KT = D // P
SEQ = 256
NX = SEQ // P
NT = 2 * NX
HALF = 512
BANKS = 8
RING = 4
BODY = 8
FFN = 2816
FT = FFN // P
EPS = 1e-6
HEADS = 4
HD = 256
DH = 8
DCOLS = 384
NEG = -3.0e38
PH = 8
TOPK = 16
KEYS = 128
PAIRS = PH * TOPK
PHASES = 2
K1 = KEYS // PHASES
OH = 4
LEVELS = 9
SEED = 5
SPAD = 68
STILES = 64
CG = 16
LAM_INIT = 0.8 - 0.6 * float(np.exp(-0.3 * 0))
TWO_PI = 2.0 * float(np.pi)
ROUND = 1.5 * 2.0 ** 23

COLS = {}
_at = 0
for _name, _n in (("g0", KT), ("g2", KT), ("n1_0", KT), ("n1_1", KT), ("n2_0", KT), ("n2_1", KT), ("ssm_d", KT),
                  ("ada_b0", 48), ("ada_b1", 48), ("conv", 64), ("bs", 8), ("ibias", 1), ("fbias", 1),
                  ("c", KT), ("cc", KT)):
    COLS[_name] = (_at, _at + _n)
    _at += _n
NCOLS = _at


class Segment:

    def __init__(self, ap, start):
        self.ap, self.start, self.n = ap, start, ap.shape[0]
        self.whole = False


def run_units(eng, n, body):
    rounds = (n - 1) // BODY
    if rounds > 1:
        with eng.Fori(0, rounds, 1) as it:
            for j in range(BODY):
                body(it, j, False)
    elif rounds == 1:
        for j in range(BODY):
            body(0, j, False)
    rest = n - rounds * BODY
    for j in range(rest):
        body(rounds, j, j == rest - 1)


class Split:

    def __init__(self, nc, ctx, name, shape):
        self.hi = ctx.enter_context(nc.sbuf_tensor(f"{name}_hi", shape, F32R))
        self.lo = ctx.enter_context(nc.sbuf_tensor(f"{name}_lo", shape, F32R))

    def parts(self, *at):
        return self.hi[at], self.lo[at]


def minus_hi(eng, out, x, hi):
    return eng.tensor_tensor(out, x, hi.bitcast(F32), ALU.subtract)


def three_passes(pe, out, lhs, rhs, start, stop, **more):
    pe.matmul(out, lhs[0], rhs[0], start=start, stop=False, **more)
    pe.matmul(out, lhs[0], rhs[1], start=False, stop=False, **more)
    return pe.matmul(out, lhs[1], rhs[0], start=False, stop=stop, **more)


class Chain:

    def __init__(self, eng, sem):
        self.eng, self.sem, self.k = eng, sem, 0

    def __call__(self, ins):
        self.k = self.k + 1
        ins.then_inc(self.sem, 1)
        self.eng.wait_ge(self.sem, self.k)

    def wait(self):
        self.eng.wait_ge(self.sem, self.k)

    def mark(self, ins):
        self.k = self.k + 1
        ins.then_inc(self.sem, 1)

    def loop(self, n, per, body):
        base = self.k
        with self.eng.Fori(0, n, 1) as i:
            self.k = base + i * per
            self.count = 0
            before = self.k
            steps = [0]
            inner = _Inner(self, before, steps)
            body(i, inner)
            assert steps[0] == per, (steps[0], per)
        self.k = base + n * per


class _Inner:
    def __init__(self, chain, base, steps):
        self.chain, self.base, self.steps = chain, base, steps

    def mark(self, ins):
        self.steps[0] += 1
        ins.then_inc(self.chain.sem, 1)

    def wait(self):
        self.chain.eng.wait_ge(self.chain.sem, self.base + self.steps[0])

    def __call__(self, ins):
        self.mark(ins)
        self.wait()


class Core:

    def __init__(self, nc, ctx):
        self.nc, self.ctx = nc, ctx
        self.loaded = [ctx.enter_context(nc.semaphore(f"slot{i}_loaded")) for i in range(RING)]
        self.units_done = ctx.enter_context(nc.semaphore("units_done"))
        self.hi_done = ctx.enter_context(nc.semaphore("unit_hi_done"))
        self.split_done = ctx.enter_context(nc.semaphore("unit_split_done"))
        self.dma_done = ctx.enter_context(nc.semaphore("small_dma_done"))
        self.dma_count = 0
        self.pools = [[ctx.enter_context(nc.semaphore(f"stage{k}_{i}")) for i in range(12)] for k in range(2)]
        self.turn = 0
        self.segments = []

    def stage(self):
        return Stage(self)

    def feed(self, sp, k):
        seg = self.segments[k]

        def load(it, j, last):
            sp.wait_ge(self.split_done, seg.start + it * BODY + j + 1)
            slot = (seg.start + j) % RING
            sp.dma_start(self.ring[:, slot, :], seg.ap[it * BODY + j + RING]).then_inc(self.loaded[slot], 16)

        run_units(sp, seg.n - RING, load)
        if k + 1 < len(self.segments):
            nxt = self.segments[k + 1]
            for v in range(RING):
                sp.wait_ge(self.split_done, nxt.start + v - RING + 1)
                slot = (nxt.start + v) % RING
                sp.dma_start(self.ring[:, slot, :], nxt.ap[v]).then_inc(self.loaded[slot], 16)

    def split_hi(self, act, g, it):
        act.wait_ge(self.loaded[g % RING], 16 * (g // RING + 1) + it * (16 * BODY // RING))
        act.wait_ge(self.units_done, g + 1 + it * BODY)
        act.activation(self.unit.hi[:, g % 2, :], self.ring[:, g % RING, :], ACT.Copy).then_inc(self.hi_done, 1)

    def split_lo(self, dve, g, it):
        dve.wait_ge(self.hi_done, g + 1 + it * BODY)
        minus_hi(dve, self.unit.lo[:, g % 2, :], self.ring[:, g % RING, :],
                 self.unit.hi[:, g % 2, :]).then_inc(self.split_done, 1)

    def split_next(self, eng, seg, it, j, last):
        if last and (seg is self.segments[-1] or self.segments[self.segments.index(seg) + 1].whole):
            return
        if eng is self.nc.scalar:
            self.split_hi(eng, seg.start + j + 1, it)
        else:
            self.split_lo(eng, seg.start + j + 1, it)

    def wait_split(self, pe, seg, it, j):
        pe.wait_ge(self.split_done, seg.start + j + 1 + it * BODY)
        return (seg.start + j) % 2

    def wait_done(self, eng, seg, it, j):
        eng.wait_ge(self.units_done, seg.start + j + 3 + it * BODY)

    def columns(self, name):
        a, b = COLS[name]
        return self.cols[:, a:b]


class Stage:

    def __init__(self, core):
        self.core = core

    def __enter__(self):
        core = self.core
        self.pool = list(core.pools[core.turn % 2])
        other = core.pools[1 - core.turn % 2]
        first = core.turn == 0
        core.turn += 1
        self.block = core.nc.Block()
        self.block.__enter__()
        if not first:
            @self.block.gpsimd
            def _(pool):
                pool.sem_clear(range(other[0].num, other[-1].num + 1))
        return self

    def sem(self):
        return self.pool.pop(0)

    def __exit__(self, *a):
        return self.block.__exit__(*a)



def product_by_feature(core, k, rhs, ntok, evacuate):
    seg = core.segments[k]
    with core.stage() as st:
        bank_free = [st.sem(), st.sem()]

        @st.block.sync
        def _(sp):
            core.feed(sp, k)

        @st.block.tensor
        def _(pe):
            def unit(it, j, last):
                b = core.wait_split(pe, seg, it, j)
                pe.wait_ge(bank_free[j % 2], it * (BODY // 2) + j // 2 + 1)
                for kt in range(KT):
                    ins = three_passes(pe, core.ps[:, j % 2, 0:ntok], core.unit.parts(slice(None), b, slice(kt * P, (kt + 1) * P)),
                                       rhs(kt), kt == 0, kt == KT - 1)
                ins.then_inc(core.units_done, 1)

            run_units(pe, seg.n, unit)

        def taker(eng, parity):
            eng.sem_inc(bank_free[parity], 1)

            def unit(it, j, last):
                core.split_next(eng, seg, it, j, last)
                if j % 2 == parity:
                    core.wait_done(eng, seg, it, j)
                    evacuate(eng, core.ps[:, j % 2, 0:ntok], it * BODY + j, j % 2).then_inc(bank_free[j % 2], 1)

            run_units(eng, seg.n, unit)

        @st.block.scalar
        def _(act):
            taker(act, 0)

        @st.block.vector
        def _(dve):
            taker(dve, 1)


def product_by_token(core, k, lhs, tiles, nk, evacuate, takers=("scalar", "vector")):
    seg = core.segments[k]
    chunks = seg.n // nk
    sets = 2 if tiles == NX else 1
    with core.stage() as st:
        set_free = [st.sem(), st.sem()]

        @st.block.sync
        def _(sp):
            core.feed(sp, k)

        @st.block.tensor
        def _(pe):
            for c in range(chunks):
                s = c % sets
                if c >= sets:
                    pe.wait_ge(set_free[s], c // sets)
                for kt in range(nk):
                    b = core.wait_split(pe, seg, 0, c * nk + kt)
                    for t in range(tiles):
                        for h in range(2):
                            last = three_passes(pe, core.ps[:, s * 4 + 2 * t + h, :], lhs(c, kt, t),
                                                core.unit.parts(slice(None), b, slice(h * HALF, (h + 1) * HALF)),
                                                kt == 0, kt == nk - 1)
                    last.then_inc(core.units_done, 1)

        def taker(eng, which):
            for c in range(chunks):
                for kt in range(nk):
                    core.split_next(eng, seg, 0, c * nk + kt, (c, kt) == (chunks - 1, nk - 1))
                if takers[c % 2] != which:
                    continue
                core.wait_done(eng, seg, 0, (c + 1) * nk - 1)
                for t in range(tiles):
                    for h in range(2):
                        last = evacuate(eng, c, t, h, core.ps[:, (c % sets) * 4 + 2 * t + h, :])
                last.then_inc(set_free[c % sets], 1)

        @st.block.scalar
        def _(act):
            taker(act, "scalar")

        @st.block.vector
        def _(dve):
            taker(dve, "vector")



def inverse_rms(core, stat, n, width):
    with core.stage() as st:
        inverted = st.sem()
        steps = st.sem()

        @st.block.vector
        def _(dve):
            step = Chain(dve, steps)
            step(dve.tensor_scalar(stat[:, 0:n], stat[:, 0:n], 1.0 / width, EPS, ALU.mult, ALU.add))
            dve.reciprocal(stat[:, 0:n], stat[:, 0:n]).then_inc(inverted, 1)

        @st.block.scalar
        def _(act):
            act.wait_ge(inverted, 1)
            act.activation(stat[:, 0:n], stat[:, 0:n], ACT.Sqrt)


def sums_of_squares(core, pieces, stat):
    width = pieces[0].shape[1]
    with ExitStack() as ctx:
        squares = ctx.enter_context(core.nc.sbuf_tensor(f"squares{core.turn}", [P, 2, width], F32))
        with core.stage() as st:
            done = st.sem()

            @st.block.scalar
            def _(act):
                for i, piece in enumerate(pieces):
                    if i >= 2:
                        act.wait_ge(done, i - 1)
                    act.activation(squares[:, i % 2, :], piece, ACT.Square,
                                   accum_out=stat[:, i:i + 1]).then_inc(done, 1)


def norm_transpose(core, tiles, gain, shift, dst):
    nc = core.nc
    n = len(tiles)
    with ExitStack() as ctx:
        stat = ctx.enter_context(nc.sbuf_tensor(f"norm_stat{core.turn}", [P, 4], F32))
        sums_of_squares(core, [core.X[:, a, :] for a, _, _ in tiles], stat)
        inverse_rms(core, stat, n, D)
        normed = ctx.enter_context(nc.sbuf_tensor(f"normed{core.turn}", [P, D], F32))
        whole = ctx.enter_context(nc.sbuf_tensor(f"normed_turned{core.turn}", [P, 2, KT, P], F32))
        with core.stage() as st:
            scaled, turned, taken, hi_ready, lo_ready = (st.sem() for _ in range(5))

            @st.block.scalar
            def _(act):
                def hi(i):
                    act.wait_ge(taken, i + 1)
                    b = tiles[i][1]
                    act.activation(dst.hi[:, :, b * P:(b + 1) * P], whole[:, i % 2, :, :], ACT.Copy).then_inc(hi_ready, 1)

                for i, (a, _, _) in enumerate(tiles):
                    if i >= 1:
                        act.wait_ge(turned, i)
                    act.activation(normed[:, :], core.X[:, a, :], ACT.Copy, scale=stat[:, i:i + 1]).then_inc(scaled, 1)
                    if i >= 1:
                        hi(i - 1)
                hi(n - 1)

            @st.block.tensor
            def _(pe):
                for i in range(n):
                    pe.wait_ge(scaled, i + 1)
                    if i >= 2:
                        pe.wait_ge(taken, i - 1)
                    for kt in range(KT):
                        last = pe.transpose(core.ps[:, 2 * (i % 2) + kt // 4, (kt % 4) * P:(kt % 4 + 1) * P],
                                            normed[:, kt * P:(kt + 1) * P], core.ident)
                    last.then_inc(turned, 1)

            @st.block.vector
            def _(dve):
                def lo(i):
                    dve.wait_ge(hi_ready, i + 1)
                    b = tiles[i][1]
                    minus_hi(dve, dst.lo[:, :, b * P:(b + 1) * P], whole[:, i % 2, :, :],
                             dst.hi[:, :, b * P:(b + 1) * P]).then_inc(lo_ready, 1)

                for i, (_, _, m) in enumerate(tiles):
                    dve.wait_ge(turned, i + 1)
                    if i >= 2:
                        dve.wait_ge(lo_ready, i - 1)
                    for kt in range(KT):
                        src = core.ps[:, 2 * (i % 2) + kt // 4, (kt % 4) * P:(kt % 4 + 1) * P]
                        to = whole[:, i % 2, kt, :]
                        if shift is None:
                            last = dve.tensor_scalar(to, src, gain(m, kt), None, ALU.mult)
                        else:
                            last = dve.tensor_scalar(to, src, gain(m, kt), shift(m, kt), ALU.mult, ALU.add)
                    last.then_inc(taken, 1)
                    if i >= 1:
                        lo(i - 1)
                lo(n - 1)


def transpose_tokens(core, pieces, dst):
    with core.stage() as st:
        turned, hi_ready, taken = st.sem(), st.sem(), st.sem()

        def halves(i):
            for h in range(2):
                yield (core.ps[:, 2 * (i % 2) + h, :].rearrange("p (k t) -> p k t", k=4),
                       dst.hi[:, 4 * h:4 * h + 4, i * P:(i + 1) * P], dst.lo[:, 4 * h:4 * h + 4, i * P:(i + 1) * P])

        @st.block.tensor
        def _(pe):
            for i, piece in enumerate(pieces):
                if i >= 2:
                    pe.wait_ge(taken, i - 1)
                for kt in range(KT):
                    last = pe.transpose(core.ps[:, 2 * (i % 2) + kt // 4, (kt % 4) * P:(kt % 4 + 1) * P],
                                        piece[:, kt * P:(kt + 1) * P], core.ident)
                last.then_inc(turned, 1)

        @st.block.scalar
        def _(act):
            for i in range(len(pieces)):
                act.wait_ge(turned, i + 1)
                for src, hi, lo in halves(i):
                    act.activation(hi, src, ACT.Copy).then_inc(hi_ready, 1)

        @st.block.vector
        def _(dve):
            for i in range(len(pieces)):
                for h, (src, hi, lo) in enumerate(halves(i)):
                    dve.wait_ge(hi_ready, 2 * i + h + 1)
                    last = minus_hi(dve, lo, src, hi)
                last.then_inc(taken, 1)


def split_tensor(core, src, dst, chunks):
    n = src.shape[1] // chunks
    with core.stage() as st:
        hi_ready = st.sem()

        @st.block.scalar
        def _(act):
            for i in range(chunks):
                a = slice(i * n, (i + 1) * n)
                act.activation(dst.hi[:, a, :], src[:, a, :], ACT.Copy).then_inc(hi_ready, 1)

        @st.block.vector
        def _(dve):
            for i in range(chunks):
                a = slice(i * n, (i + 1) * n)
                dve.wait_ge(hi_ready, i + 1)
                minus_hi(dve, dst.lo[:, a, :], src[:, a, :], dst.hi[:, a, :])


def add_normed(core, src, gain_row, n):
    nc = core.nc
    with ExitStack() as ctx:
        stat = ctx.enter_context(nc.sbuf_tensor(f"add_stat{core.turn}", [P, n], F32))
        scaled = ctx.enter_context(nc.sbuf_tensor(f"add_scaled{core.turn}", [P, n, D], F32))
        sums_of_squares(core, [src[:, t, :] for t in range(n)], stat)
        inverse_rms(core, stat, n, D)
        with core.stage() as st:
            steps = st.sem()

            @st.block.vector
            def _(dve):
                step = Chain(dve, steps)
                for t in range(n):
                    step.mark(dve.scalar_tensor_tensor(out=scaled[:, t, :], in0=src[:, t, :], scalar=stat[:, t:t + 1],
                                                       in1=gain_row, op0=ALU.mult, op1=ALU.mult))
                step.wait()
                for t in range(n):
                    dve.tensor_tensor(core.X[:, t, :], core.X[:, t, :], scaled[:, t, :], ALU.add)


def small_loads(core, pairs):
    with core.stage() as st:
        @st.block.scalar
        def _(act):
            for dst, src in pairs:
                core.dma_count += 16
                act.dma_start(dst, src).then_inc(core.dma_done, 16)
            act.wait_ge(core.dma_done, core.dma_count)



def gate_rows(core, wg, G):
    with core.stage() as st:
        gates_ready = st.sem()

        @st.block.tensor
        def _(pe):
            for which in range(2):
                for kt in range(KT):
                    for n, part in enumerate(core.xs.parts(slice(None), kt, slice(None))):
                        last = pe.matmul(core.ps[0:HEADS, which, 0:SEQ], wg[:, kt, which * HEADS:(which + 1) * HEADS],
                                         part.bitcast(F32), start=(kt == 0 and n == 0), stop=(kt == KT - 1 and n == 1))
                last.then_inc(gates_ready, 1)

        @st.block.vector
        def _(dve):
            for which, name in ((0, "ibias"), (1, "fbias")):
                dve.wait_ge(gates_ready, which + 1)
                dve.tensor_scalar(G[:, which, :], core.ps[0:HEADS, which, 0:SEQ], core.columns(name)[0:HEADS, :],
                                  None, ALU.add)


def gate_weights(core, G, W, mask):
    nc = core.nc
    with ExitStack() as ctx:
        def rows(name):
            return ctx.enter_context(nc.sbuf_tensor(name, [HEADS, SEQ], F32))

        e, lf, F, a, M, en, ones, zeros = (rows(f"gate_{x}") for x in ("e", "lf", "F", "a", "M", "en", "one", "zero"))
        a_col = ctx.enter_context(nc.sbuf_tensor("a_col", [P, NX, HEADS], F32))
        with core.stage() as st:
            absolute, logged, summed, floored, turned, steps, asteps = (st.sem() for _ in range(7))

            @st.block.vector
            def _(dve):
                step = Chain(dve, steps)
                step.mark(dve.memset(ones[:, :], 1.0))
                step.mark(dve.memset(zeros[:, :], 0.0))
                dve.scalar_tensor_tensor(out=e[:, :], in0=G[:, 1, :], scalar=-1.0, in1=G[:, 1, :], op0=ALU.mult,
                                         op1=ALU.max).then_inc(absolute, 1)
                dve.wait_ge(logged, 1)
                step(dve.scalar_tensor_tensor(out=lf[:, :], in0=G[:, 1, :], scalar=0.0, in1=e[:, :],
                                              op0=ALU.min, op1=ALU.subtract))
                step(dve.tensor_tensor_scan(F[:, :], ones[:, :], lf[:, :], 0.0, ALU.mult, ALU.add))
                step(dve.tensor_tensor(a[:, :], G[:, 0, :], F[:, :], ALU.subtract))
                step(dve.tensor_tensor_scan(M[:, :], zeros[:, :], a[:, :], 0.0, ALU.add, ALU.max))
                dve.tensor_tensor(en[:, :], F[:, :], M[:, :], ALU.add).then_inc(summed, 1)
                dve.wait_ge(turned, 1)
                last = dve.tensor_copy(a_col[:, :, :], core.ps[:, 0, 0:NX * HEADS].rearrange("p (t h) -> p t h", t=NX))
                last = dve.tensor_copy(core.floor[:, :, :], core.ps[:, 1, 0:NX * HEADS].rearrange("p (t h) -> p t h", t=NX))

            @st.block.scalar
            def _(act):
                step = Chain(act, asteps)
                act.wait_ge(absolute, 1)
                step(act.activation(e[:, :], e[:, :], ACT.Exp, scale=-1.0))
                act.activation(e[:, :], e[:, :], ACT.Ln, bias=1.0).then_inc(logged, 1)
                act.wait_ge(summed, 1)
                act.activation(en[:, :], en[:, :], ACT.Exp, scale=-1.0).then_inc(floored, 1)

            @st.block.tensor
            def _(pe):
                pe.wait_ge(floored, 1)
                for which, row in ((0, a), (1, en)):
                    for t in range(NX):
                        last = pe.transpose(core.ps[:, which, t * HEADS:(t + 1) * HEADS], row[:, t * P:(t + 1) * P],
                                            core.ident[0:HEADS, 0:HEADS])
                last.then_inc(turned, 1)

        with core.stage() as st:
            spread, bounded, raised, steps = (st.sem() for _ in range(4))

            @st.block.tensor
            def _(pe):
                for h in range(HEADS):
                    pe.matmul(core.ps[:, 2 + h, 0:SEQ], core.sel[0:HEADS, h, :], M[:, :],
                              start=True, stop=True).then_inc(spread, 1)

            @st.block.vector
            def _(dve):
                for h in range(HEADS):
                    dve.wait_ge(spread, h + 1)
                    dve.tensor_scalar(W[:, h, 0:SEQ], core.ps[:, 2 + h, 0:SEQ], a_col[:, 0, h:h + 1], 0.0,
                                      ALU.subtract, ALU.max)
                    dve.tensor_scalar(W[:, h, SEQ:DCOLS], core.ps[:, 2 + h, P:SEQ], a_col[:, 1, h:h + 1], 0.0,
                                      ALU.subtract, ALU.max).then_inc(bounded, 1)
                for h in range(HEADS):
                    dve.wait_ge(raised, h + 1)
                    dve.tensor_tensor(W[:, h, :], W[:, h, :], mask, ALU.mult)

            @st.block.scalar
            def _(act):
                for h in range(HEADS):
                    act.wait_ge(bounded, h + 1)
                    act.activation(W[:, h, :], W[:, h, :], ACT.Exp, scale=-1.0).then_inc(raised, 1)


def causal_conv(core, FM, first, CV):
    a0 = COLS["conv"][0]
    n = 2 * KT
    with core.stage() as st:
        convolved, steps = st.sem(), st.sem()

        @st.block.vector
        def _(dve):
            chain = Chain(dve, steps)

            def tile(i, step):
                x = FM[:, first + i, :]

                def tap(j):
                    return core.cols[:, a0 + j * n + i:a0 + j * n + i + 1]

                step(dve.tensor_scalar(CV[:, i, :], x, tap(3), None, ALU.mult))
                for lag in (1, 2, 3):
                    step(dve.scalar_tensor_tensor(out=CV[:, i, lag:SEQ], in0=FM[:, first + i, 0:SEQ - lag],
                                                  scalar=tap(3 - lag), in1=CV[:, i, lag:SEQ],
                                                  op0=ALU.mult, op1=ALU.add))

            for i in range(n):
                tile(i, chain)
            dve.engine_nop().then_inc(convolved, 1)

        @st.block.scalar
        def _(act):
            act.wait_ge(convolved, 1)
            act.activation(FM[:, first:first + n, :], CV[:, :, :], ACT.Silu)


def linear_attention(core, FM, q0, k0, vals, W, ST, HB, h0, normalise, ones_col):
    nc = core.nc
    with core.stage() as st:
        scored, weighted, steps = st.sem(), st.sem(), st.sem()

        @st.block.tensor
        def _(pe):
            for h in range(HEADS):
                for s, (ta, ca, cb) in enumerate(((0, 0, SEQ), (P, SEQ, DCOLS))):
                    for d in range(2):
                        last = pe.matmul(core.ps[:, h, ca:cb], FM[:, k0 + 2 * h + d, s * P:(s + 1) * P],
                                         FM[:, q0 + 2 * h + d, ta:SEQ], start=(d == 0), stop=(d == 1))
                last.then_inc(scored, 1)

        @st.block.vector
        def _(dve):
            for h in range(HEADS):
                dve.wait_ge(scored, h + 1)
                dve.tensor_tensor(ST[:, h, :], core.ps[:, h, 0:DCOLS], W[:, h, :], ALU.mult)

    with ExitStack() as ctx:
        den = ctx.enter_context(nc.sbuf_tensor(f"den{h0}", [P, NX, HEADS], F32))
        with core.stage() as st:
            summed, ready, steps = st.sem(), st.sem(), st.sem()

            @st.block.tensor
            def _(pe):
                for h in range(HEADS):
                    for t, tiles in ((0, ((0, 0),)), (1, ((0, P), (1, SEQ)))):
                        for n, (s, c) in enumerate(tiles):
                            w = ST[:, h, c:c + P]
                            edge = dict(start=(n == 0), stop=(n == len(tiles) - 1))
                            last = pe.matmul(core.ps[:, 2 * h + t, 0:HD], w, vals(s, h), skip_group_check=True, **edge)
                        if normalise:
                            for n, (s, c) in enumerate(tiles):
                                w = ST[:, h, c:c + P]
                                last = pe.matmul(core.ps[:, 2 * h + t, HD:HD + 1], w, ones_col,
                                                 start=(n == 0), stop=(n == len(tiles) - 1), skip_group_check=True)
                last.then_inc(summed, 1)

            @st.block.vector
            def _(dve):
                step = Chain(dve, steps)
                dve.wait_ge(summed, 1)
                banks = core.ps[:, :, :].rearrange("p (h t) c -> p h t c", t=NX)
                if normalise:
                    step(dve.tensor_copy(den[:, :, :], banks[:, :, :, HD].rearrange("p h t -> p t h")))
                    step(dve.scalar_tensor_tensor(out=den[:, :, :], in0=den[:, :, :], scalar=-1.0, in1=den[:, :, :],
                                                  op0=ALU.mult, op1=ALU.max))
                    step(dve.tensor_tensor(den[:, :, :], den[:, :, :], core.floor[:, :, :], ALU.max))
                    step(dve.reciprocal(den[:, :, :], den[:, :, :]))
                for h in range(HEADS):
                    for t in range(NX):
                        if normalise:
                            dve.tensor_scalar(HB[:, t, h0 + h, :], banks[:, h, t, 0:HD], den[:, t, h:h + 1], None, ALU.mult)
                        else:
                            dve.tensor_copy(HB[:, t, h0 + h, :], banks[:, h, t, 0:HD])


def gated_head_norm(core, HB, gates):
    with ExitStack() as ctx:
        stat = ctx.enter_context(core.nc.sbuf_tensor("head_stat", [P, 2 * DH], F32))
        sums_of_squares(core, [HB[:, t, h, :] for t in range(NX) for h in range(2 * HEADS)], stat)
        inverse_rms(core, stat, 16, HD)
        with core.stage() as st:
            @st.block.vector
            def _(dve):
                for t in range(NX):
                    for h in range(2 * HEADS):
                        i = t * 8 + h
                        dve.scalar_tensor_tensor(out=HB[:, t, h, :], in0=HB[:, t, h, :], scalar=stat[:, i:i + 1],
                                                 in1=gates(t, h), op0=ALU.mult, op1=ALU.mult)


def diff_attention(core, FM, vals, S, alibi, AT, HDO, lam_rows, subln):
    nc = core.nc
    with core.stage() as st:
        scored, taken = st.sem(), st.sem()

        @st.block.tensor
        def _(pe):
            for n in range(2 * DH):
                h, c = n // 2, n % 2
                if n >= BANKS:
                    pe.wait_ge(taken, n - BANKS + 1)
                rows = slice(64 * c, 64 * c + 64)
                for t, (ca, cb, kb) in enumerate(((0, P, P), (P, DCOLS, SEQ))):
                    last = pe.matmul(core.ps[:, n % BANKS, ca:cb], FM[rows, h, t * P:(t + 1) * P],
                                     FM[rows, KT + h, 0:kb], start=True, stop=True)
                last.then_inc(scored, 1)

        @st.block.vector
        def _(dve):
            for n in range(2 * DH):
                h, c = n // 2, n % 2
                dve.wait_ge(scored, n + 1)
                dve.scalar_tensor_tensor(out=S[:, h, c, :], in0=core.ps[:, n % BANKS, 0:DCOLS], scalar=0.125,
                                         in1=alibi[:, h, :], op0=ALU.mult, op1=ALU.add).then_inc(taken, 1)

    with ExitStack() as ctx:
        stat = ctx.enter_context(nc.sbuf_tensor("softmax_stat", [P, 2, 2 * DH], F32))
        lam = ctx.enter_context(nc.sbuf_tensor("lam", [P, 4], F32))
        parts = ((0, 0, P), (1, P, DCOLS))
        flat = S.rearrange("p h c k -> p (h c) k")
        with core.stage() as st:
            shifted, raised, lam_dots, lam_raised, steps = (st.sem() for _ in range(5))

            @st.block.vector
            def _(dve):
                step = Chain(dve, steps)
                step.mark(dve.tensor_tensor(lam_rows[:, 0:64], lam_rows[:, 0:64], lam_rows[:, 64:128], ALU.mult))
                step(dve.tensor_tensor(lam_rows[:, 128:192], lam_rows[:, 128:192], lam_rows[:, 192:256], ALU.mult))
                dve.tensor_reduce(lam[:, 0:1], lam_rows[:, 0:64], AX_X, ALU.add)
                dve.tensor_reduce(lam[:, 1:2], lam_rows[:, 128:192], AX_X, ALU.add).then_inc(lam_dots, 1)
                for q, a, b in parts:
                    step.mark(dve.tensor_reduce(stat[:, q, :], flat[:, :, a:b], AX_X, ALU.max))
                step.wait()
                for q, a, b in parts:
                    last = dve.tensor_tensor(flat[:, :, a:b], flat[:, :, a:b],
                                             stat[:, q, :].unsqueeze(2).broadcast_to([P, 2 * DH, b - a]), ALU.subtract)
                last.then_inc(shifted, 1)
                dve.wait_ge(lam_raised, 1)
                step(dve.tensor_tensor(lam[:, 2:3], lam[:, 0:1], lam[:, 1:2], ALU.subtract))
                step(dve.tensor_scalar(lam[:, 3:4], lam[:, 2:3], LAM_INIT, None, ALU.add))
                dve.wait_ge(raised, 1)
                for q, a, b in parts:
                    step.mark(dve.tensor_reduce(stat[:, q, :], flat[:, :, a:b], AX_X, ALU.add))
                step.wait()
                step(dve.reciprocal(stat[:, :, :], stat[:, :, :]))
                halves = stat[:, :, :].rearrange("p q (h c) -> p q h c", c=2)
                step(dve.tensor_scalar(halves[:, :, :, 1], halves[:, :, :, 1], lam[:, 3:4], None, ALU.mult))
                for q, a, b in parts:
                    for c in range(2):
                        step.mark(dve.tensor_tensor(S[:, :, c, a:b], S[:, :, c, a:b],
                                                    halves[:, q, :, c].unsqueeze(2).broadcast_to([P, DH, b - a]),
                                                    ALU.mult))
                step.wait()
                dve.tensor_tensor(S[:, :, 0, :], S[:, :, 0, :], S[:, :, 1, :], ALU.subtract)

            @st.block.scalar
            def _(act):
                act.wait_ge(lam_dots, 1)
                act.activation(lam[:, 0:2], lam[:, 0:2], ACT.Exp).then_inc(lam_raised, 1)
                act.wait_ge(shifted, 1)
                act.activation(flat, flat, ACT.Exp).then_inc(raised, 1)

    with core.stage() as st:
        turned, taken = st.sem(), st.sem()

        @st.block.tensor
        def _(pe):
            for h in range(DH):
                if h >= 4:
                    pe.wait_ge(taken, h - 3)
                for i in range(3):
                    last = pe.transpose(core.ps[:, h % 4, i * P:(i + 1) * P], S[:, h, 0, i * P:(i + 1) * P], core.ident)
                last.then_inc(turned, 1)
            for h in range(DH):
                pe.wait_ge(taken, h + 1)
                pe.matmul(core.ps[:, 4 + h // 4, (h % 4) * P:(h % 4 + 1) * P], AT(h, 0, P), vals(0, h),
                          start=True, stop=True, skip_group_check=True)
                for n in range(2):
                    pe.matmul(core.ps[:, 6 + h // 4, (h % 4) * P:(h % 4 + 1) * P], AT(h, (n + 1) * P, (n + 2) * P),
                              vals(n, h), start=(n == 0), stop=(n == 1), skip_group_check=True)

        @st.block.scalar
        def _(act):
            for h in range(DH):
                act.wait_ge(turned, h + 1)
                act.activation(AT(h, 0, DCOLS), core.ps[:, h % 4, 0:DCOLS], ACT.Copy).then_inc(taken, 1)

    with ExitStack() as ctx:
        stat = ctx.enter_context(nc.sbuf_tensor("sub_stat", [P, 2 * DH], F32))
        heads = core.ps[:, 4:8, :].rearrange("p b (h e) -> p (b h) e", h=4)
        sums_of_squares(core, [heads[:, i, :] for i in range(2 * DH)], stat)
        inverse_rms(core, stat, 2 * DH, P)
        with core.stage() as st:
            steps = st.sem()

            @st.block.vector
            def _(dve):
                step = Chain(dve, steps)
                step(dve.tensor_scalar(stat[:, :], stat[:, :], 1.0 - LAM_INIT, None, ALU.mult))
                for i in range(2 * DH):
                    t, h = i // DH, i % DH
                    dve.scalar_tensor_tensor(out=HDO[:, t, h, :], in0=heads[:, i, :],
                                             scalar=stat[:, i:i + 1], in1=subln, op0=ALU.mult, op1=ALU.mult)


def first_block(core, A):
    nc = core.nc
    with ExitStack() as scope:
        def sb(name, shape, ctx=scope):
            return ctx.enter_context(nc.sbuf_tensor(name, shape, F32))

        xs = core.xs = Split(nc, scope, "xs", [P, KT, SEQ])
        norm_transpose(core, [(t, t, 0) for t in range(NX)], lambda m, kt: core.columns("g0")[:, kt:kt + 1], None, xs)

        def by_tile(c, kt, t):
            return xs.parts(slice(None), kt, slice(t * P, (t + 1) * P))

        branches = scope.enter_context(ExitStack())
        TM = sb("by_token", [P, NX, 8, D], branches)
        FM = sb("by_feature", [P, 48, SEQ], branches)
        G = sb("gate_rows", [HEADS, 2, SEQ], branches)
        core.floor = sb("den_floor", [P, NX, HEADS], branches)

        def to_features(eng, ps, f, slot):
            if eng is core.nc.scalar:
                return eng.activation(FM[:, f, :], ps, ACT.Copy)
            return eng.tensor_copy(FM[:, f, :], ps)

        product_by_feature(core, 0, lambda kt: xs.parts(slice(None), kt, slice(None)), SEQ, to_features)

        def to_tokens(eng, c, t, h, ps):
            f = ACT.Copy if c < 3 else ACT.Sigmoid if c < 7 else ACT.Silu
            return eng.activation(TM[:, t, c, h * HALF:(h + 1) * HALF], ps, f)

        product_by_token(core, 1, by_tile, NX, KT, to_tokens,
                         ("scalar", "scalar"))
        with ExitStack() as ctx:
            wg = sb("gate_weights", [P, KT, 2 * HEADS], ctx)
            small_loads(core, [(wg[:, :, :], A["w_gate"])])
            gate_rows(core, wg, G)

        with ExitStack() as ctx:
            CV = sb("conv", [P, 2 * KT, SEQ], ctx)
            causal_conv(core, FM, 2 * KT, CV)
        HB = FM[:, 16:32, :].rearrange("p (t h) e -> p t h e", t=NX)
        with ExitStack() as ctx:
            W = sb("mlstm_weights", [P, HEADS, DCOLS], ctx)
            spare = core.X[:, NX:NT, :].rearrange("p t d -> p (t d)")
            R = spare[:, 0:HEADS * DCOLS].rearrange("p (h c) -> p h c", h=HEADS)
            mask = spare[:, HEADS * DCOLS:(HEADS + 1) * DCOLS]
            ones_col = sb("ones_col", [P, 1], ctx)
            core.sel = sb("sel", [HEADS, HEADS, P], ctx)
            small_loads(core, [(core.sel[:, :, :], A["k_sel"]), (R, A["k_retention"]), (mask, A["k_mask"])])
            with core.stage() as st:
                @st.block.vector
                def _(dve):
                    dve.memset(ones_col[:, :], 1.0)
            gate_weights(core, G, W, mask)
            ST = sb("weighted_scores", [P, HEADS, DCOLS], ctx)
            linear_attention(core, FM, 2 * KT, 3 * KT, lambda s, h: TM[:, s, 0, h * HD:(h + 1) * HD], W, ST, HB, 0,
                             True, ones_col[:, 0:1])
            linear_attention(core, FM, 4 * KT, 5 * KT, lambda s, h: TM[:, s, 1, h * HD:(h + 1) * HD], R, ST, HB, HEADS,
                             False, None)
        gated_head_norm(core, HB, lambda t, h: TM[:, t, 3 if h < HEADS else 7, (h % HEADS) * HD:(h % HEADS + 1) * HD])

        with ExitStack() as ctx:
            alibi = FM[:, 32:44, :].rearrange("p a b -> p (a b)").rearrange("p (h c) -> p h c", h=DH)
            lam_rows = sb("lam_rows", [P, 256], ctx)
            subln = sb("subln", [P, P], ctx)
            spare = TM[:, :, 0:2, :].rearrange("p t a b -> p t (a b)")

            def AT(h, a, b):
                return spare[:, h // 4, (h % 4) * DCOLS + a:(h % 4) * DCOLS + b]

            small_loads(core, [(alibi, A["k_alibi"]),
                               (lam_rows[:, :], A["diff_lambda"].broadcast_to([P, 256])),
                               (subln[:, :], A["diff_subln"].broadcast_to([P, P]))])
            S = sb("attention", [P, DH, 2, DCOLS], ctx)[:, :, :, :]
            HDO = FM[:, 0:8, :].rearrange("p (t a) (b e) -> p t (a b) e", t=NX, b=2)
            diff_attention(core, FM, lambda s, h: TM[:, s, 2, h * P:(h + 1) * P], S, alibi, AT, HDO, lam_rows,
                           subln[:, :])

        heads = FM[:, 16:32, :].rearrange("p (t r h) e -> p t r (h e)", t=NX, r=2)
        diffs = FM[:, 0:8, :].rearrange("p (t a) b -> p t (a b)", t=NX)
        Y = FM[:, 8:16, :].rearrange("p (t a) b -> p t (a b)", t=NX)
        for c, piece in enumerate((lambda t: heads[:, t, 0], lambda t: diffs[:, t], lambda t: heads[:, t, 1])):
            transpose_tokens(core, [piece(t) for t in range(NX)], xs)

            def mix(eng, _, t, h, ps, c=c):
                cols = slice(h * HALF, (h + 1) * HALF)
                gate = TM[:, t, 4 + c, cols]
                return eng.tensor_tensor(Y[:, t, cols] if c == 0 else gate, ps, gate, ALU.mult)

            product_by_token(core, 2 + c, by_tile, NX, KT, mix, ("vector", "vector"))
        with core.stage() as st:
            steps = st.sem()

            @st.block.vector
            def _(dve):
                step = Chain(dve, steps)
                step(dve.tensor_tensor(Y, Y, TM[:, :, 5, :], ALU.add))
                step(dve.tensor_tensor(Y, Y, TM[:, :, 6, :], ALU.add))
        transpose_tokens(core, [Y[:, t] for t in range(NX)], xs)
        branches.close()

        Y2 = sb("mixed", [P, NX, D])
        rows = sb("gain_rows", [P, 2, D])
        small_loads(core, [(rows[:, i, :], A["gain_rows"][i:i + 1, :].broadcast_to([P, D])) for i in range(2)])

        def keep(eng, c, t, h, ps):
            return eng.activation(Y2[:, t, h * HALF:(h + 1) * HALF], ps, ACT.Copy)

        product_by_token(core, 5, by_tile, NX, KT, keep, ("scalar", "scalar"))
        add_normed(core, Y2, rows[:, 0, :], NX)

        norm_transpose(core, [(t, t, 0) for t in range(NX)], lambda m, kt: core.columns("g2")[:, kt:kt + 1], None, xs)
        fT = Split(nc, scope, "ffn_hidden", [P, FT, SEQ])
        with ExitStack() as ctx:
            hidden = sb("ffn_product", [P, FT, SEQ], ctx)
            silu = sb("ffn_silu", [P, 2, SEQ], ctx)
            seg = core.segments[6]
            with core.stage() as st:
                bank_free = [st.sem(), st.sem()]

                @st.block.sync
                def _(sp):
                    core.feed(sp, 6)

                @st.block.tensor
                def _(pe):
                    def unit(it, j, last):
                        b = core.wait_split(pe, seg, it, j)
                        pe.wait_ge(bank_free[j % 2], it * (BODY // 2) + j // 2 + 1)
                        for kt in range(KT):
                            ins = three_passes(pe, core.ps[:, j % 2, 0:SEQ],
                                               core.unit.parts(slice(None), b, slice(kt * P, (kt + 1) * P)),
                                               xs.parts(slice(None), kt, slice(None)), kt == 0, kt == KT - 1)
                        ins.then_inc(core.units_done, 1)

                    run_units(pe, seg.n, unit)

                @st.block.scalar
                def _(act):
                    act.sem_inc(bank_free[0], 1)
                    act.sem_inc(bank_free[1], 1)

                    def unit(it, j, last):
                        core.split_next(act, seg, it, j, last)
                        if j % 2:
                            return
                        core.wait_done(act, seg, it, j)
                        if j < 2:
                            act.wait_ge(bank_free[1], it * (BODY // 2) + j // 2 + 1)
                        else:
                            act.wait_ge(bank_free[1], it * (BODY // 2) + j // 2)
                        act.activation(silu[:, (j // 2) % 2, :], core.ps[:, 0, 0:SEQ], ACT.Silu).then_inc(bank_free[0], 1)

                    run_units(act, seg.n, unit)

                @st.block.vector
                def _(dve):
                    def unit(it, j, last):
                        core.split_next(dve, seg, it, j, last)
                        if j % 2 == 0:
                            return
                        dve.wait_ge(bank_free[0], it * (BODY // 2) + j // 2 + 2)
                        core.wait_done(dve, seg, it, j)
                        dve.tensor_tensor(hidden[:, it * (BODY // 2) + j // 2, :], core.ps[:, 1, 0:SEQ],
                                          silu[:, (j // 2) % 2, :], ALU.mult).then_inc(bank_free[1], 1)

                    run_units(dve, seg.n, unit)
            split_tensor(core, hidden[:, :, :], fT, 11)

        product_by_token(core, 7, lambda c, kt, t: fT.parts(slice(None), kt, slice(t * P, (t + 1) * P)), NX, FT, keep,
                         ("scalar", "scalar"))
        add_normed(core, Y2, rows[:, 1, :], NX)
        small_loads(core, [(Y2[:, :, :], A["k_positions"]),
                           (core.X[:, NX:NT, :], A["ctx"].rearrange("b (t p) d -> p (b t) d", p=P))])
        with core.stage() as st:
            @st.block.vector
            def _(dve):
                dve.tensor_tensor(core.X[:, 0:NX, :], core.X[:, 0:NX, :], Y2[:, :, :], ALU.add)



def modulation(core, k, bias):
    MOD = core.MOD

    seg = core.segments[k]
    with core.stage() as st:
        @st.block.sync
        def _(sp):
            core.feed(sp, k)

        @st.block.tensor
        def _(pe):
            def unit(it, j, last):
                slot = (seg.start + j) % RING
                pe.wait_ge(core.loaded[slot], 16 * ((seg.start + j) // RING + 1) + it * (16 * BODY // RING))
                f = it * BODY + j
                to = core.ps[:, 0, 2 * f:2 * f + 2] if isinstance(f, int) else core.ps[:, 0, bass.ds(f * 2, 2)]
                for kt in range(KT):
                    ins = pe.matmul(to, core.ring[:, slot, kt * P:(kt + 1) * P], core.silu_c[:, kt, :],
                                    start=(kt == 0), stop=(kt == KT - 1), skip_group_check=True)
                ins.then_inc(core.units_done, 1)

            run_units(pe, seg.n, unit)

        @st.block.vector
        def _(dve):
            def unit(it, j, last):
                core.wait_done(dve, seg, it, j)
                dve.sem_inc(core.hi_done, 1)
                dve.sem_inc(core.split_done, 1)

            run_units(dve, seg.n, unit)
            dve.tensor_copy(MOD[:, :, :], core.ps[:, 0, 0:96].rearrange("p (f s) -> p f s", s=2))
            core.split_lo(dve, seg.start + seg.n, 0)

        @st.block.scalar
        def _(act):
            core.split_hi(act, seg.start + seg.n, 0)

    with core.stage() as st:
        steps = st.sem()

        @st.block.vector
        def _(dve):
            step = Chain(dve, steps)
            step(dve.tensor_tensor(MOD[:, :, :], MOD[:, :, :],
                                   core.columns(bias).unsqueeze(2).broadcast_to([P, 48, 2]), ALU.add))
            for a, name in ((8, "n1"), (32, "n2")):
                step(dve.tensor_scalar(core.gains[:, a // 32, :, :], MOD[:, a:a + 8, :], 1.0, None, ALU.add))
                step(dve.tensor_tensor(core.gains[:, a // 32, :, :], core.gains[:, a // 32, :, :],
                                       core.columns(f"{name}_{bias[-1]}").unsqueeze(2).broadcast_to([P, 8, 2]),
                                       ALU.mult))


def spread_rows(core, first, nsets, dst):
    with ExitStack() as ctx:
        wide = ctx.enter_context(core.nc.sbuf_tensor(f"wide{core.turn}", [P, nsets, KT, P], F32))
        with core.stage() as st:
            widened, spread = st.sem(), st.sem()

            @st.block.vector
            def _(dve):
                for s in range(nsets):
                    src = core.MOD[:, first:first + KT, s:s + 1].broadcast_to([P, KT, P])
                    dve.tensor_copy(wide[:, s, :, :], src).then_inc(widened, 1)

            @st.block.tensor
            def _(pe):
                for s in range(nsets):
                    pe.wait_ge(widened, s + 1)
                    for kt in range(KT):
                        last = pe.matmul(core.ps[:, 2 * s + kt // 4, (kt % 4) * P:(kt % 4 + 1) * P], wide[:, s, kt, :],
                                         core.ident, start=True, stop=True)
                    last.then_inc(spread, 1)

            @st.block.scalar
            def _(act):
                for s in range(nsets):
                    act.wait_ge(spread, s + 1)
                    for h in range(2):
                        act.activation(dst[:, s, h * HALF:(h + 1) * HALF], core.ps[:, 2 * s + h, :], ACT.Copy)


def add_gated(core, k, lhs, tiles, gate):
    with ExitStack() as ctx:
        out = ctx.enter_context(core.nc.sbuf_tensor(f"gated{k}", [P, tiles, D], F32))

        def take(eng, c, t, h, ps):
            cols = slice(h * HALF, (h + 1) * HALF)
            return eng.tensor_tensor(out[:, t, cols], ps, gate(t)[:, cols], ALU.mult)

        product_by_token(core, k, lhs, tiles, KT, take, ("vector", "vector"))
        with core.stage() as st:
            @st.block.vector
            def _(dve):
                dve.tensor_tensor(core.X[:, 0:tiles, :], core.X[:, 0:tiles, :], out[:, :, :], ALU.add)


def chunk_mixer(core, A, k_in, k_out):
    nc = core.nc
    with ExitStack() as ctx:
        def sb(name, shape):
            return ctx.enter_context(nc.sbuf_tensor(name, shape, F32))

        xs = Split(nc, ctx, "cm_xs", [P, KT, 2 * SEQ])

        def by_tile(c, kt, t):
            return xs.parts(slice(None), kt, slice(t * P, (t + 1) * P))

        gate_rows_ = sb("cm_gate_rows", [P, 2, D])
        spread_rows(core, 16, 2, gate_rows_)
        norm_transpose(core, [(t, t, t // NX) for t in range(NT)],
                       lambda m, kt: core.gains[:, 0, kt, m:m + 1], lambda m, kt: core.MOD[:, kt, m:m + 1], xs)
        Z = sb("cm_z", [P, NT, 2, D])
        rows = sb("cm_rows", [P, 2, D])
        ws = sb("cm_ws", [P, 8, P])
        small_loads(core, [(rows[:, i, :], A["gain_rows"][2 + i:3 + i, :].broadcast_to([P, D])) for i in range(2)] +
                    [(ws[:, :, :], A["cm_ws"])])

        def gelu(eng, c, t, h, ps):
            return eng.activation(Z[:, t, c, h * HALF:(h + 1) * HALF], ps, ACT.Gelu_apprx_tanh)

        product_by_token(core, k_in, by_tile, NT, KT, gelu,
                         ("scalar", "scalar"))
        stat = sb("cm_stat", [P, NT])
        mean = sb("cm_mean", [P, NT])
        with core.stage() as st:
            steps = st.sem()

            @st.block.vector
            def _(dve):
                step = Chain(dve, steps)
                step(dve.tensor_reduce(mean[:, :], Z[:, :, 1, :], AX_X, ALU.add))
                step(dve.tensor_scalar(mean[:, :], mean[:, :], 1.0 / D, None, ALU.mult))
                for t in range(NT):
                    dve.tensor_scalar(Z[:, t, 1, :], Z[:, t, 1, :], mean[:, t:t + 1], None, ALU.subtract)
        sums_of_squares(core, [Z[:, t, 1, :] for t in range(NT)], stat)
        inverse_rms(core, stat, NT, D)
        with core.stage() as st:
            steps, mixed, normed = st.sem(), st.sem(), st.sem()

            @st.block.vector
            def _(dve):
                step = Chain(dve, steps)
                for t in range(NT):
                    step(dve.scalar_tensor_tensor(out=Z[:, t, 1, :], in0=Z[:, t, 1, :], scalar=stat[:, t:t + 1],
                                                  in1=rows[:, 0, :], op0=ALU.mult, op1=ALU.mult))
                    dve.tensor_tensor(Z[:, t, 1, :], Z[:, t, 1, :], rows[:, 1, :], ALU.add).then_inc(normed, 1)
                for t in range(NT):
                    dve.wait_ge(mixed, t + 1)
                    for h in range(8):
                        cols = slice(h * P, (h + 1) * P)
                        bank = core.ps[:, 2 * t + h // 4, (h % 4) * P:(h % 4 + 1) * P]
                        dve.scalar_tensor_tensor(out=Z[:, t, 0, cols], in0=bank, scalar=core.columns("bs")[:, h:h + 1],
                                                 in1=Z[:, t, 0, cols], op0=ALU.add, op1=ALU.mult)

            @st.block.tensor
            def _(pe):
                for t in range(NT):
                    pe.wait_ge(normed, t + 1)
                    for h in range(8):
                        last = pe.matmul(core.ps[:, 2 * t + h // 4, (h % 4) * P:(h % 4 + 1) * P], ws[:, h, :],
                                         Z[:, t, 1, h * P:(h + 1) * P], start=True, stop=True, skip_group_check=True)
                    last.then_inc(mixed, 1)

        transpose_tokens(core, [Z[:, t, 0, :] for t in range(NT)], xs)
        add_gated(core, k_out, by_tile, NT,
                  lambda t: gate_rows_[:, t // NX, :])


def choose_experts(core, keysT, qT, tiles, pair_keys, pair_weight):
    nc = core.nc
    with ExitStack() as ctx:
        def sb(name, shape, dt=F32):
            return ctx.enter_context(nc.sbuf_tensor(f"{name}{core.turn}", shape, dt))

        scores = sb("key_scores", [P, 2 * PH, KEYS])
        rest = sb("key_rest", [P, 2 * PH, KEYS])
        best = sb("key_best", [P, PH, 2, TOPK])
        where = sb("key_where", [P, PH, 2, TOPK], U32)
        where_f = sb("key_where_f", [P, PH, 2, TOPK])
        cand = sb("cand", [P, PH, TOPK * TOPK])
        cand_rest = sb("cand_rest", [P, PH, TOPK * TOPK])
        top = sb("cand_top", [P, PH, TOPK])
        at = sb("cand_at", [P, PH, TOPK], U32)
        digit = sb("cand_digit", [P, 2, PH, TOPK], U32)
        digit_f = sb("cand_digit_f", [P, 2, PH, TOPK])
        sums = sb("softmax_sums", [P, PH])
        pairs = sb("pairs", [P, 3, PAIRS])
        with core.stage() as st:
            scored, copied, chosen, shifted, raised, turned, taken, steps = (st.sem() for _ in range(8))

            @st.block.tensor
            def _(pe):
                def score(t):
                    if t:
                        pe.wait_ge(copied, t)
                    for hk in range(2 * PH):
                        for d in range(2):
                            last = pe.matmul(core.ps[:, hk // 4, (hk % 4) * KEYS:(hk % 4 + 1) * KEYS],
                                             qT[:, 2 * hk + d, t * P:(t + 1) * P], keysT[:, 2 * hk + d, :],
                                             start=(d == 0), stop=(d == 1), skip_group_check=True)
                    last.then_inc(scored, 1)

                score(0)
                for t in range(tiles):
                    if t + 1 < tiles:
                        score(t + 1)
                    pe.wait_ge(chosen, t + 2)
                    if t:
                        pe.wait_ge(taken, t)
                    for i in range(3):
                        last = pe.transpose(core.ps[:, 4, i * P:(i + 1) * P], pairs[:, i, :], core.ident)
                    last.then_inc(turned, 1)

            @st.block.scalar
            def _(act):
                act.sem_inc(chosen, 1)
                with act.Fori(0, tiles, 1) as t:
                    act.wait_ge(scored, t + 1)
                    act.wait_ge(chosen, t + 1)
                    act.activation(scores[:, :, :], core.ps[:, 0:4, :].rearrange("p b (k m) -> p (b k) m", m=KEYS),
                                   ACT.Copy).then_inc(copied, 1)
                    act.wait_ge(shifted, t + 1)
                    act.activation(pairs[:, 2, :], pairs[:, 2, :], ACT.Exp).then_inc(raised, 1)
                    act.wait_ge(turned, t + 1)
                    act.activation(pair_keys[:, :, bass.ds(t * P, P)],
                                   core.ps[:, 4, 0:2 * P].rearrange("p (i n) -> p i n", i=2), ACT.Copy)
                    act.activation(pair_weight[:, bass.ds(t * P, P)], core.ps[:, 4, 2 * P:3 * P],
                                   ACT.Copy).then_inc(taken, 1)

            @st.block.vector
            def _(dve):
                chain = Chain(dve, steps)

                def tile(t, step):
                    dve.wait_ge(copied, t + 1)
                    for hk in range(2 * PH):
                        step.mark(dve.max(best[:, hk // 2, hk % 2, 0:8], scores[:, hk, :]))
                    step.wait()
                    for hk in range(2 * PH):
                        step.mark(dve.max_index(where[:, hk // 2, hk % 2, 0:8], best[:, hk // 2, hk % 2, 0:8], scores[:, hk, :]))
                        step.mark(dve.match_replace(rest[:, hk, :], best[:, hk // 2, hk % 2, 0:8], scores[:, hk, :], NEG))
                    step.wait()
                    for hk in range(2 * PH):
                        step.mark(dve.max(best[:, hk // 2, hk % 2, 8:16], rest[:, hk, :]))
                    step.wait()
                    for hk in range(2 * PH):
                        step.mark(dve.max_index(where[:, hk // 2, hk % 2, 8:16], best[:, hk // 2, hk % 2, 8:16], rest[:, hk, :]))
                    step.wait()
                    square = [P, PH, TOPK, TOPK]
                    step.mark(dve.tensor_copy(where_f[:, :, :, :], where[:, :, :, :]))
                    step(dve.tensor_tensor(cand[:, :, :].rearrange("p h (i j) -> p h i j", i=TOPK),
                                           best[:, :, 0, :].unsqueeze(3).broadcast_to(square),
                                           best[:, :, 1, :].unsqueeze(2).broadcast_to(square), ALU.add))
                    for h in range(PH):
                        step.mark(dve.max(top[:, h, 0:8], cand[:, h, :]))
                    step.wait()
                    for h in range(PH):
                        step.mark(dve.max_index(at[:, h, 0:8], top[:, h, 0:8], cand[:, h, :]))
                        step.mark(dve.match_replace(cand_rest[:, h, :], top[:, h, 0:8], cand[:, h, :], NEG))
                    step.wait()
                    for h in range(PH):
                        step.mark(dve.max(top[:, h, 8:16], cand_rest[:, h, :]))
                    step.wait()
                    for h in range(PH):
                        step.mark(dve.max_index(at[:, h, 8:16], top[:, h, 8:16], cand_rest[:, h, :]))
                    dve.wait_ge(turned, t)
                    dve.tensor_tensor(pairs[:, 2, :].rearrange("p (h j) -> p h j", h=PH), top[:, :, :],
                                      top[:, :, 0:1].broadcast_to([P, PH, TOPK]), ALU.subtract).then_inc(shifted, 1)
                    step.wait()
                    step.mark(dve.tensor_scalar(digit[:, 0, :, :], at[:, :, :], 4, None, ALU.logical_shift_right))
                    step(dve.tensor_scalar(digit[:, 1, :, :], at[:, :, :], 15, None, ALU.bitwise_and))
                    step(dve.tensor_copy(digit_f[:, :, :, :], digit[:, :, :, :]))
                    for k, pick in ((0, cand), (1, cand_rest)):
                        picked = pick[:, :, :].rearrange("p h (j i) -> p h j i", i=TOPK)
                        step.mark(dve.tensor_tensor(picked, digit_f[:, k, :, :].unsqueeze(3).broadcast_to(square),
                                                    core.iota[:, 0:TOPK].unsqueeze(1).unsqueeze(1).broadcast_to(square),
                                                    ALU.is_equal))
                    step.wait()
                    for k, pick in ((0, cand), (1, cand_rest)):
                        picked = pick[:, :, :].rearrange("p h (j i) -> p h j i", i=TOPK)
                        step.mark(dve.tensor_tensor(picked, picked, where_f[:, :, k, :].unsqueeze(2).broadcast_to(square),
                                                    ALU.mult))
                    step.wait()
                    for k, pick in ((0, cand), (1, cand_rest)):
                        picked = pick[:, :, :].rearrange("p h (j i) -> p (h j) i", i=TOPK)
                        step.mark(dve.tensor_reduce(pairs[:, k, :], picked, AX_X, ALU.add))
                    dve.wait_ge(raised, t + 1)
                    weights = pairs[:, 2, :].rearrange("p (h j) -> p h j", h=PH)
                    step(dve.tensor_reduce(sums[:, :], weights, AX_X, ALU.add))
                    step(dve.reciprocal(sums[:, :], sums[:, :]))
                    dve.tensor_tensor(weights, weights, sums[:, :].unsqueeze(2).broadcast_to([P, PH, TOPK]),
                                      ALU.mult).then_inc(chosen, 1)

                for t in range(tiles):
                    tile(t, chain)


def routing_weights(core, part, pair_keys, pair_weight, tokens, G):
    nc = core.nc
    batches = tokens // OH
    per_loop = 2
    with ExitStack() as ctx:
        hot2 = ctx.enter_context(nc.sbuf_tensor(f"hot2_{core.turn}", [P, 2, OH, KEYS], F32))
        hot1 = ctx.enter_context(nc.sbuf_tensor(f"hot1_{core.turn}", [P, 2, OH, K1], F32))
        with core.stage() as st:
            built, steps = st.sem(), st.sem()
            multiplied, taken = [st.sem(), st.sem()], [st.sem(), st.sem()]

            @st.block.vector
            def _(dve):
                dve.sem_inc(multiplied[0], 1)
                dve.sem_inc(multiplied[1], 1)
                chain = Chain(dve, steps)

                def two(i, step):
                    for b in range(per_loop):
                        n0 = i * (per_loop * OH) + b * OH
                        dve.wait_ge(multiplied[b], i + 1)

                        def spread(row, width):
                            row = pair_weight[:, bass.ds(n0, OH)] if row == 2 else pair_keys[:, row, bass.ds(n0, OH)]
                            return row.unsqueeze(2).broadcast_to([P, OH, width])

                        step.mark(dve.tensor_tensor(hot1[:, b, :, :], spread(0, K1),
                                                    core.iota[:, part * K1:(part + 1) * K1].unsqueeze(1)
                                                    .broadcast_to([P, OH, K1]), ALU.is_equal))
                        step(dve.tensor_tensor(hot2[:, b, :, :], spread(1, KEYS),
                                               core.iota[:, :].unsqueeze(1).broadcast_to([P, OH, KEYS]), ALU.is_equal))
                        dve.tensor_tensor(hot1[:, b, :, :], hot1[:, b, :, :], spread(2, K1), ALU.mult).then_inc(built, 1)

                chain.loop(batches // per_loop, 4, two)

            @st.block.tensor
            def _(pe):
                with pe.Fori(0, batches // per_loop, 1) as i:
                    for b in range(per_loop):
                        pe.wait_ge(built, i * per_loop + b + 1)
                        pe.wait_ge(taken[b], i + 1)
                        for n in range(OH):
                            last = pe.matmul(core.ps[:, b, n * K1:(n + 1) * K1], hot2[:, b, n, :], hot1[:, b, n, :],
                                             start=True, stop=True, skip_group_check=True)
                        last.then_inc(multiplied[b], 1)

            @st.block.scalar
            def _(act):
                act.sem_inc(taken[0], 1)
                act.sem_inc(taken[1], 1)
                with act.Fori(0, batches // per_loop, 1) as i:
                    for b in range(per_loop):
                        n0 = i * (per_loop * OH) + b * OH
                        act.wait_ge(multiplied[b], i + 2)
                        act.activation(G[:, :, bass.ds(n0, OH)],
                                       core.ps[:, b, 0:OH * K1].rearrange("p (n k) -> p k n", n=OH),
                                       ACT.Copy).then_inc(taken[b], 1)


def expert_inputs(core, k, xs, G, tokens):
    seg = core.segments[k]
    with ExitStack() as ctx:
        act_out = ctx.enter_context(core.nc.sbuf_tensor(f"expert_act{core.turn}", [P, 2, tokens], F32))
        with core.stage() as st:
            raised, used = [st.sem(), st.sem()], [st.sem(), st.sem()]

            @st.block.sync
            def _(sp):
                core.feed(sp, k)

            @st.block.tensor
            def _(pe):
                def unit(it, j, last):
                    b = core.wait_split(pe, seg, it, j)
                    pe.wait_ge(raised[j % 2], it * (BODY // 2) + j // 2 + 1)
                    for kt in range(KT):
                        ins = three_passes(pe, core.ps[:, j % 2, 0:tokens],
                                           core.unit.parts(slice(None), b, slice(kt * P, (kt + 1) * P)),
                                           xs.parts(slice(None), kt, slice(0, tokens)), kt == 0, kt == KT - 1)
                    ins.then_inc(core.units_done, 1)

                run_units(pe, seg.n, unit)

            @st.block.scalar
            def _(act):
                for b in range(2):
                    act.sem_inc(raised[b], 1)
                    act.sem_inc(used[b], 1)

                def unit(it, j, last):
                    core.split_next(act, seg, it, j, last)
                    core.wait_done(act, seg, it, j)
                    act.wait_ge(used[j % 2], it * (BODY // 2) + j // 2 + 1)
                    act.activation(act_out[:, j % 2, :], core.ps[:, j % 2, 0:tokens],
                                   ACT.Gelu_apprx_tanh).then_inc(raised[j % 2], 1)

                run_units(act, seg.n, unit)

            @st.block.vector
            def _(dve):
                def unit(it, j, last):
                    core.split_next(dve, seg, it, j, last)
                    dve.wait_ge(raised[j % 2], it * (BODY // 2) + j // 2 + 2)
                    g = G[:, it * BODY + j, :]
                    dve.tensor_tensor(g, g, act_out[:, j % 2, :], ALU.mult).then_inc(used[j % 2], 1)

                run_units(dve, seg.n, unit)


def expert_outputs(core, k, G, tokens, YT):
    seg = core.segments[k]
    with ExitStack() as ctx:
        g = Split(core.nc, ctx, f"expert_g{core.turn}", [P, 2, tokens])
        with core.stage() as st:
            g_hi, g_split = st.sem(), st.sem()

            @st.block.sync
            def _(sp):
                core.feed(sp, k)

            @st.block.scalar
            def _(act):
                def unit(it, j, last):
                    act.wait_ge(core.units_done, seg.start + j + 1 + it * BODY)
                    act.activation(g.hi[:, j % 2, :], G[:, it * BODY + j, :], ACT.Copy).then_inc(g_hi, 1)
                    core.split_next(act, seg, it, j, last)

                run_units(act, seg.n, unit)

            @st.block.vector
            def _(dve):
                def unit(it, j, last):
                    dve.wait_ge(g_hi, it * BODY + j + 1)
                    minus_hi(dve, g.lo[:, j % 2, :], G[:, it * BODY + j, :], g.hi[:, j % 2, :]).then_inc(g_split, 1)
                    core.split_next(dve, seg, it, j, last)

                run_units(dve, seg.n, unit)

            @st.block.tensor
            def _(pe):
                def unit(it, j, start, stop):
                    b = core.wait_split(pe, seg, it, j)
                    pe.wait_ge(g_split, it * BODY + j + 1)
                    for kt in range(KT):
                        last = three_passes(pe, core.ps[:, kt, 0:tokens],
                                            core.unit.parts(slice(None), b, slice(kt * P, (kt + 1) * P)),
                                            g.parts(slice(None), j % 2, slice(None)), start, stop)
                    last.then_inc(core.units_done, 1)

                rounds = seg.n // BODY
                for j in range(BODY):
                    unit(0, j, j == 0, False)
                with pe.Fori(1, rounds - 1, 1) as it:
                    for j in range(BODY):
                        unit(it, j, False, False)
                for j in range(BODY):
                    unit(rounds - 1, j, False, j == BODY - 1)
    with core.stage() as st:
        @st.block.vector
        def _(dve):
            for kt in range(0, KT):
                for s in range(tokens // SEQ):
                    dve.tensor_scalar(YT[:, kt, s * SEQ:(s + 1) * SEQ], core.ps[:, kt, s * SEQ:(s + 1) * SEQ],
                                      core.MOD[:, 40 + kt, s:s + 1], None, ALU.mult)


def park(core, store, X):
    parked = core.parked[:, 0:X.shape[1], :]
    small_loads(core, [(parked, X) if store else (X, parked)])


def peer(core, A, layer, k_first, sets):
    nc = core.nc
    tokens = sets * SEQ
    tiles = tokens // P
    with ExitStack() as scope:
        xs = Split(nc, scope, f"peer_xs{layer}", [P, KT, tokens])
        with ExitStack() as ctx:
            core.X = ctx.enter_context(nc.sbuf_tensor(f"peer_x{layer}", [P, tiles, D], F32))
            park(core, False, core.X[:, :, :])
            norm_transpose(core, [(t, t, t // NX) for t in range(tiles)],
                           lambda m, kt: core.gains[:, 1, kt, m:m + 1], lambda m, kt: core.MOD[:, 24 + kt, m:m + 1], xs)
        pair_keys = scope.enter_context(nc.sbuf_tensor(f"pair_keys{layer}", [P, 2, tokens], BF16))
        pair_weight = scope.enter_context(nc.sbuf_tensor(f"pair_weight{layer}", [P, tokens], F32))
        with ExitStack() as ctx:
            qT = ctx.enter_context(nc.sbuf_tensor(f"queries{layer}", [P, 32, tokens], F32))
            keysT = ctx.enter_context(nc.sbuf_tensor(f"keys{layer}", [P, 32, KEYS], F32))
            small_loads(core, [(keysT[:, :, :], A[f"keys{layer}"])])

            def keep(eng, ps, f, slot):
                if eng is core.nc.scalar:
                    return eng.activation(qT[:, f, :], ps, ACT.Copy)
                return eng.tensor_copy(qT[:, f, :], ps)

            product_by_feature(core, k_first, lambda kt: xs.parts(slice(None), kt, slice(None)), tokens, keep)
            choose_experts(core, keysT, qT, tiles, pair_keys, pair_weight)
        G = scope.enter_context(nc.sbuf_tensor(f"routing{layer}", [P, K1, tokens], F32))
        YT = G[:, 0:KT, :]
        per = D // tokens
        for part in range(PHASES):
            routing_weights(core, part, pair_keys, pair_weight, tokens, G)
            expert_inputs(core, k_first + 1 + 2 * part, xs, G, tokens)
            expert_outputs(core, k_first + 2 + 2 * part, G, tokens, YT)
            X = G[:, KT:KT + per * tiles, :].rearrange("p (t a) b -> p t (a b)", t=tiles)
            park(core, False, X)
            with core.stage() as st:
                turned, added = st.sem(), st.sem()

                @st.block.tensor
                def _(pe):
                    for t in range(tiles):
                        for kt in range(KT):
                            last = pe.transpose(core.ps[:, 2 * t + kt // 4, (kt % 4) * P:(kt % 4 + 1) * P],
                                                YT[:, kt, t * P:(t + 1) * P], core.ident)
                        last.then_inc(turned, 1)

                @st.block.vector
                def _(dve):
                    for t in range(tiles):
                        dve.wait_ge(turned, t + 1)
                        for h in range(2):
                            x = X[:, t, h * HALF:(h + 1) * HALF]
                            dve.tensor_tensor(x, x, core.ps[:, 2 * t + h, :], ALU.add)
            park(core, True, X)


def ssm_parameters(core, A, ctx):
    nc = core.nc

    def sb(name, shape):
        return ctx.enter_context(nc.sbuf_tensor(name, shape, F32))

    mag = sb("ssm_mag", [P, STILES])
    phases = sb("ssm_phases", [P, 2, SPAD, 1 << SEED])
    power = sb("ssm_power", [P, 3, LEVELS, SPAD])
    inject = sb("ssm_inject", [P, 16, 2, P])
    readout = sb("ssm_readout", [P, STILES, 2, 32])
    with ExitStack() as tmp:
        def t(name, shape):
            return tmp.enter_context(nc.sbuf_tensor(name, shape, F32))

        lam = t("ssm_lam", [P, 3, STILES])
        b = t("ssm_b", [P, 2, STILES, CG])
        c = t("ssm_c", [P, 2, STILES, CG])
        w = t("ssm_work", [P, 12, STILES])
        wide = t("ssm_wide", [P, 2, STILES, CG])
        small_loads(core, [(lam[:, :, :], A["ssm_lam"]), (b[:, :, :, :], A["ssm_b"]), (c[:, :, :, :], A["ssm_c"])])
        BD = t("ssm_blocks", [P, 2, STILES, 32])
        lr, li, ls = lam[:, 0, :], lam[:, 1, :], lam[:, 2, :]
        with core.stage() as st:
            steps, asteps, ready, sined = (st.sem() for _ in range(4))

            @st.block.scalar
            def _(act):
                step = Chain(act, asteps)
                step(act.activation(w[:, 0, :], ls, ACT.Exp))
                act.wait_ge(ready, 1)
                step(act.activation(mag[:, :], w[:, 1, :], ACT.Exp))
                act.activation(w[:, 4:6, :], w[:, 4:6, :], ACT.Sin).then_inc(sined, 1)

            @st.block.vector
            def _(dve):
                step = Chain(dve, steps)
                step.mark(dve.memset(BD[:, :, :, :], 0.0))
                step.mark(dve.memset(power[:, :, :, STILES:SPAD], 0.0))
                step.mark(dve.memset(phases[:, :, STILES:SPAD, :], 0.0))
                step(dve.memset(readout[:, :, :, :], 0.0))
                dve.wait_ge(asteps, 1)
                step.mark(dve.tensor_tensor(w[:, 1, :], lr, w[:, 0, :], ALU.mult))
                step(dve.tensor_tensor(w[:, 2, :], li, w[:, 0, :], ALU.mult))
                step.mark(dve.tensor_scalar(w[:, 4, :], w[:, 2, :], 0.25 * TWO_PI, None, ALU.add))
                step(dve.tensor_copy(w[:, 5, :], w[:, 2, :]))
                step(dve.tensor_scalar(w[:, 6:8, :], w[:, 4:6, :], 1.0 / TWO_PI, None, ALU.mult))
                step(dve.tensor_scalar(w[:, 6:8, :], w[:, 6:8, :], ROUND, -ROUND, ALU.add, ALU.add))
                for part in (6.28125, 0.0019350051879882812, 3.019916e-07):
                    step(dve.scalar_tensor_tensor(out=w[:, 4:6, :], in0=w[:, 6:8, :], scalar=-part,
                                                  in1=w[:, 4:6, :], op0=ALU.mult, op1=ALU.add))
                step(dve.tensor_scalar(w[:, 4:6, :], w[:, 4:6, :], 3.1415925, -3.1415925, ALU.min, ALU.max))
                dve.engine_nop().then_inc(ready, 1)
                dve.wait_ge(sined, 1)
                cos, sin, nsin = (power[:, i, 0, 0:STILES] for i in range(3))
                step.mark(dve.tensor_copy(cos, w[:, 4, :]))
                step(dve.tensor_copy(sin, w[:, 5, :]))
                step(dve.tensor_scalar(nsin, sin, -1.0, None, ALU.mult))
                for k in range(1, LEVELS):
                    c0, s0 = power[:, 0, k - 1, 0:STILES], power[:, 1, k - 1, 0:STILES]
                    step.mark(dve.tensor_tensor(w[:, 6, :], c0, c0, ALU.mult))
                    step.mark(dve.tensor_tensor(w[:, 7, :], s0, s0, ALU.mult))
                    step(dve.tensor_tensor(w[:, 8, :], c0, s0, ALU.mult))
                    step.mark(dve.tensor_tensor(power[:, 0, k, 0:STILES], w[:, 6, :], w[:, 7, :], ALU.subtract))
                    step.mark(dve.tensor_scalar(power[:, 1, k, 0:STILES], w[:, 8, :], 2.0, None, ALU.mult))
                    step(dve.tensor_scalar(power[:, 2, k, 0:STILES], w[:, 8, :], -2.0, None, ALU.mult))
                a_r, a_i, den, cr, ci, x = (w[:, i, :] for i in (1, 2, 3, 6, 7, 8))
                step.mark(dve.tensor_tensor(a_r, mag[:, :], cos, ALU.mult))
                step.mark(dve.tensor_tensor(a_i, mag[:, :], sin, ALU.mult))
                step.mark(dve.tensor_tensor(den, lr, lr, ALU.mult))
                step(dve.tensor_tensor(x, li, li, ALU.mult))
                step.mark(dve.tensor_scalar(a_r, a_r, -1.0, None, ALU.add))
                step(dve.tensor_tensor(den, den, x, ALU.add))
                step(dve.reciprocal(den, den))
                step.mark(dve.tensor_tensor(cr, a_r, lr, ALU.mult))
                step(dve.tensor_tensor(x, a_i, li, ALU.mult))
                step.mark(dve.tensor_tensor(cr, cr, x, ALU.add))
                step(dve.tensor_tensor(ci, a_i, lr, ALU.mult))
                step(dve.tensor_tensor(x, a_r, li, ALU.mult))
                step(dve.tensor_tensor(ci, ci, x, ALU.subtract))
                step.mark(dve.tensor_tensor(cr, cr, den, ALU.mult))
                step(dve.tensor_tensor(ci, ci, den, ALU.mult))

                def over(y):
                    return y.unsqueeze(2).broadcast_to([P, STILES, CG])

                for part, (p0, p1, op) in enumerate(((cr, ci, ALU.subtract), (ci, cr, ALU.add))):
                    step.mark(dve.tensor_tensor(wide[:, 0, :, :], b[:, 0, :, :], over(p0), ALU.mult))
                    step(dve.tensor_tensor(wide[:, 1, :, :], b[:, 1, :, :], over(p1), ALU.mult))
                    for g in range(2):
                        rows = slice(64 * g, 64 * g + 64)
                        step.mark(dve.tensor_tensor(BD[rows, part, :, g * CG:(g + 1) * CG], wide[rows, 0, :, :],
                                                    wide[rows, 1, :, :], op))
                    step.wait()
                for g in range(2):
                    rows = slice(64 * g, 64 * g + 64)
                    dve.tensor_copy(readout[rows, :, 0, g * CG:(g + 1) * CG], c[rows, 0, :, :])
                    dve.tensor_scalar(readout[rows, :, 1, g * CG:(g + 1) * CG], c[rows, 1, :, :], -1.0, None, ALU.mult)

        with core.stage() as st:
            turned, taken = st.sem(), st.sem()

            @st.block.tensor
            def _(pe):
                for i in range(16):
                    if i >= 2:
                        pe.wait_ge(taken, i - 1)
                    for part in range(2):
                        last = pe.transpose(core.ps[:, i % 2, part * P:(part + 1) * P],
                                            BD[:, part, 4 * i:4 * i + 4, :].rearrange("p q c -> p (q c)"), core.ident)
                    last.then_inc(turned, 1)

            @st.block.scalar
            def _(act):
                for i in range(16):
                    act.wait_ge(turned, i + 1)
                    act.activation(inject[:, i, :, :].rearrange("p r s -> p (r s)"), core.ps[:, i % 2, 0:2 * P],
                                   ACT.Copy).then_inc(taken, 1)
    with ExitStack() as tmp:
        prod = tmp.enter_context(nc.sbuf_tensor("ssm_phase_products", [P, 4, STILES, 1 << (SEED - 1)], F32))
        with core.stage() as st:
            steps = st.sem()

            @st.block.vector
            def _(dve):
                step = Chain(dve, steps)
                tiles = slice(0, STILES)
                step.mark(dve.memset(phases[:, 0, tiles, 0:1], 1.0))
                step(dve.memset(phases[:, 1, tiles, 0:1], 0.0))
                for k in range(SEED):
                    n = 1 << k
                    re, im = phases[:, 0, tiles, 0:n], phases[:, 1, tiles, 0:n]
                    c0, s0 = (power[:, x, k, tiles].unsqueeze(2).broadcast_to([P, STILES, n]) for x in range(2))
                    for x, (a, b) in enumerate(((re, c0), (im, s0), (im, c0), (re, s0))):
                        step.mark(dve.tensor_tensor(prod[:, x, :, 0:n], a, b, ALU.mult))
                    step.wait()
                    step.mark(dve.tensor_tensor(phases[:, 0, tiles, n:2 * n], prod[:, 0, :, 0:n], prod[:, 1, :, 0:n],
                                                ALU.subtract))
                    step(dve.tensor_tensor(phases[:, 1, tiles, n:2 * n], prod[:, 2, :, 0:n], prod[:, 3, :, 0:n], ALU.add))
    return mag, power, phases, inject, readout


def ssm_scan(core, U, mag, power, phases, inject, readout, YD):
    nc = core.nc
    T = 2 * SEQ
    GROUPS = STILES // 4
    with ExitStack() as ctx:
        def sb(name, shape):
            return ctx.enter_context(nc.sbuf_tensor(name, shape, F32))

        u = sb("scan_u", [P, 2, T])
        inj = sb("scan_inject", [P, 2, 2, P])
        rd = sb("scan_readout", [P, 2, 4, 2, 32])
        phase = sb("scan_phase", [P, 2, 2, T])
        part = sb("scan_part", [P, 2, T // 2])
        prod = sb("scan_prod", [P, 4, T])
        turning = sb("scan_turning", [P, 2, T])
        state = sb("scan_state", [P, 2, T])
        back = sb("scan_back", [P, 4, SEQ])
        with core.stage() as st:
            (staged, driven, turned_dve, turned, scanned, back_dve, back_pool, read, kept, parted,
             doubled) = (st.sem() for _ in range(11))

            def pick(t):
                return slice(t, t + 1) if isinstance(t, int) else bass.ds(t, 1)

            def bodies(eng, body):
                body(0, True, False)
                with eng.Fori(1, GROUPS // 2 - 1, 1) as i:
                    body(i, False, False)
                body(GROUPS // 2 - 1, False, True)

            @st.block.scalar
            def _(act):
                def stage(g, b):
                    act.activation(u[:, b, :], U[:, g, :], ACT.Copy)
                    act.activation(inj[:, b, :, :], inject[:, g, :, :], ACT.Copy)
                    act.activation(rd[:, b, :, :, :], readout[:, bass.ds(g * 4, 4), :, :] if not isinstance(g, int)
                                   else readout[:, g * 4:g * 4 + 4, :, :], ACT.Copy).then_inc(staged, 1)

                def table(t, b):
                    act.activation(phase[:, b, :, 0:1 << SEED], phases[:, :, t, :], ACT.Copy).then_inc(parted, 1)
                    for k in range(SEED, LEVELS):
                        n = 1 << k
                        act.wait_ge(parted, t * 5 + (k - SEED) + 1)
                        if k > SEED:
                            act.wait_ge(doubled, t * 4 + (k - SEED))
                        act.activation(part[:, 0, 0:n], phase[:, b, 1, 0:n], ACT.Copy, scale=power[:, 2, k, pick(t)])
                        act.activation(part[:, 1, 0:n], phase[:, b, 0, 0:n], ACT.Copy,
                                       scale=power[:, 1, k, pick(t)]).then_inc(parted, 1)

                act.sem_inc(read, 2)
                act.sem_inc(kept, 1)
                act.sem_inc(turned_dve, 1)
                stage(0, 0)
                table(0, 0)

                def body(i, first, last):
                    for x in range(8):
                        t = i * 8 + x
                        if not (last and x == 7):
                            act.wait_ge(back_dve, t + 1)
                            act.wait_ge(back_pool, t + 1)
                            act.wait_ge(doubled, t * 4 + 4)
                            table(t + 1, (x + 1) % 2)
                        if x % 4 == 1:
                            g, h = i * 2 + x // 4, x // 4
                            if not (first and x == 1):
                                act.wait_ge(read, g * 4 + 2)
                                act.activation(YD[:, g - 1, :], core.ps[:, 4 + (h + 1) % 2, 0:SEQ],
                                               ACT.Copy).then_inc(kept, 1)
                            if not (last and x == 5):
                                stage(g + 1, (h + 1) % 2)

                bodies(act, body)
                act.wait_ge(read, STILES + 2)
                act.activation(YD[:, GROUPS - 1, :], core.ps[:, 5, 0:SEQ], ACT.Copy)

            @st.block.tensor
            def _(pe):
                def drive(t, x):
                    q, b = x % 4, (x // 4) % 2
                    rows = slice(32 * q, 32 * q + 32)
                    for r in range(2):
                        last = pe.matmul(core.ps[:, 2 * (x % 2) + r, :], inj[rows, b, r, :], u[rows, b, :],
                                         start=True, stop=True)
                    last.then_inc(driven, 1)

                def readout_of(x):
                    q, b = x % 4, (x // 4) % 2
                    for n, r in enumerate((0, 0, 1, 1)):
                        last = pe.matmul(core.ps[32 * q:32 * q + 32, 4 + b, 0:SEQ], rd[:, b, q, r, :], back[:, n, :],
                                         start=(n == 0), stop=(n == 3), skip_group_check=True)
                    last.then_inc(read, 1)

                pe.wait_ge(staged, 1)
                drive(0, 0)

                def body(i, first, last):
                    for x in range(8):
                        t = i * 8 + x
                        if not (last and x == 7):
                            pe.wait_ge(turned_dve, t + 1)
                            if x % 4 == 3:
                                pe.wait_ge(staged, i * 2 + x // 4 + 2)
                            drive(t + 1, x + 1)
                        if not (first and x == 0):
                            pe.wait_ge(back_dve, t + 1)
                            pe.wait_ge(back_pool, t + 1)
                            if x % 4 == 1:
                                pe.wait_ge(kept, i * 2 + x // 4)
                            readout_of((x + 7) % 8)

                bodies(pe, body)
                pe.wait_ge(back_dve, STILES + 1)
                pe.wait_ge(back_pool, STILES + 1)
                readout_of(7)

            @st.block.vector
            def _(dve):
                def double(t, b, k):
                    n = 1 << k
                    dve.wait_ge(parted, t * 5 + (k - SEED) + 2)
                    if k > SEED:
                        dve.wait_ge(doubled, t * 4 + (k - SEED))
                    for r in range(2):
                        last = dve.scalar_tensor_tensor(out=phase[:, b, r, n:2 * n], in0=phase[:, b, r, 0:n],
                                                        scalar=power[:, 0, k, pick(t)], in1=part[:, r, 0:n],
                                                        op0=ALU.mult, op1=ALU.add)
                    last.then_inc(doubled, 1)

                def turn_back(t, b):
                    dve.wait_ge(scanned, t + 1)
                    dve.wait_ge(read, t + 1)
                    late = slice(SEQ, T)
                    dve.tensor_tensor(back[:, 0, :], state[:, 0, late], phase[:, b, 0, late], ALU.mult)
                    dve.scalar_tensor_tensor(out=back[:, 1, :], in0=state[:, 1, late], scalar=-1.0,
                                             in1=phase[:, b, 1, late], op0=ALU.mult, op1=ALU.mult).then_inc(back_dve, 1)

                dve.memset(phase[:, 1, :, :], 0.0)
                dve.memset(state[:, :, :], 0.0).then_inc(scanned, 1)
                for k in range(SEED, LEVELS):
                    double(0, 0, k)

                def body(i, first, last):
                    for x in range(8):
                        t, b = i * 8 + x, x % 2
                        nxt = not (last and x == 7)
                        turn_back(t, 1 - b)
                        dve.wait_ge(driven, t + 1)
                        dve.wait_ge(doubled, t * 4 + 4)
                        re, im = core.ps[:, 2 * b, :], core.ps[:, 2 * b + 1, :]
                        cos, sin = phase[:, b, 0, :], phase[:, b, 1, :]
                        dve.tensor_tensor(prod[:, 0, :], re, cos, ALU.mult)
                        dve.tensor_tensor(prod[:, 1, :], im, sin, ALU.mult)
                        if nxt:
                            double(t + 1, 1 - b, SEED)
                        dve.tensor_tensor(prod[:, 2, :], im, cos, ALU.mult)
                        dve.tensor_tensor(prod[:, 3, :], re, sin, ALU.mult).then_inc(turned_dve, 1)
                        if nxt:
                            double(t + 1, 1 - b, SEED + 1)
                            double(t + 1, 1 - b, SEED + 2)
                        dve.wait_ge(turned, t * 2 + 1)
                        dve.wait_ge(back_pool, t + 1)
                        scale = mag[:, pick(t)].broadcast_to([P, T])
                        dve.tensor_tensor_scan(state[:, 0, :], scale, turning[:, 0, :], 0.0, ALU.mult, ALU.add)
                        if nxt:
                            double(t + 1, 1 - b, SEED + 3)
                        dve.wait_ge(turned, t * 2 + 2)
                        dve.tensor_tensor_scan(state[:, 1, :], scale, turning[:, 1, :], 0.0, ALU.mult,
                                               ALU.add).then_inc(scanned, 1)

                bodies(dve, body)
                turn_back(STILES, 1)

            @st.block.gpsimd
            def _(pool):
                late = slice(SEQ, T)

                def turn_back(t, b):
                    pool.wait_ge(scanned, t + 1)
                    pool.wait_ge(read, t + 1)
                    pool.tensor_tensor(back[:, 2, :], state[:, 0, late], phase[:, b, 1, late], ALU.mult)
                    pool.tensor_tensor(back[:, 3, :], state[:, 1, late], phase[:, b, 0, late],
                                       ALU.mult).then_inc(back_pool, 1)

                def body(i, first, last):
                    for x in range(8):
                        t = i * 8 + x
                        turn_back(t, 1 - x % 2)
                        pool.wait_ge(turned_dve, t + 2)
                        pool.tensor_tensor(turning[:, 0, :], prod[:, 0, :], prod[:, 1, :], ALU.add).then_inc(turned, 1)
                        pool.tensor_tensor(turning[:, 1, :], prod[:, 2, :], prod[:, 3, :],
                                           ALU.subtract).then_inc(turned, 1)

                bodies(pool, body)
                turn_back(STILES, 1)


def ssm_mixer(core, A, k_in, k_out):
    nc = core.nc
    with ExitStack() as ctx:
        def sb(name, shape):
            return ctx.enter_context(nc.sbuf_tensor(name, shape, F32))

        gate_row = sb("ssm_gate_row", [P, 1, D])
        spread_rows(core, 16, 1, gate_row)
        U = sb("ssm_u", [P, 16, 2 * SEQ])
        before = ctx.enter_context(ExitStack())
        xs = Split(nc, before, "ssm_xs", [P, KT, 2 * SEQ])
        norm_transpose(core, [(t, (t + NX) % NT, t // NX) for t in range(NT)],
                       lambda m, kt: core.gains[:, 0, kt, m:m + 1], lambda m, kt: core.MOD[:, kt, m:m + 1], xs)
        def keep(eng, ps, f, slot):
            if eng is core.nc.scalar:
                return eng.activation(U[:, f, :], ps, ACT.Copy)
            return eng.tensor_copy(U[:, f, :], ps)

        product_by_feature(core, k_in, lambda kt: xs.parts(slice(None), kt, slice(None)), 2 * SEQ, keep)
        before.close()
        YD = sb("ssm_y", [P, 16, SEQ])
        with core.stage() as st:
            @st.block.vector
            def _(dve):
                for half in range(2):
                    fwd = U[:, 0:8, half * SEQ:(half + 1) * SEQ]
                    dve.tensor_copy(U[:, 8:16, half * SEQ:(half + 1) * SEQ], fwd[:, :, ::-1])
        with ExitStack() as inner:
            mag, power, phases, inject, readout = ssm_parameters(core, A, inner)
            ssm_scan(core, U, mag, power, phases, inject, readout, YD)
        with core.stage() as st:
            steps, summed = st.sem(), st.sem()

            @st.block.vector
            def _(dve):
                step = Chain(dve, steps)
                step(dve.tensor_tensor(YD[:, 0:8, :], YD[:, 0:8, :], YD[:, 8:16, ::-1], ALU.add))
                for f in range(KT):
                    last = dve.scalar_tensor_tensor(out=YD[:, f, :], in0=U[:, f, SEQ:2 * SEQ],
                                                    scalar=core.columns("ssm_d")[:, f:f + 1], in1=YD[:, f, :],
                                                    op0=ALU.mult, op1=ALU.add)
                last.then_inc(summed, 1)

            @st.block.scalar
            def _(act):
                act.wait_ge(summed, 1)
                act.activation(YD[:, 8:16, :], YD[:, 0:8, :], ACT.Gelu_apprx_tanh)
        ys = Split(nc, ctx, "ssm_ys", [P, KT, SEQ])
        split_tensor(core, YD[:, 8:16, :], ys, 4)
        out = U[:, :, :].rearrange("p (t s a) b -> p t s (a b)", t=NX, s=4)

        def take(eng, c, t, h, ps):
            return eng.activation(out[:, t, c, h * HALF:(h + 1) * HALF], ps, ACT.Sigmoid if c else ACT.Copy)

        product_by_token(core, k_out, lambda c, kt, t: ys.parts(slice(None), kt, slice(t * P, (t + 1) * P)), NX, KT, take,
                         ("scalar", "scalar"))
        with core.stage() as st:
            steps = st.sem()

            @st.block.vector
            def _(dve):
                step = Chain(dve, steps)
                step(dve.tensor_tensor(out[:, :, 0, :], out[:, :, 0, :], out[:, :, 1, :], ALU.mult))
                step(dve.tensor_tensor(out[:, :, 0, :], out[:, :, 0, :],
                                       gate_row[:, :, :].broadcast_to([P, NX, D]), ALU.mult))
                dve.tensor_tensor(core.X[:, 0:NX, :], core.X[:, 0:NX, :], out[:, :, 0, :], ALU.add)


def program(nc, A, out, stop=99):
    with ExitStack() as ctx:
        core = Core(nc, ctx)

        def sb(name, shape):
            return ctx.enter_context(nc.sbuf_tensor(name, shape, F32))

        core.ring = sb("ring", [P, RING, D])
        core.unit = Split(nc, ctx, "unit", [P, 2, D])
        core.parked = nc.dram_tensor("parked_x", (P, NT, D), F32, kind="Internal").ap()
        core.cols = sb("cols", [P, NCOLS])
        consts = sb("consts", [P, 2 * P])
        core.ident, core.iota = consts[:, 0:P], consts[:, P:2 * P]
        core.silu_c = sb("silu_c", [P, KT, 2])
        core.MOD = sb("mod", [P, 48, 2])
        core.gains = sb("mod_gains", [P, 2, KT, 2])
        core.ps = ctx.enter_context(nc.psum_tensor("banks", [P, BANKS, HALF], F32))
        start = 0
        for name in SEGMENTS:
            core.segments.append(Segment(A[name], start))
            core.segments[-1].whole = name.startswith("s_ada")
            start += core.segments[-1].n

        with core.stage() as st:
            @st.block.sync
            def _(sp):
                for v in range(RING):
                    sp.dma_start(core.ring[:, v, :], core.segments[0].ap[v]).then_inc(core.loaded[v], 16)

        def tokens_in(name, tiles, scope):
            core.X = scope.enter_context(nc.sbuf_tensor(name, [P, tiles, D], F32))

        with ExitStack() as scope:
            tokens_in("X_first", NT, scope)
            small_loads(core, [(core.X[:, 0:NX, :], A["x"].rearrange("b (t p) d -> p (b t) d", p=P)),
                               (core.cols[:, :], A["cols"]), (consts[:, :], A["k_consts"])])
            with core.stage() as st:
                @st.block.scalar
                def _(act):
                    act.sem_inc(core.units_done, 2)
                    core.split_hi(act, 0, 0)
                    act.activation(core.silu_c[:, :, 0], core.columns("c"), ACT.Silu)
                    act.activation(core.silu_c[:, :, 1], core.columns("cc"), ACT.Silu)

                @st.block.vector
                def _(dve):
                    core.split_lo(dve, 0, 0)
            first_block(core, A)
            modulation(core, 8, "ada_b0")
            chunk_mixer(core, A, 9, 10)
            park(core, True, core.X[:, :, :])
        if stop > 2:
            peer(core, A, 0, 11, 2)
        if stop > 3:
            with ExitStack() as scope:
                tokens_in("X_second", NT, scope)
                park(core, False, core.X[:, :, :])
                modulation(core, 16, "ada_b1")
                ssm_mixer(core, A, 17, 18)
                park(core, True, core.X[:, :, :])
        if stop > 4:
            peer(core, A, 1, 19, 1)

        tokens_in("X_last", NT, ctx)
        park(core, False, core.X[:, :, :])
        final = sb("final", [P, NX, D])
        row = sb("final_row", [P, D])
        stat = sb("final_stat", [P, NX])
        small_loads(core, [(row[:, :], A["gain_rows"][4:5, :].broadcast_to([P, D]))])
        sums_of_squares(core, [core.X[:, t, :] for t in range(NX)], stat)
        inverse_rms(core, stat, NX, D)
        with core.stage() as st:
            normed, stored = st.sem(), st.sem()

            @st.block.vector
            def _(dve):
                for t in range(NX):
                    dve.scalar_tensor_tensor(out=final[:, t, :], in0=core.X[:, t, :], scalar=stat[:, t:t + 1],
                                             in1=row[:, :], op0=ALU.mult, op1=ALU.mult).then_inc(normed, 1)

            @st.block.sync
            def _(sp):
                sp.wait_ge(normed, NX)
                sp.dma_start(out.rearrange("b (t p) d -> p (b t) d", p=P),
                             final[:, :, :] if stop > 4 else core.X[:, 0:NX, :]).then_inc(stored, 16)
                sp.wait_ge(stored, 16)


SEGMENTS = ["s_features", "s_tokens", "s_w_mlstm", "s_w_diff", "s_w_ret", "s_w_out", "s_ffn_in", "s_ffn_out",
            "s_ada0", "s_cm_in", "s_cm_out", "s_wq0", "s_u00", "s_v00", "s_u01", "s_v01",
            "s_ada1", "s_ssm_in", "s_ssm_out", "s_wq1", "s_u10", "s_v10", "s_u11", "s_v11"]


def constants():
    f = np.float32
    ident = np.eye(P, dtype=f)
    iota = np.broadcast_to(np.arange(P, dtype=f), (P, P))
    sel = np.zeros((HEADS, HEADS, P), f)
    for h in range(HEADS):
        sel[h, h] = 1.0
    s = np.arange(P)[:, None]
    t = np.concatenate([np.arange(SEQ), np.arange(P)])[None, :]
    lag = (t - s).astype(f)
    scale = f(HD) ** f(-0.5)
    mask = np.where(lag >= 0, scale, 0).astype(f)
    log_gamma = np.log(1.0 - 2.0 ** (-5.0 - np.arange(HEADS, dtype=np.float64)))
    ret = np.where(lag[:, None] >= 0, np.exp(log_gamma[None, :, None] * np.maximum(lag, 0)[:, None]) * scale, 0)
    slopes = 2.0 ** (-8.0 * (np.arange(DH) + 1.0) / DH)
    tq = np.concatenate([np.broadcast_to(s, (P, P)), np.broadcast_to(s + P, (P, SEQ))], 1)
    tk = np.concatenate([np.arange(P), np.arange(SEQ)])[None, :]
    alibi = np.where((tk // 64 <= tq // 64)[:, None], -slopes[None, :, None] * np.abs(tq - tk)[:, None], NEG)

    def sincos(pos, dim):
        omega = (1.0 / (f(10000.0) ** (np.arange(dim // 2, dtype=f) / f(dim // 2)))).astype(f)
        ang = pos[:, None] * omega[None, :]
        return np.concatenate([np.sin(ang), np.cos(ang)], -1)

    grid = 64
    r = np.repeat(np.arange(SEQ // grid, dtype=f), grid)
    c = np.tile(np.arange(grid, dtype=f), SEQ // grid)
    pos = np.concatenate([sincos(r, D // 2), sincos(c, D // 2)], -1).astype(f)
    return {
        "k_consts": np.concatenate([ident, iota], 1),
        "k_sel": sel,
        "k_mask": mask,
        "k_retention": ret.astype(f),
        "k_alibi": alibi.astype(f),
        "k_positions": pos.reshape(NX, P, D).transpose(1, 0, 2),
    }


def layouts(i):
    def column(v):
        return np.reshape(v, (-1, P)).T

    def by_feature(w):
        k, n = w.shape
        return w.reshape(k // P, P, n // P, P).transpose(2, 1, 0, 3).reshape(n // P, P, k)

    def by_token(w):
        k, n = w.shape
        return w.reshape(k // P, P, n // D, D).transpose(2, 0, 1, 3).reshape(-1, P, D)

    w_in = i["w_in"][0]
    cut = dict(zip("mq mk mv mo mif dq dk dv rq rk rv rg gm gd gr".split(),
                   np.split(w_in, np.cumsum([D] * 4 + [8] + [D] * 9), axis=1)))
    g = i["norm_gains"][0]
    pad = np.zeros((P - HEADS,), np.float32)
    ffn = i["w_ffn_in"][0].reshape(D, 2, FT, P).transpose(0, 2, 1, 3).reshape(D, 2 * FFN)
    cols = [column(g[0]), column(g[2]), column(i["norm1_g_2"][0]), column(i["norm1_g_2"][1]),
            column(i["norm2_g_2"][0]), column(i["norm2_g_2"][1]), column(i["ssm_d_2"][0]),
            column(i["ada_b_2"][0]), column(i["ada_b_2"][1]), column(i["mlstm_conv"][0]),
            i["cm_b_s_2"][0].T,
            np.concatenate([i["mlstm_gate_bias"][0, 0], pad])[:, None],
            np.concatenate([i["mlstm_gate_bias"][0, 1], pad])[:, None],
            column(i["c_2"][0]), column(i["c_ctx_2"])]

    def states(v):
        rest = v.shape[3:]
        v = v.reshape(2, 32, 2, 64, *rest)
        v = np.moveaxis(v, (2, 3, 0, 1), (0, 1, 2, 3))
        return v.reshape(P, STILES, *rest)

    step = np.broadcast_to(i["ssm_log_step_2"][0][:, :, None], (2, 64, 64))
    a = {
        "x": i["x"], "ctx": i["ctx_2"],
        "cols": np.concatenate(cols, 1),
        "gain_rows": np.stack([g[1], g[3], i["cm_ln_g_2"][0], i["cm_ln_b_2"][0], i["final_g_2"]]),
        "diff_lambda": i["diff_lambda"].reshape(1, 256), "diff_subln": i["diff_subln"].reshape(1, P),
        "w_gate": cut["mif"].reshape(KT, P, 8).transpose(1, 0, 2),
        "cm_ws": i["cm_w_s_2"][0].transpose(2, 0, 1),
        "s_features": by_feature(np.concatenate([cut[n] for n in ("dq", "dk", "mq", "mk", "rq", "rk")], 1)),
        "s_tokens": by_token(np.concatenate([cut[n] for n in ("mv", "rv", "dv", "mo", "gm", "gd", "gr", "rg")], 1)),
        "s_w_mlstm": by_token(i["w_mlstm_out"][0]), "s_w_diff": by_token(i["w_diff_out"][0]),
        "s_w_ret": by_token(i["w_ret_out"][0]),
        "s_w_out": by_token(i["w_out"][0]),
        "s_ffn_in": by_feature(ffn),
        "s_ffn_out": by_token(i["w_ffn_out"][0]),
        "s_cm_in": by_token(i["cm_w_in_2"][0]),
        "s_cm_out": by_token(i["cm_w_out_2"][0]),
        "s_ssm_in": by_feature(i["ssm_w_in_2"][0]),
        "s_ssm_out": by_token(i["ssm_w_out_2"][0]),
        "ssm_lam": np.stack([states(i["ssm_lam_re_2"][0]), states(i["ssm_lam_im_2"][0]), states(step)], 1),
        "ssm_b": np.stack([states(i["ssm_b_re_2"][0]), states(i["ssm_b_im_2"][0])], 1),
        "ssm_c": np.stack([states(i[n][0].transpose(0, 1, 3, 2)) for n in ("ssm_c_re_2", "ssm_c_im_2")], 1),
    }
    for l in range(2):
        a[f"s_ada{l}"] = by_feature(i["ada_w_2"][l])
        a[f"s_wq{l}"] = by_feature(i["peer_w_q_2"][l])
        a[f"keys{l}"] = i["peer_keys_2"][l].reshape(16, KEYS, 2, P).transpose(3, 0, 2, 1).reshape(P, 32, KEYS)
        u = i["peer_u_2"][l].reshape(KEYS, KEYS, KT, P).transpose(0, 3, 2, 1).reshape(KEYS, P, D)
        v = i["peer_v_2"][l].reshape(KEYS, KEYS, D)
        for part in range(PHASES):
            a[f"s_u{l}{part}"] = u[part * K1:(part + 1) * K1]
            a[f"s_v{l}{part}"] = v[part * K1:(part + 1) * K1]
    a.update(constants())
    return {n: np.ascontiguousarray(v) for n, v in a.items()}


def kernel(**inputs):
    import concourse.bacc as bacc
    from concourse.bass_utils import run_bass_kernel_spmd as run

    laid = layouts({n: np.asarray(v) for n, v in inputs.items()})
    nc = bacc.Bacc("TRN2", target_bir_lowering=False, num_devices=1)
    arrays = {f"in_{n}": v for n, v in laid.items()}
    aps = {n: nc.dram_tensor(f"in_{n}", v.shape, mybir.dt.from_np(v.dtype), kind="ExternalInput").ap()
           for n, v in laid.items()}
    out = nc.dram_tensor("out", (1, SEQ, D), F32, kind="ExternalOutput").ap()
    program(nc, aps, out)
    r = run(nc, [arrays], core_ids=[0])
    return r.results[0]["out"]
```

```python
from contextlib import ExitStack

import numpy as np

import concourse.bass as bass
from concourse import mybir

F32 = mybir.dt.float32
F32R = mybir.dt.float32r
BF16 = mybir.dt.bfloat16
U32 = mybir.dt.uint32
ALU = mybir.AluOpType
ACT = mybir.ActivationFunctionType
AX_X = mybir.AxisListType.X

P = 128
D = 1024
KT = D // P
SEQ = 256
NX = SEQ // P
NT = 2 * NX
HALF = 512
BANKS = 8
RING = 4
BODY = 8
FFN = 2816
FT = FFN // P
EPS = 1e-6
HEADS = 4
HD = 256
DH = 8
DCOLS = 384
NEG = -3.0e38
PH = 8
TOPK = 16
KEYS = 128
PAIRS = PH * TOPK
PARTS = (2, 1)
OH = 4
LEVELS = 9
SEED = 5
SPAD = 68
STILES = 64
CG = 16
LAM_INIT = 0.8 - 0.6 * float(np.exp(-0.3 * 0))
TWO_PI = 2.0 * float(np.pi)
ROUND = 1.5 * 2.0 ** 23

COLS = {}
_at = 0
for _name, _n in (("g0", KT), ("g2", KT), ("n1_0", KT), ("n1_1", KT), ("n2_0", KT), ("n2_1", KT), ("ssm_d", KT),
                  ("ada_b0", 48), ("ada_b1", 48), ("conv", 64), ("bs", 8), ("ibias", 1), ("fbias", 1),
                  ("c", KT), ("cc", KT)):
    COLS[_name] = (_at, _at + _n)
    _at += _n
NCOLS = _at


class Segment:

    def __init__(self, ap, start):
        self.ap, self.start, self.n = ap, start, ap.shape[0]
        self.whole = False


def run_units(eng, n, body):
    rounds = (n - 1) // BODY
    if rounds > 1:
        with eng.Fori(0, rounds, 1) as it:
            for j in range(BODY):
                body(it, j, False)
    elif rounds == 1:
        for j in range(BODY):
            body(0, j, False)
    rest = n - rounds * BODY
    for j in range(rest):
        body(rounds, j, j == rest - 1)


class Split:

    def __init__(self, nc, ctx, name, shape):
        self.hi = ctx.enter_context(nc.sbuf_tensor(f"{name}_hi", shape, F32R))
        self.lo = ctx.enter_context(nc.sbuf_tensor(f"{name}_lo", shape, F32R))

    def parts(self, *at):
        return self.hi[at], self.lo[at]


def minus_hi(eng, out, x, hi):
    return eng.tensor_tensor(out, x, hi.bitcast(F32), ALU.subtract)


def three_passes(pe, out, lhs, rhs, start, stop, **more):
    pe.matmul(out, lhs[0], rhs[0], start=start, stop=False, **more)
    pe.matmul(out, lhs[0], rhs[1], start=False, stop=False, **more)
    return pe.matmul(out, lhs[1], rhs[0], start=False, stop=stop, **more)


class Chain:

    def __init__(self, eng, sem):
        self.eng, self.sem, self.k = eng, sem, 0

    def __call__(self, ins):
        self.k = self.k + 1
        ins.then_inc(self.sem, 1)
        self.eng.wait_ge(self.sem, self.k)

    def wait(self):
        self.eng.wait_ge(self.sem, self.k)

    def mark(self, ins):
        self.k = self.k + 1
        ins.then_inc(self.sem, 1)

    def loop(self, n, per, body):
        base = self.k
        with self.eng.Fori(0, n, 1) as i:
            self.k = base + i * per
            self.count = 0
            before = self.k
            steps = [0]
            inner = _Inner(self, before, steps)
            body(i, inner)
            assert steps[0] == per, (steps[0], per)
        self.k = base + n * per


class _Inner:
    def __init__(self, chain, base, steps):
        self.chain, self.base, self.steps = chain, base, steps

    def mark(self, ins):
        self.steps[0] += 1
        ins.then_inc(self.chain.sem, 1)

    def wait(self):
        self.chain.eng.wait_ge(self.chain.sem, self.base + self.steps[0])

    def __call__(self, ins):
        self.mark(ins)
        self.wait()


class Core:

    def __init__(self, nc, ctx):
        self.nc, self.ctx = nc, ctx
        self.loaded = [ctx.enter_context(nc.semaphore(f"slot{i}_loaded")) for i in range(RING)]
        self.units_done = ctx.enter_context(nc.semaphore("units_done"))
        self.hi_done = ctx.enter_context(nc.semaphore("unit_hi_done"))
        self.split_done = ctx.enter_context(nc.semaphore("unit_split_done"))
        self.dma_done = ctx.enter_context(nc.semaphore("small_dma_done"))
        self.dma_count = 0
        self.pools = [[ctx.enter_context(nc.semaphore(f"stage{k}_{i}")) for i in range(12)] for k in range(2)]
        self.turn = 0
        self.segments = []
        self.beside = []

    def stage(self):
        return Stage(self)

    def feed(self, sp, k):
        seg = self.segments[k]
        beside, self.beside = self.beside, []
        for to, src in beside:
            self.dma_count += 16
            sp.dma_start(to, src).then_inc(self.dma_done, 16)

        def load(it, j, last):
            sp.wait_ge(self.split_done, 2 * (seg.start + it * BODY + j + 1))
            slot = (seg.start + j) % RING
            sp.dma_start(self.ring[:, slot, :], seg.ap[it * BODY + j + RING]).then_inc(self.loaded[slot], 16)

        run_units(sp, seg.n - RING, load)
        if k + 1 < len(self.segments):
            nxt = self.segments[k + 1]
            for v in range(RING):
                sp.wait_ge(self.split_done, 2 * (nxt.start + v - RING + 1))
                slot = (nxt.start + v) % RING
                sp.dma_start(self.ring[:, slot, :], nxt.ap[v]).then_inc(self.loaded[slot], 16)
        if beside:
            sp.wait_ge(self.dma_done, self.dma_count)

    def split_hi(self, act, g, it):
        act.wait_ge(self.loaded[g % RING], 16 * (g // RING + 1) + it * (16 * BODY // RING))
        act.wait_ge(self.units_done, g + 1 + it * BODY)
        for half in range(2):
            at = slice(half * HALF, (half + 1) * HALF)
            act.activation(self.unit.hi[:, g % 2, at], self.ring[:, g % RING, at], ACT.Copy).then_inc(self.hi_done, 1)

    def split_lo(self, dve, g, it):
        for half in range(2):
            at = slice(half * HALF, (half + 1) * HALF)
            dve.wait_ge(self.hi_done, 2 * (g + it * BODY) + half + 1)
            minus_hi(dve, self.unit.lo[:, g % 2, at], self.ring[:, g % RING, at],
                     self.unit.hi[:, g % 2, at]).then_inc(self.split_done, 1)

    def split_next(self, eng, seg, it, j, last):
        if last and (seg is self.segments[-1] or self.segments[self.segments.index(seg) + 1].whole):
            return
        if eng is self.nc.scalar:
            self.split_hi(eng, seg.start + j + 1, it)
        else:
            self.split_lo(eng, seg.start + j + 1, it)

    def wait_split(self, pe, seg, it, j, half=0):
        pe.wait_ge(self.split_done, 2 * (seg.start + j + it * BODY) + half + 1)
        return (seg.start + j) % 2

    def wait_done(self, eng, seg, it, j):
        eng.wait_ge(self.units_done, seg.start + j + 3 + it * BODY)

    def columns(self, name):
        a, b = COLS[name]
        return self.cols[:, a:b]


class Stage:

    def __init__(self, core):
        self.core = core

    def __enter__(self):
        core = self.core
        self.pool = list(core.pools[core.turn % 2])
        other = core.pools[1 - core.turn % 2]
        first = core.turn == 0
        core.turn += 1
        self.block = core.nc.Block()
        self.block.__enter__()
        if not first:
            @self.block.gpsimd
            def _(pool):
                pool.sem_clear(range(other[0].num, other[-1].num + 1))
        return self

    def sem(self):
        return self.pool.pop(0)

    def __exit__(self, *a):
        return self.block.__exit__(*a)



def product_by_feature(core, k, rhs, ntok, evacuate):
    seg = core.segments[k]
    with core.stage() as st:
        bank_free = [st.sem(), st.sem()]

        @st.block.sync
        def _(sp):
            core.feed(sp, k)

        @st.block.tensor
        def _(pe):
            def unit(it, j, last):
                b = core.wait_split(pe, seg, it, j)
                pe.wait_ge(bank_free[j % 2], it * (BODY // 2) + j // 2 + 1)
                for kt in range(KT):
                    if kt == KT // 2:
                        core.wait_split(pe, seg, it, j, 1)
                    ins = three_passes(pe, core.ps[:, j % 2, 0:ntok], core.unit.parts(slice(None), b, slice(kt * P, (kt + 1) * P)),
                                       rhs(kt), kt == 0, kt == KT - 1)
                ins.then_inc(core.units_done, 1)

            run_units(pe, seg.n, unit)

        def taker(eng, parity):
            eng.sem_inc(bank_free[parity], 1)

            def unit(it, j, last):
                core.split_next(eng, seg, it, j, last)
                if j % 2 == parity:
                    core.wait_done(eng, seg, it, j)
                    evacuate(eng, core.ps[:, j % 2, 0:ntok], it * BODY + j, j % 2).then_inc(bank_free[j % 2], 1)

            run_units(eng, seg.n, unit)

        @st.block.scalar
        def _(act):
            taker(act, 0)

        @st.block.vector
        def _(dve):
            taker(dve, 1)


def product_by_token(core, k, lhs, tiles, nk, evacuate, takers=("scalar", "vector")):
    seg = core.segments[k]
    chunks = seg.n // nk
    sets = 2 if tiles == NX else 1
    with core.stage() as st:
        set_free = [st.sem(), st.sem()]

        @st.block.sync
        def _(sp):
            core.feed(sp, k)

        @st.block.tensor
        def _(pe):
            for c in range(chunks):
                s = c % sets
                if c >= sets:
                    pe.wait_ge(set_free[s], c // sets)
                for kt in range(nk):
                    b = core.wait_split(pe, seg, 0, c * nk + kt)
                    for h in range(2):
                        if h:
                            core.wait_split(pe, seg, 0, c * nk + kt, 1)
                        for t in range(tiles):
                            last = three_passes(pe, core.ps[:, s * 4 + 2 * t + h, :], lhs(c, kt, t),
                                                core.unit.parts(slice(None), b, slice(h * HALF, (h + 1) * HALF)),
                                                kt == 0, kt == nk - 1)
                    last.then_inc(core.units_done, 1)

        def taker(eng, which):
            for c in range(chunks):
                for kt in range(nk):
                    core.split_next(eng, seg, 0, c * nk + kt, (c, kt) == (chunks - 1, nk - 1))
                if takers[c % 2] != which:
                    continue
                core.wait_done(eng, seg, 0, (c + 1) * nk - 1)
                for t in range(tiles):
                    for h in range(2):
                        last = evacuate(eng, c, t, h, core.ps[:, (c % sets) * 4 + 2 * t + h, :])
                last.then_inc(set_free[c % sets], 1)

        @st.block.scalar
        def _(act):
            taker(act, "scalar")

        @st.block.vector
        def _(dve):
            taker(dve, "vector")



def inverse_norms(core, pieces, stat):
    width, n = pieces[0].shape[1], len(pieces)
    with ExitStack() as ctx:
        squares = ctx.enter_context(core.nc.sbuf_tensor(f"squares{core.turn}", [P, 2, width], F32))
        with core.stage() as st:
            squared, steps, inverted = (st.sem() for _ in range(3))

            @st.block.scalar
            def _(act):
                for i, piece in enumerate(pieces):
                    if i >= 2:
                        act.wait_ge(squared, i - 1)
                    act.activation(squares[:, i % 2, :], piece, ACT.Square,
                                   accum_out=stat[:, i:i + 1]).then_inc(squared, 1)
                act.wait_ge(inverted, 1)
                act.activation(stat[:, 0:n], stat[:, 0:n], ACT.Sqrt)

            @st.block.vector
            def _(dve):
                step = Chain(dve, steps)
                dve.wait_ge(squared, n)
                step(dve.tensor_scalar(stat[:, 0:n], stat[:, 0:n], 1.0 / width, EPS, ALU.mult, ALU.add))
                dve.reciprocal(stat[:, 0:n], stat[:, 0:n]).then_inc(inverted, 1)


def norm_transpose(core, tiles, gain, shift, dst):
    nc = core.nc
    n = len(tiles)
    with ExitStack() as ctx:
        stat = ctx.enter_context(nc.sbuf_tensor(f"norm_stat{core.turn}", [P, 4], F32))
        inverse_norms(core, [core.X[:, a, :] for a, _, _ in tiles], stat)
        normed = ctx.enter_context(nc.sbuf_tensor(f"normed{core.turn}", [P, 2, D], F32))
        whole = ctx.enter_context(nc.sbuf_tensor(f"normed_turned{core.turn}", [P, 2, KT, P], F32))
        with core.stage() as st:
            scaled, turned, taken, hi_ready, lo_ready = (st.sem() for _ in range(5))

            @st.block.scalar
            def _(act):
                def hi(i):
                    act.wait_ge(taken, i + 1)
                    b = tiles[i][1]
                    act.activation(dst.hi[:, :, b * P:(b + 1) * P], whole[:, i % 2, :, :], ACT.Copy).then_inc(hi_ready, 1)

                for i, (a, _, _) in enumerate(tiles):
                    if i >= 2:
                        act.wait_ge(turned, i - 1)
                    act.activation(normed[:, i % 2, :], core.X[:, a, :], ACT.Copy, scale=stat[:, i:i + 1]).then_inc(scaled, 1)
                    if i >= 1:
                        hi(i - 1)
                hi(n - 1)

            @st.block.tensor
            def _(pe):
                for i in range(n):
                    pe.wait_ge(scaled, i + 1)
                    if i >= 2:
                        pe.wait_ge(taken, i - 1)
                    for kt in range(KT):
                        last = pe.transpose(core.ps[:, 2 * (i % 2) + kt // 4, (kt % 4) * P:(kt % 4 + 1) * P],
                                            normed[:, i % 2, kt * P:(kt + 1) * P], core.ident)
                    last.then_inc(turned, 1)

            @st.block.vector
            def _(dve):
                def lo(i):
                    dve.wait_ge(hi_ready, i + 1)
                    b = tiles[i][1]
                    minus_hi(dve, dst.lo[:, :, b * P:(b + 1) * P], whole[:, i % 2, :, :],
                             dst.hi[:, :, b * P:(b + 1) * P]).then_inc(lo_ready, 1)

                for i, (_, _, m) in enumerate(tiles):
                    dve.wait_ge(turned, i + 1)
                    if i >= 2:
                        dve.wait_ge(lo_ready, i - 1)
                    for kt in range(KT):
                        src = core.ps[:, 2 * (i % 2) + kt // 4, (kt % 4) * P:(kt % 4 + 1) * P]
                        to = whole[:, i % 2, kt, :]
                        if shift is None:
                            last = dve.tensor_scalar(to, src, gain(m, kt), None, ALU.mult)
                        else:
                            last = dve.tensor_scalar(to, src, gain(m, kt), shift(m, kt), ALU.mult, ALU.add)
                    last.then_inc(taken, 1)
                    if i >= 1:
                        lo(i - 1)
                lo(n - 1)


def transpose_tokens(core, pieces, dst):
    with core.stage() as st:
        turned, hi_ready, taken = st.sem(), st.sem(), st.sem()

        def halves(i):
            for h in range(2):
                yield (core.ps[:, 2 * (i % 2) + h, :].rearrange("p (k t) -> p k t", k=4),
                       dst.hi[:, 4 * h:4 * h + 4, i * P:(i + 1) * P], dst.lo[:, 4 * h:4 * h + 4, i * P:(i + 1) * P])

        @st.block.tensor
        def _(pe):
            for i, piece in enumerate(pieces):
                if i >= 2:
                    pe.wait_ge(taken, i - 1)
                for kt in range(KT):
                    last = pe.transpose(core.ps[:, 2 * (i % 2) + kt // 4, (kt % 4) * P:(kt % 4 + 1) * P],
                                        piece[:, kt * P:(kt + 1) * P], core.ident)
                last.then_inc(turned, 1)

        @st.block.scalar
        def _(act):
            for i in range(len(pieces)):
                act.wait_ge(turned, i + 1)
                for src, hi, lo in halves(i):
                    act.activation(hi, src, ACT.Copy).then_inc(hi_ready, 1)

        @st.block.vector
        def _(dve):
            for i in range(len(pieces)):
                for h, (src, hi, lo) in enumerate(halves(i)):
                    dve.wait_ge(hi_ready, 2 * i + h + 1)
                    last = minus_hi(dve, lo, src, hi)
                last.then_inc(taken, 1)


def split_tensor(core, src, dst, chunks):
    n = src.shape[1] // chunks
    with core.stage() as st:
        hi_ready = st.sem()

        @st.block.scalar
        def _(act):
            for i in range(chunks):
                a = slice(i * n, (i + 1) * n)
                act.activation(dst.hi[:, a, :], src[:, a, :], ACT.Copy).then_inc(hi_ready, 1)

        @st.block.vector
        def _(dve):
            for i in range(chunks):
                a = slice(i * n, (i + 1) * n)
                dve.wait_ge(hi_ready, i + 1)
                minus_hi(dve, dst.lo[:, a, :], src[:, a, :], dst.hi[:, a, :])


def add_normed(core, src, gain_row, n):
    nc = core.nc
    with ExitStack() as ctx:
        stat = ctx.enter_context(nc.sbuf_tensor(f"add_stat{core.turn}", [P, n], F32))
        scaled = ctx.enter_context(nc.sbuf_tensor(f"add_scaled{core.turn}", [P, n, D], F32))
        inverse_norms(core, [src[:, t, :] for t in range(n)], stat)
        with core.stage() as st:
            steps = st.sem()

            @st.block.vector
            def _(dve):
                step = Chain(dve, steps)
                for t in range(n):
                    step.mark(dve.scalar_tensor_tensor(out=scaled[:, t, :], in0=src[:, t, :], scalar=stat[:, t:t + 1],
                                                       in1=gain_row, op0=ALU.mult, op1=ALU.mult))
                step.wait()
                for t in range(n):
                    dve.tensor_tensor(core.X[:, t, :], core.X[:, t, :], scaled[:, t, :], ALU.add)


def small_loads(core, pairs):
    with core.stage() as st:
        @st.block.scalar
        def _(act):
            for dst, src in pairs:
                core.dma_count += 16
                act.dma_start(dst, src).then_inc(core.dma_done, 16)
            act.wait_ge(core.dma_done, core.dma_count)


class ModulationPart:

    def __init__(self, core, stage, k, first, rows):
        self.core, self.k, self.first, self.rows = core, k, first, rows
        self.seg = core.segments[k]
        self.chunks = self.seg.n // KT
        self.taken, self.turned = stage.sem(), stage.sem()

        @stage.block.sync
        def _(sp):
            core.feed(sp, k)

        @stage.block.tensor
        def _(pe):
            self.multiply(pe)

        @stage.block.gpsimd
        def _(pool):
            for u in range(self.seg.n):
                core.wait_done(pool, self.seg, 0, u)
                pool.sem_inc(core.hi_done, 2)
                pool.sem_inc(core.split_done, 2)
            if not core.segments[k + 1].whole:
                core.split_lo(pool, self.seg.start + self.seg.n, 0)

    def multiply(self, pe):
        core = self.core

        def turn(c):
            pe.wait_ge(self.taken, c + 1)
            for f in range(KT):
                at = 2 * (c * KT + f)
                last = pe.transpose(core.ps[:, 4, at:at + 2], self.rows[:, c % 2, f * P:(f + 1) * P],
                                    core.ident[0:2, 0:2])
            last.then_inc(self.turned, 1)

        for c in range(self.chunks):
            if c >= 2:
                pe.wait_ge(self.taken, c - 1)
            for kt in range(KT):
                u = self.seg.start + c * KT + kt
                pe.wait_ge(core.loaded[u % RING], 16 * (u // RING + 1))
                for h in range(2):
                    last = pe.matmul(core.ps[0:2, 2 * (c % 2) + h, :], core.silu_c[:, kt, :],
                                     core.ring[:, u % RING, h * HALF:(h + 1) * HALF],
                                     start=(kt == 0), stop=(kt == KT - 1))
                last.then_inc(core.units_done, 1)
            if c:
                turn(c - 1)
        turn(self.chunks - 1)

    def take(self, act, c):
        self.core.wait_done(act, self.seg, 0, c * KT + KT - 1)
        if c >= 2:
            act.wait_ge(self.turned, c - 1)
        act.activation(self.rows[:, c % 2, :].rearrange("p (h n) -> p h n", h=2),
                       self.core.ps[0:2, 2 * (c % 2):2 * (c % 2) + 2, :], ACT.Copy).then_inc(self.taken, 1)

    def keep(self, act):
        n = self.chunks * KT
        act.wait_ge(self.turned, self.chunks)
        act.activation(self.core.MOD[:, self.first:self.first + n, :],
                       self.core.ps[:, 4, 0:2 * n].rearrange("p (f s) -> p f s", s=2), ACT.Copy)
        if not self.core.segments[self.k + 1].whole:
            self.core.split_hi(act, self.seg.start + self.seg.n, 0)



def gate_rows(core, wg, G):
    with core.stage() as st:
        gates_ready = st.sem()

        @st.block.tensor
        def _(pe):
            for which in range(2):
                for kt in range(KT):
                    for n, part in enumerate(core.xs.parts(slice(None), kt, slice(None))):
                        last = pe.matmul(core.ps[0:HEADS, which, 0:SEQ], wg[:, kt, which * HEADS:(which + 1) * HEADS],
                                         part.bitcast(F32), start=(kt == 0 and n == 0), stop=(kt == KT - 1 and n == 1))
                last.then_inc(gates_ready, 1)

        @st.block.vector
        def _(dve):
            for which, name in ((0, "ibias"), (1, "fbias")):
                dve.wait_ge(gates_ready, which + 1)
                dve.tensor_scalar(G[:, which, :], core.ps[0:HEADS, which, 0:SEQ], core.columns(name)[0:HEADS, :],
                                  None, ALU.add)


def gate_weights(core, G, W, mask):
    nc = core.nc
    with ExitStack() as ctx:
        def rows(name):
            return ctx.enter_context(nc.sbuf_tensor(name, [HEADS, SEQ], F32))

        e, lf, F, a, M, en, ones, zeros = (rows(f"gate_{x}") for x in ("e", "lf", "F", "a", "M", "en", "one", "zero"))
        a_col = ctx.enter_context(nc.sbuf_tensor("a_col", [P, NX, HEADS], F32))
        with core.stage() as st:
            absolute, logged, summed, floored, turned, steps, asteps = (st.sem() for _ in range(7))

            @st.block.vector
            def _(dve):
                step = Chain(dve, steps)
                step.mark(dve.memset(ones[:, :], 1.0))
                step.mark(dve.memset(zeros[:, :], 0.0))
                dve.scalar_tensor_tensor(out=e[:, :], in0=G[:, 1, :], scalar=-1.0, in1=G[:, 1, :], op0=ALU.mult,
                                         op1=ALU.max).then_inc(absolute, 1)
                dve.wait_ge(logged, 1)
                step(dve.scalar_tensor_tensor(out=lf[:, :], in0=G[:, 1, :], scalar=0.0, in1=e[:, :],
                                              op0=ALU.min, op1=ALU.subtract))
                step(dve.tensor_tensor_scan(F[:, :], ones[:, :], lf[:, :], 0.0, ALU.mult, ALU.add))
                step(dve.tensor_tensor(a[:, :], G[:, 0, :], F[:, :], ALU.subtract))
                step(dve.tensor_tensor_scan(M[:, :], zeros[:, :], a[:, :], 0.0, ALU.add, ALU.max))
                dve.tensor_tensor(en[:, :], F[:, :], M[:, :], ALU.add).then_inc(summed, 1)
                dve.wait_ge(turned, 1)
                last = dve.tensor_copy(a_col[:, :, :], core.ps[:, 0, 0:NX * HEADS].rearrange("p (t h) -> p t h", t=NX))
                last = dve.tensor_copy(core.floor[:, :, :], core.ps[:, 1, 0:NX * HEADS].rearrange("p (t h) -> p t h", t=NX))

            @st.block.scalar
            def _(act):
                step = Chain(act, asteps)
                act.wait_ge(absolute, 1)
                step(act.activation(e[:, :], e[:, :], ACT.Exp, scale=-1.0))
                act.activation(e[:, :], e[:, :], ACT.Ln, bias=1.0).then_inc(logged, 1)
                act.wait_ge(summed, 1)
                act.activation(en[:, :], en[:, :], ACT.Exp, scale=-1.0).then_inc(floored, 1)

            @st.block.tensor
            def _(pe):
                pe.wait_ge(floored, 1)
                for which, row in ((0, a), (1, en)):
                    for t in range(NX):
                        last = pe.transpose(core.ps[:, which, t * HEADS:(t + 1) * HEADS], row[:, t * P:(t + 1) * P],
                                            core.ident[0:HEADS, 0:HEADS])
                last.then_inc(turned, 1)

        with core.stage() as st:
            spread, bounded, raised, steps = (st.sem() for _ in range(4))

            @st.block.tensor
            def _(pe):
                for h in range(HEADS):
                    pe.matmul(core.ps[:, 2 + h, 0:SEQ], core.sel[0:HEADS, h, :], M[:, :],
                              start=True, stop=True).then_inc(spread, 1)

            @st.block.vector
            def _(dve):
                for h in range(HEADS):
                    dve.wait_ge(spread, h + 1)
                    dve.tensor_scalar(W[:, h, 0:SEQ], core.ps[:, 2 + h, 0:SEQ], a_col[:, 0, h:h + 1], 0.0,
                                      ALU.subtract, ALU.max)
                    dve.tensor_scalar(W[:, h, SEQ:DCOLS], core.ps[:, 2 + h, P:SEQ], a_col[:, 1, h:h + 1], 0.0,
                                      ALU.subtract, ALU.max).then_inc(bounded, 1)
                for h in range(HEADS):
                    dve.wait_ge(raised, h + 1)
                    dve.tensor_tensor(W[:, h, :], W[:, h, :], mask, ALU.mult)

            @st.block.scalar
            def _(act):
                for h in range(HEADS):
                    act.wait_ge(bounded, h + 1)
                    act.activation(W[:, h, :], W[:, h, :], ACT.Exp, scale=-1.0).then_inc(raised, 1)


def causal_conv(core, FM, first, CV, rows):
    a0 = COLS["conv"][0]
    n = 2 * KT
    with core.stage() as st:
        convolved, steps = st.sem(), st.sem()
        mod = ModulationPart(core, st, 2, 0, rows)

        @st.block.vector
        def _(dve):
            step = Chain(dve, steps)

            def tap(i, j):
                return core.cols[:, a0 + j * n + i:a0 + j * n + i + 1]

            for i in range(n):
                step.mark(dve.tensor_scalar(CV[:, i, :], FM[:, first + i, :], tap(i, 3), None, ALU.mult))
            for lag in (1, 2, 3):
                step.wait()
                for i in range(n):
                    step.mark(dve.scalar_tensor_tensor(out=CV[:, i, lag:SEQ], in0=FM[:, first + i, 0:SEQ - lag],
                                                       scalar=tap(i, 3 - lag), in1=CV[:, i, lag:SEQ],
                                                       op0=ALU.mult, op1=ALU.add))
            step.wait()
            dve.engine_nop().then_inc(convolved, 1)

        @st.block.scalar
        def _(act):
            for c in range(mod.chunks):
                mod.take(act, c)
            mod.keep(act)
            act.wait_ge(convolved, 1)
            act.activation(FM[:, first:first + n, :], CV[:, :, :], ACT.Silu)


def linear_attention(core, FM, q0, k0, vals, W, ST, HB, h0, normalise, ones_col):
    nc = core.nc
    with core.stage() as st:
        scored, weighted, steps = st.sem(), st.sem(), st.sem()

        @st.block.tensor
        def _(pe):
            for h in range(HEADS):
                for s, (ta, ca, cb) in enumerate(((0, 0, SEQ), (P, SEQ, DCOLS))):
                    for d in range(2):
                        last = pe.matmul(core.ps[:, h, ca:cb], FM[:, k0 + 2 * h + d, s * P:(s + 1) * P],
                                         FM[:, q0 + 2 * h + d, ta:SEQ], start=(d == 0), stop=(d == 1))
                last.then_inc(scored, 1)

        @st.block.vector
        def _(dve):
            for h in range(HEADS):
                dve.wait_ge(scored, h + 1)
                dve.tensor_tensor(ST[:, h, :], core.ps[:, h, 0:DCOLS], W[:, h, :], ALU.mult)

    with ExitStack() as ctx:
        den = ctx.enter_context(nc.sbuf_tensor(f"den{h0}", [P, NX, HEADS], F32))
        with core.stage() as st:
            summed, ready, steps = st.sem(), st.sem(), st.sem()

            @st.block.tensor
            def _(pe):
                for h in range(HEADS):
                    for t, tiles in ((0, ((0, 0),)), (1, ((0, P), (1, SEQ)))):
                        for n, (s, c) in enumerate(tiles):
                            w = ST[:, h, c:c + P]
                            edge = dict(start=(n == 0), stop=(n == len(tiles) - 1))
                            last = pe.matmul(core.ps[:, 2 * h + t, 0:HD], w, vals(s, h), skip_group_check=True, **edge)
                        if normalise:
                            for n, (s, c) in enumerate(tiles):
                                w = ST[:, h, c:c + P]
                                last = pe.matmul(core.ps[:, 2 * h + t, HD:HD + 1], w, ones_col,
                                                 start=(n == 0), stop=(n == len(tiles) - 1), skip_group_check=True)
                last.then_inc(summed, 1)

            @st.block.vector
            def _(dve):
                step = Chain(dve, steps)
                dve.wait_ge(summed, 1)
                banks = core.ps[:, :, :].rearrange("p (h t) c -> p h t c", t=NX)
                if normalise:
                    step(dve.tensor_copy(den[:, :, :], banks[:, :, :, HD].rearrange("p h t -> p t h")))
                    step(dve.scalar_tensor_tensor(out=den[:, :, :], in0=den[:, :, :], scalar=-1.0, in1=den[:, :, :],
                                                  op0=ALU.mult, op1=ALU.max))
                    step(dve.tensor_tensor(den[:, :, :], den[:, :, :], core.floor[:, :, :], ALU.max))
                    step(dve.reciprocal(den[:, :, :], den[:, :, :]))
                for h in range(HEADS):
                    for t in range(NX):
                        if normalise:
                            dve.tensor_scalar(HB[:, t, h0 + h, :], banks[:, h, t, 0:HD], den[:, t, h:h + 1], None, ALU.mult)
                        else:
                            dve.tensor_copy(HB[:, t, h0 + h, :], banks[:, h, t, 0:HD])


def gated_head_norm(core, HB, gates):
    with ExitStack() as ctx:
        stat = ctx.enter_context(core.nc.sbuf_tensor("head_stat", [P, 2 * DH], F32))
        inverse_norms(core, [HB[:, t, h, :] for t in range(NX) for h in range(2 * HEADS)], stat)
        with core.stage() as st:
            @st.block.vector
            def _(dve):
                for t in range(NX):
                    for h in range(2 * HEADS):
                        i = t * 8 + h
                        dve.scalar_tensor_tensor(out=HB[:, t, h, :], in0=HB[:, t, h, :], scalar=stat[:, i:i + 1],
                                                 in1=gates(t, h), op0=ALU.mult, op1=ALU.mult)


def diff_attention(core, FM, vals, S, alibi, AT, HDO, lam_rows, subln):
    nc = core.nc
    with core.stage() as st:
        scored, taken = st.sem(), st.sem()

        @st.block.tensor
        def _(pe):
            for n in range(2 * DH):
                h, c = n // 2, n % 2
                if n >= BANKS:
                    pe.wait_ge(taken, n - BANKS + 1)
                rows = slice(64 * c, 64 * c + 64)
                for t, (ca, cb, kb) in enumerate(((0, P, P), (P, DCOLS, SEQ))):
                    last = pe.matmul(core.ps[:, n % BANKS, ca:cb], FM[rows, h, t * P:(t + 1) * P],
                                     FM[rows, KT + h, 0:kb], start=True, stop=True)
                last.then_inc(scored, 1)

        @st.block.vector
        def _(dve):
            for n in range(2 * DH):
                h, c = n // 2, n % 2
                dve.wait_ge(scored, n + 1)
                dve.scalar_tensor_tensor(out=S[:, h, c, :], in0=core.ps[:, n % BANKS, 0:DCOLS], scalar=0.125,
                                         in1=alibi[:, h, :], op0=ALU.mult, op1=ALU.add).then_inc(taken, 1)

    with ExitStack() as ctx:
        stat = ctx.enter_context(nc.sbuf_tensor("softmax_stat", [P, 2, 2 * DH], F32))
        lam = ctx.enter_context(nc.sbuf_tensor("lam", [P, 4], F32))
        parts = ((0, 0, P), (1, P, DCOLS))
        flat = S.rearrange("p h c k -> p (h c) k")
        with core.stage() as st:
            shifted, raised, lam_dots, lam_raised, steps = (st.sem() for _ in range(5))
            spare = FM[0:2, KT:2 * KT, :].rearrange("p (s a) b -> p s (a b)", s=2)
            mod = ModulationPart(core, st, 3, 2 * KT, spare)

            @st.block.vector
            def _(dve):
                step = Chain(dve, steps)
                step.mark(dve.tensor_tensor(lam_rows[:, 0:64], lam_rows[:, 0:64], lam_rows[:, 64:128], ALU.mult))
                step(dve.tensor_tensor(lam_rows[:, 128:192], lam_rows[:, 128:192], lam_rows[:, 192:256], ALU.mult))
                dve.tensor_reduce(lam[:, 0:1], lam_rows[:, 0:64], AX_X, ALU.add)
                dve.tensor_reduce(lam[:, 1:2], lam_rows[:, 128:192], AX_X, ALU.add).then_inc(lam_dots, 1)
                for q, a, b in parts:
                    step.mark(dve.tensor_reduce(stat[:, q, :], flat[:, :, a:b], AX_X, ALU.max))
                step.wait()
                for q, a, b in parts:
                    last = dve.tensor_tensor(flat[:, :, a:b], flat[:, :, a:b],
                                             stat[:, q, :].unsqueeze(2).broadcast_to([P, 2 * DH, b - a]), ALU.subtract)
                last.then_inc(shifted, 1)
                dve.wait_ge(lam_raised, 1)
                step(dve.tensor_tensor(lam[:, 2:3], lam[:, 0:1], lam[:, 1:2], ALU.subtract))
                step(dve.tensor_scalar(lam[:, 3:4], lam[:, 2:3], LAM_INIT, None, ALU.add))
                dve.wait_ge(raised, 1)
                for q, a, b in parts:
                    step.mark(dve.tensor_reduce(stat[:, q, :], flat[:, :, a:b], AX_X, ALU.add))
                step.wait()
                step(dve.reciprocal(stat[:, :, :], stat[:, :, :]))
                halves = stat[:, :, :].rearrange("p q (h c) -> p q h c", c=2)
                step(dve.tensor_scalar(halves[:, :, :, 1], halves[:, :, :, 1], lam[:, 3:4], None, ALU.mult))
                for q, a, b in parts:
                    for c in range(2):
                        step.mark(dve.tensor_tensor(S[:, :, c, a:b], S[:, :, c, a:b],
                                                    halves[:, q, :, c].unsqueeze(2).broadcast_to([P, DH, b - a]),
                                                    ALU.mult))
                step.wait()
                dve.tensor_tensor(S[:, :, 0, :], S[:, :, 0, :], S[:, :, 1, :], ALU.subtract)

            @st.block.scalar
            def _(act):
                act.wait_ge(lam_dots, 1)
                act.activation(lam[:, 0:2], lam[:, 0:2], ACT.Exp).then_inc(lam_raised, 1)
                mod.take(act, 0)
                act.wait_ge(shifted, 1)
                act.activation(flat, flat, ACT.Exp).then_inc(raised, 1)
                for c in range(1, mod.chunks):
                    mod.take(act, c)
                mod.keep(act)

    with core.stage() as st:
        turned, taken = st.sem(), st.sem()

        @st.block.tensor
        def _(pe):
            for h in range(DH):
                if h >= 4:
                    pe.wait_ge(taken, h - 3)
                for i in range(3):
                    last = pe.transpose(core.ps[:, h % 4, i * P:(i + 1) * P], S[:, h, 0, i * P:(i + 1) * P], core.ident)
                last.then_inc(turned, 1)
            for h in range(DH):
                pe.wait_ge(taken, h + 1)
                pe.matmul(core.ps[:, 4 + h // 4, (h % 4) * P:(h % 4 + 1) * P], AT(h, 0, P), vals(0, h),
                          start=True, stop=True, skip_group_check=True)
                for n in range(2):
                    pe.matmul(core.ps[:, 6 + h // 4, (h % 4) * P:(h % 4 + 1) * P], AT(h, (n + 1) * P, (n + 2) * P),
                              vals(n, h), start=(n == 0), stop=(n == 1), skip_group_check=True)

        @st.block.scalar
        def _(act):
            for h in range(DH):
                act.wait_ge(turned, h + 1)
                act.activation(AT(h, 0, DCOLS), core.ps[:, h % 4, 0:DCOLS], ACT.Copy).then_inc(taken, 1)

    with ExitStack() as ctx:
        stat = ctx.enter_context(nc.sbuf_tensor("sub_stat", [P, 2 * DH], F32))
        heads = core.ps[:, 4:8, :].rearrange("p b (h e) -> p (b h) e", h=4)
        inverse_norms(core, [heads[:, i, :] for i in range(2 * DH)], stat)
        with core.stage() as st:
            steps = st.sem()

            @st.block.vector
            def _(dve):
                step = Chain(dve, steps)
                step(dve.tensor_scalar(stat[:, :], stat[:, :], 1.0 - LAM_INIT, None, ALU.mult))
                for i in range(2 * DH):
                    t, h = i // DH, i % DH
                    dve.scalar_tensor_tensor(out=HDO[:, t, h, :], in0=heads[:, i, :],
                                             scalar=stat[:, i:i + 1], in1=subln, op0=ALU.mult, op1=ALU.mult)


def first_block(core, A):
    nc = core.nc
    with ExitStack() as scope:
        def sb(name, shape, ctx=scope):
            return ctx.enter_context(nc.sbuf_tensor(name, shape, F32))

        xs = core.xs = Split(nc, scope, "xs", [P, KT, SEQ])
        norm_transpose(core, [(t, t, 0) for t in range(NX)], lambda m, kt: core.columns("g0")[:, kt:kt + 1], None, xs)

        def by_tile(c, kt, t):
            return xs.parts(slice(None), kt, slice(t * P, (t + 1) * P))

        branches = scope.enter_context(ExitStack())
        TM = sb("by_token", [P, NX, 8, D], branches)
        FM = sb("by_feature", [P, 48, SEQ], branches)
        G = sb("gate_rows", [HEADS, 2, SEQ], branches)
        core.floor = sb("den_floor", [P, NX, HEADS], branches)

        def to_features(eng, ps, f, slot):
            if eng is core.nc.scalar:
                return eng.activation(FM[:, f, :], ps, ACT.Copy)
            return eng.tensor_copy(FM[:, f, :], ps)

        product_by_feature(core, 0, lambda kt: xs.parts(slice(None), kt, slice(None)), SEQ, to_features)

        spare = core.X[:, NX:NT, :].rearrange("p t d -> p (t d)")
        R = spare[:, 0:HEADS * DCOLS].rearrange("p (h c) -> p h c", h=HEADS)
        mask = spare[:, HEADS * DCOLS:(HEADS + 1) * DCOLS]
        wg = sb("gate_weights", [P, KT, 2 * HEADS], branches)
        core.beside = [(wg[:, :, :], A["w_gate"]), (R, A["k_retention"]), (mask, A["k_mask"])]

        def to_tokens(eng, c, t, h, ps):
            f = ACT.Copy if c < 3 else ACT.Sigmoid if c < 7 else ACT.Silu
            return eng.activation(TM[:, t, c, h * HALF:(h + 1) * HALF], ps, f)

        product_by_token(core, 1, by_tile, NX, KT, to_tokens,
                         ("scalar", "scalar"))
        gate_rows(core, wg, G)

        with ExitStack() as ctx:
            CV = sb("conv", [P, 2 * KT, SEQ], ctx)
            rows = sb("mod_rows", [2, 2, D], ctx)
            causal_conv(core, FM, 2 * KT, CV, rows)
        HB = FM[:, 16:32, :].rearrange("p (t h) e -> p t h e", t=NX)
        with ExitStack() as ctx:
            W = sb("mlstm_weights", [P, HEADS, DCOLS], ctx)
            ones_col = sb("ones_col", [P, 1], ctx)
            core.sel = sb("sel", [HEADS, HEADS, P], ctx)
            small_loads(core, [(core.sel[:, :, :], A["k_sel"])])
            with core.stage() as st:
                @st.block.vector
                def _(dve):
                    dve.memset(ones_col[:, :], 1.0)
            gate_weights(core, G, W, mask)
            ST = sb("weighted_scores", [P, HEADS, DCOLS], ctx)
            linear_attention(core, FM, 2 * KT, 3 * KT, lambda s, h: TM[:, s, 0, h * HD:(h + 1) * HD], W, ST, HB, 0,
                             True, ones_col[:, 0:1])
            linear_attention(core, FM, 4 * KT, 5 * KT, lambda s, h: TM[:, s, 1, h * HD:(h + 1) * HD], R, ST, HB, HEADS,
                             False, None)
        gated_head_norm(core, HB, lambda t, h: TM[:, t, 3 if h < HEADS else 7, (h % HEADS) * HD:(h % HEADS + 1) * HD])

        with ExitStack() as ctx:
            alibi = FM[:, 32:44, :].rearrange("p a b -> p (a b)").rearrange("p (h c) -> p h c", h=DH)
            lam_rows = sb("lam_rows", [P, 256], ctx)
            subln = sb("subln", [P, P], ctx)
            spare = TM[:, :, 0:2, :].rearrange("p t a b -> p t (a b)")

            def AT(h, a, b):
                return spare[:, h // 4, (h % 4) * DCOLS + a:(h % 4) * DCOLS + b]

            small_loads(core, [(alibi, A["k_alibi"]),
                               (lam_rows[:, :], A["diff_lambda"].broadcast_to([P, 256])),
                               (subln[:, :], A["diff_subln"].broadcast_to([P, P]))])
            S = sb("attention", [P, DH, 2, DCOLS], ctx)[:, :, :, :]
            HDO = FM[:, 0:8, :].rearrange("p (t a) (b e) -> p t (a b) e", t=NX, b=2)
            diff_attention(core, FM, lambda s, h: TM[:, s, 2, h * P:(h + 1) * P], S, alibi, AT, HDO, lam_rows,
                           subln[:, :])

        heads = FM[:, 16:32, :].rearrange("p (t r h) e -> p t r (h e)", t=NX, r=2)
        diffs = FM[:, 0:8, :].rearrange("p (t a) b -> p t (a b)", t=NX)
        Y = FM[:, 8:16, :].rearrange("p (t a) b -> p t (a b)", t=NX)
        for c, piece in enumerate((lambda t: heads[:, t, 0], lambda t: diffs[:, t], lambda t: heads[:, t, 1])):
            transpose_tokens(core, [piece(t) for t in range(NX)], xs)

            def mix(eng, _, t, h, ps, c=c):
                cols = slice(h * HALF, (h + 1) * HALF)
                gate = TM[:, t, 4 + c, cols]
                return eng.tensor_tensor(Y[:, t, cols] if c == 0 else gate, ps, gate, ALU.mult)

            product_by_token(core, 4 + c, by_tile, NX, KT, mix, ("vector", "vector"))
        with core.stage() as st:
            steps = st.sem()

            @st.block.vector
            def _(dve):
                step = Chain(dve, steps)
                step(dve.tensor_tensor(Y, Y, TM[:, :, 5, :], ALU.add))
                step(dve.tensor_tensor(Y, Y, TM[:, :, 6, :], ALU.add))
        transpose_tokens(core, [Y[:, t] for t in range(NX)], xs)
        branches.close()

        Y2 = sb("mixed", [P, NX, D])
        rows = sb("gain_rows", [P, 2, D])
        core.beside = [(rows[:, i, :], A["gain_rows"][i:i + 1, :].broadcast_to([P, D])) for i in range(2)]

        def keep(eng, c, t, h, ps):
            return eng.activation(Y2[:, t, h * HALF:(h + 1) * HALF], ps, ACT.Copy)

        product_by_token(core, 7, by_tile, NX, KT, keep, ("scalar", "scalar"))
        add_normed(core, Y2, rows[:, 0, :], NX)

        norm_transpose(core, [(t, t, 0) for t in range(NX)], lambda m, kt: core.columns("g2")[:, kt:kt + 1], None, xs)
        fT = Split(nc, scope, "ffn_hidden", [P, FT, SEQ])
        with ExitStack() as ctx:
            hidden = sb("ffn_product", [P, FT, SEQ], ctx)
            silu = sb("ffn_silu", [P, 2, SEQ], ctx)
            seg = core.segments[8]
            with core.stage() as st:
                bank_free = [st.sem(), st.sem()]

                @st.block.sync
                def _(sp):
                    core.feed(sp, 8)

                @st.block.tensor
                def _(pe):
                    def unit(it, j, last):
                        b = core.wait_split(pe, seg, it, j)
                        pe.wait_ge(bank_free[j % 2], it * (BODY // 2) + j // 2 + 1)
                        for kt in range(KT):
                            if kt == KT // 2:
                                core.wait_split(pe, seg, it, j, 1)
                            ins = three_passes(pe, core.ps[:, j % 2, 0:SEQ],
                                               core.unit.parts(slice(None), b, slice(kt * P, (kt + 1) * P)),
                                               xs.parts(slice(None), kt, slice(None)), kt == 0, kt == KT - 1)
                        ins.then_inc(core.units_done, 1)

                    run_units(pe, seg.n, unit)

                @st.block.scalar
                def _(act):
                    act.sem_inc(bank_free[0], 1)
                    act.sem_inc(bank_free[1], 1)

                    def unit(it, j, last):
                        core.split_next(act, seg, it, j, last)
                        if j % 2:
                            return
                        core.wait_done(act, seg, it, j)
                        if j < 2:
                            act.wait_ge(bank_free[1], it * (BODY // 2) + j // 2 + 1)
                        else:
                            act.wait_ge(bank_free[1], it * (BODY // 2) + j // 2)
                        act.activation(silu[:, (j // 2) % 2, :], core.ps[:, 0, 0:SEQ], ACT.Silu).then_inc(bank_free[0], 1)

                    run_units(act, seg.n, unit)

                @st.block.vector
                def _(dve):
                    def unit(it, j, last):
                        core.split_next(dve, seg, it, j, last)
                        if j % 2 == 0:
                            return
                        dve.wait_ge(bank_free[0], it * (BODY // 2) + j // 2 + 2)
                        core.wait_done(dve, seg, it, j)
                        dve.tensor_tensor(hidden[:, it * (BODY // 2) + j // 2, :], core.ps[:, 1, 0:SEQ],
                                          silu[:, (j // 2) % 2, :], ALU.mult).then_inc(bank_free[1], 1)

                    run_units(dve, seg.n, unit)
            split_tensor(core, hidden[:, :, :], fT, 11)

        positions = sb("positions", [P, NX, D])
        core.beside = [(positions[:, :, :], A["k_positions"]),
                       (core.X[:, NX:NT, :], A["ctx"].rearrange("b (t p) d -> p (b t) d", p=P))]
        product_by_token(core, 9, lambda c, kt, t: fT.parts(slice(None), kt, slice(t * P, (t + 1) * P)), NX, FT, keep,
                         ("scalar", "scalar"))
        add_normed(core, Y2, rows[:, 1, :], NX)
        with core.stage() as st:
            @st.block.vector
            def _(dve):
                dve.tensor_tensor(core.X[:, 0:NX, :], core.X[:, 0:NX, :], positions[:, :, :], ALU.add)



def finish_modulation(core, bias):
    MOD = core.MOD
    with core.stage() as st:
        steps = st.sem()

        @st.block.vector
        def _(dve):
            step = Chain(dve, steps)
            step(dve.tensor_tensor(MOD[:, :, :], MOD[:, :, :],
                                   core.columns(bias).unsqueeze(2).broadcast_to([P, 48, 2]), ALU.add))
            for a, name in ((8, "n1"), (32, "n2")):
                step(dve.tensor_scalar(core.gains[:, a // 32, :, :], MOD[:, a:a + 8, :], 1.0, None, ALU.add))
                step(dve.tensor_tensor(core.gains[:, a // 32, :, :], core.gains[:, a // 32, :, :],
                                       core.columns(f"{name}_{bias[-1]}").unsqueeze(2).broadcast_to([P, 8, 2]),
                                       ALU.mult))
            dve.tensor_copy(core.gate2[:, :, :], MOD[:, 40:48, :])


def spread_rows(core, first, nsets, dst):
    with ExitStack() as ctx:
        wide = ctx.enter_context(core.nc.sbuf_tensor(f"wide{core.turn}", [P, nsets, KT, P], F32))
        with core.stage() as st:
            widened, spread = st.sem(), st.sem()

            @st.block.vector
            def _(dve):
                for s in range(nsets):
                    src = core.MOD[:, first:first + KT, s:s + 1].broadcast_to([P, KT, P])
                    dve.tensor_copy(wide[:, s, :, :], src).then_inc(widened, 1)

            @st.block.tensor
            def _(pe):
                for s in range(nsets):
                    pe.wait_ge(widened, s + 1)
                    for kt in range(KT):
                        last = pe.matmul(core.ps[:, 2 * s + kt // 4, (kt % 4) * P:(kt % 4 + 1) * P], wide[:, s, kt, :],
                                         core.ident, start=True, stop=True)
                    last.then_inc(spread, 1)

            @st.block.scalar
            def _(act):
                for s in range(nsets):
                    act.wait_ge(spread, s + 1)
                    for h in range(2):
                        act.activation(dst[:, s, h * HALF:(h + 1) * HALF], core.ps[:, 2 * s + h, :], ACT.Copy)


def add_gated(core, k, lhs, tiles, gate):
    with ExitStack() as ctx:
        out = ctx.enter_context(core.nc.sbuf_tensor(f"gated{k}", [P, tiles, D], F32))

        def take(eng, c, t, h, ps):
            cols = slice(h * HALF, (h + 1) * HALF)
            return eng.tensor_tensor(out[:, t, cols], ps, gate(t)[:, cols], ALU.mult)

        product_by_token(core, k, lhs, tiles, KT, take, ("vector", "vector"))
        with core.stage() as st:
            @st.block.vector
            def _(dve):
                dve.tensor_tensor(core.X[:, 0:tiles, :], core.X[:, 0:tiles, :], out[:, :, :], ALU.add)


def chunk_mixer(core, A, k_in, k_out):
    nc = core.nc
    with ExitStack() as ctx:
        def sb(name, shape):
            return ctx.enter_context(nc.sbuf_tensor(name, shape, F32))

        xs = Split(nc, ctx, "cm_xs", [P, KT, 2 * SEQ])

        def by_tile(c, kt, t):
            return xs.parts(slice(None), kt, slice(t * P, (t + 1) * P))

        gate_rows_ = sb("cm_gate_rows", [P, 2, D])
        spread_rows(core, 16, 2, gate_rows_)
        norm_transpose(core, [(t, t, t // NX) for t in range(NT)],
                       lambda m, kt: core.gains[:, 0, kt, m:m + 1], lambda m, kt: core.MOD[:, kt, m:m + 1], xs)
        Z = sb("cm_z", [P, NT, 2, D])
        rows = sb("cm_rows", [P, 2, D])
        ws = sb("cm_ws", [P, 8, P])
        core.beside = [(rows[:, i, :], A["gain_rows"][2 + i:3 + i, :].broadcast_to([P, D])) for i in range(2)] + [
            (ws[:, :, :], A["cm_ws"])]

        def gelu(eng, c, t, h, ps):
            return eng.activation(Z[:, t, c, h * HALF:(h + 1) * HALF], ps, ACT.Gelu_apprx_tanh)

        product_by_token(core, k_in, by_tile, NT, KT, gelu,
                         ("scalar", "scalar"))
        stat = sb("cm_stat", [P, NT])
        mean = sb("cm_mean", [P, NT])
        with core.stage() as st:
            steps = st.sem()

            @st.block.vector
            def _(dve):
                step = Chain(dve, steps)
                step(dve.tensor_reduce(mean[:, :], Z[:, :, 1, :], AX_X, ALU.add))
                step(dve.tensor_scalar(mean[:, :], mean[:, :], 1.0 / D, None, ALU.mult))
                for t in range(NT):
                    dve.tensor_scalar(Z[:, t, 1, :], Z[:, t, 1, :], mean[:, t:t + 1], None, ALU.subtract)
        inverse_norms(core, [Z[:, t, 1, :] for t in range(NT)], stat)
        with core.stage() as st:
            steps, mixed, normed = st.sem(), st.sem(), st.sem()

            @st.block.vector
            def _(dve):
                step = Chain(dve, steps)
                for t in range(NT):
                    step(dve.scalar_tensor_tensor(out=Z[:, t, 1, :], in0=Z[:, t, 1, :], scalar=stat[:, t:t + 1],
                                                  in1=rows[:, 0, :], op0=ALU.mult, op1=ALU.mult))
                    dve.tensor_tensor(Z[:, t, 1, :], Z[:, t, 1, :], rows[:, 1, :], ALU.add).then_inc(normed, 1)
                for t in range(NT):
                    dve.wait_ge(mixed, t + 1)
                    for h in range(8):
                        cols = slice(h * P, (h + 1) * P)
                        bank = core.ps[:, 2 * t + h // 4, (h % 4) * P:(h % 4 + 1) * P]
                        dve.scalar_tensor_tensor(out=Z[:, t, 0, cols], in0=bank, scalar=core.columns("bs")[:, h:h + 1],
                                                 in1=Z[:, t, 0, cols], op0=ALU.add, op1=ALU.mult)

            @st.block.tensor
            def _(pe):
                for t in range(NT):
                    pe.wait_ge(normed, t + 1)
                    for h in range(8):
                        last = pe.matmul(core.ps[:, 2 * t + h // 4, (h % 4) * P:(h % 4 + 1) * P], ws[:, h, :],
                                         Z[:, t, 1, h * P:(h + 1) * P], start=True, stop=True, skip_group_check=True)
                    last.then_inc(mixed, 1)

        transpose_tokens(core, [Z[:, t, 0, :] for t in range(NT)], xs)
        add_gated(core, k_out, by_tile, NT,
                  lambda t: gate_rows_[:, t // NX, :])


def choose_experts(core, k, xs, keysT, tiles, pair_keys, pair_weight):
    nc = core.nc
    seg = core.segments[k]
    UNITS = seg.n // PH
    tokens = tiles * P
    fetched = core.dma_count + 16
    square = [P, tiles, TOPK, TOPK]
    with ExitStack() as ctx:
        def sb(name, shape, dt=F32):
            return ctx.enter_context(nc.sbuf_tensor(f"{name}{core.turn}", shape, dt))

        qT = sb("queries", [P, 2, UNITS, tokens])
        scores = sb("key_scores", [P, 2, 2 * tiles, KEYS])
        rest = sb("key_rest", [P, 2 * tiles, KEYS])
        best = sb("key_best", [P, tiles, 2, TOPK])
        where = sb("key_where", [P, tiles, 2, TOPK], U32)
        where_f = sb("key_where_f", [P, 2, tiles, 2, TOPK], BF16)
        cand = sb("cand", [P, tiles, TOPK * TOPK])
        cand_rest = sb("cand_rest", [P, tiles, TOPK * TOPK])
        top = sb("cand_top", [P, tiles, TOPK])
        at = sb("cand_at", [P, tiles, TOPK], U32)
        digit = sb("cand_digit", [P, 2, tiles, TOPK], U32)
        digit_f = sb("cand_digit_f", [P, 2, tiles, TOPK], BF16)
        places = sb("places", [P, TOPK, TOPK], BF16)
        chosen = sb("chosen", [P, 2, 2, tiles, TOPK, TOPK], BF16)
        picked = sb("picked", [P, 2, tiles, TOPK, TOPK], BF16)
        sums = sb("softmax_sums", [P, tiles * PH])
        pairs = sb("pairs", [P, 3, tiles, PAIRS])
        with core.stage() as st:
            (kept, scored, copied, searched, compared, picks, reduced, shifted, raised, turned,
             steps) = (st.sem() for _ in range(11))

            @st.block.sync
            def _(sp):
                core.feed(sp, k)

            @st.block.tensor
            def _(pe):
                def score(h):
                    if h == 0:
                        pe.wait_ge(core.dma_done, fetched)
                    pe.wait_ge(kept, UNITS * (h + 1))
                    if h >= 2:
                        pe.wait_ge(copied, h - 1)
                    for i in range(2 * tiles):
                        t, half = i // 2, i % 2
                        to = core.ps[:, 2 + 2 * (h % 2) + i // 4, (i % 4) * KEYS:(i % 4 + 1) * KEYS]
                        for d in range(2):
                            last = pe.matmul(to, qT[:, h % 2, 2 * half + d, t * P:(t + 1) * P],
                                             keysT[:, UNITS * h + 2 * half + d, :], start=(d == 0), stop=(d == 1),
                                             skip_group_check=True)
                    last.then_inc(scored, 1)

                for u in range(seg.n):
                    b = core.wait_split(pe, seg, 0, u)
                    if u >= 2:
                        pe.wait_ge(kept, u - 1)
                    for kt in range(KT):
                        if kt == KT // 2:
                            core.wait_split(pe, seg, 0, u, 1)
                        last = three_passes(pe, core.ps[:, u % 2, 0:tokens],
                                            core.unit.parts(slice(None), b, slice(kt * P, (kt + 1) * P)),
                                            xs.parts(slice(None), kt, slice(None)), kt == 0, kt == KT - 1)
                    last.then_inc(core.units_done, 1)
                    if u >= UNITS and u % UNITS == 0:
                        score(u // UNITS - 1)
                score(PH - 1)
                pe.wait_ge(raised, 2)
                for t in range(tiles):
                    for i in range(3):
                        last = pe.transpose(core.ps[:, t, i * P:(i + 1) * P], pairs[:, i, t, :], core.ident)
                    last.then_inc(turned, 1)

            @st.block.scalar
            def _(act):
                def copy(h):
                    act.wait_ge(scored, h + 1)
                    if h >= 2:
                        act.wait_ge(searched, h - 1)
                    banks = core.ps[:, 2 + 2 * (h % 2):2 + 2 * (h % 2) + (2 * tiles + 3) // 4, :]
                    act.activation(scores[:, h % 2, :, :], banks.rearrange("p b (i m) -> p (b i) m", m=KEYS),
                                   ACT.Copy).then_inc(copied, 1)

                for u in range(seg.n):
                    core.split_next(act, seg, 0, u, u == seg.n - 1)
                    h = u // UNITS
                    core.wait_done(act, seg, 0, u)
                    if h >= 2:
                        act.wait_ge(scored, h - 1)
                    act.activation(qT[:, h % 2, u % UNITS, :], core.ps[:, u % 2, 0:tokens], ACT.Copy).then_inc(kept, 1)
                    if u >= UNITS and u % UNITS == 0:
                        copy(h - 1)
                copy(PH - 1)
                act.wait_ge(shifted, PH)
                act.activation(pairs[:, 2, :, :], pairs[:, 2, :, :], ACT.Exp).then_inc(raised, 1)
                for t in range(tiles):
                    act.wait_ge(turned, t + 1)
                    act.activation(pair_keys[:, :, t * P:(t + 1) * P],
                                   core.ps[:, t, 0:2 * P].rearrange("p (i n) -> p i n", i=2), ACT.Copy)
                    act.activation(pair_weight[:, t * P:(t + 1) * P], core.ps[:, t, 2 * P:3 * P], ACT.Copy)

            @st.block.vector
            def _(dve):
                step = Chain(dve, steps)

                def reduce(h):
                    dve.wait_ge(picks, h + 1)
                    for i in range(2):
                        last = dve.tensor_reduce(pairs[:, i, :, h * TOPK:(h + 1) * TOPK], picked[:, i, :, :, :].rearrange("p t i j -> p t j i"),
                                                 AX_X, ALU.add)
                    last.then_inc(reduced, 1)

                step.mark(dve.tensor_copy(places[:, :, :], core.iota[:, 0:TOPK].unsqueeze(2).broadcast_to([P, TOPK, TOPK])))
                for h in range(PH):
                    b = h % 2
                    rows = [(t, half, scores[:, b, 2 * t + half, :], rest[:, 2 * t + half, :])
                            for t in range(tiles) for half in range(2)]
                    dve.wait_ge(copied, h + 1)
                    for t, half, score, _ in rows:
                        step.mark(dve.max(best[:, t, half, 0:8], score))
                    step.wait()
                    for t, half, score, other in rows:
                        step.mark(dve.max_index(where[:, t, half, 0:8], best[:, t, half, 0:8], score))
                        last = dve.match_replace(other, best[:, t, half, 0:8], score, NEG)
                        step.mark(last)
                    step.wait()
                    dve.sem_inc(searched, 1)
                    for t, half, _, other in rows:
                        step.mark(dve.max(best[:, t, half, 8:16], other))
                    step.wait()
                    for t, half, _, other in rows:
                        step.mark(dve.max_index(where[:, t, half, 8:16], best[:, t, half, 8:16], other))
                    step.mark(dve.tensor_tensor(cand[:, :, :].rearrange("p t (i j) -> p t i j", i=TOPK),
                                                best[:, :, 0, :].unsqueeze(3).broadcast_to(square),
                                                best[:, :, 1, :].unsqueeze(2).broadcast_to(square), ALU.add))
                    if h >= 1:
                        reduce(h - 1)
                    step.wait()
                    for t in range(tiles):
                        step.mark(dve.max(top[:, t, 0:8], cand[:, t, :]))
                    if h >= 2:
                        dve.wait_ge(picks, h - 1)
                    step.mark(dve.tensor_copy(where_f[:, b, :, :, :], where[:, :, :, :]))
                    step.wait()
                    for t in range(tiles):
                        step.mark(dve.max_index(at[:, t, 0:8], top[:, t, 0:8], cand[:, t, :]))
                        step.mark(dve.match_replace(cand_rest[:, t, :], top[:, t, 0:8], cand[:, t, :], NEG))
                    step.wait()
                    for t in range(tiles):
                        step.mark(dve.max(top[:, t, 8:16], cand_rest[:, t, :]))
                    step.wait()
                    for t in range(tiles):
                        step.mark(dve.max_index(at[:, t, 8:16], top[:, t, 8:16], cand_rest[:, t, :]))
                    step.mark(dve.tensor_tensor(pairs[:, 2, :, h * TOPK:(h + 1) * TOPK], top[:, :, :],
                                                top[:, :, 0:1].broadcast_to([P, tiles, TOPK]), ALU.subtract))
                    step.wait()
                    dve.sem_inc(shifted, 1)
                    step.mark(dve.tensor_scalar(digit[:, 0, :, :], at[:, :, :], 4, None, ALU.logical_shift_right))
                    step(dve.tensor_scalar(digit[:, 1, :, :], at[:, :, :], 15, None, ALU.bitwise_and))
                    step(dve.tensor_copy(digit_f[:, :, :, :], digit[:, :, :, :]))
                    for i in range(2):
                        last = dve.tensor_tensor(chosen[:, b, i, :, :, :], digit_f[:, i, :, :].unsqueeze(2).broadcast_to(square),
                                                 places[:, :, :].unsqueeze(1).broadcast_to(square), ALU.is_equal)
                        step.mark(last)
                    step.wait()
                    dve.sem_inc(compared, 1)
                reduce(PH - 1)
                dve.wait_ge(raised, 1)
                weights = pairs[:, 2, :, :].rearrange("p t (h j) -> p (t h) j", j=TOPK)
                step(dve.tensor_reduce(sums[:, :], weights, AX_X, ALU.add))
                step(dve.reciprocal(sums[:, :], sums[:, :]))
                dve.wait_ge(reduced, PH)
                dve.tensor_tensor(weights, weights, sums[:, :].unsqueeze(2).broadcast_to([P, tiles * PH, TOPK]),
                                  ALU.mult).then_inc(raised, 1)

            @st.block.gpsimd
            def _(pool):
                def pick(h):
                    b = h % 2
                    pool.wait_ge(compared, h + 1)
                    if h >= 1:
                        pool.wait_ge(reduced, h)
                    for i in range(2):
                        last = pool.tensor_tensor(picked[:, i, :, :, :], chosen[:, b, i, :, :, :],
                                                  where_f[:, b, :, i, :].unsqueeze(3).broadcast_to(square), ALU.mult)
                    last.then_inc(picks, 1)

                for u in range(seg.n):
                    core.split_next(pool, seg, 0, u, u == seg.n - 1)
                    h = u // UNITS
                    if h >= 2 and u % UNITS == 1:
                        pick(h - 2)
                pick(PH - 2)
                pick(PH - 1)


def split_weights(core, pair_weight, parts):
    with core.stage() as st:
        steps = st.sem()

        @st.block.vector
        def _(dve):
            step = Chain(dve, steps)
            for i in range(3):
                step(dve.tensor_copy(parts[:, i, :], pair_weight))
                if i < 2:
                    step(dve.tensor_tensor(pair_weight, pair_weight, parts[:, i, :], ALU.subtract))


def routing_weights(core, first, keys, pair_keys, weight_parts, tokens, G, mod=None, mod_first=0):
    nc = core.nc
    batches = tokens // OH
    per_loop = 16
    rounds = batches // per_loop
    seg = None if mod is None else core.segments[mod]
    with_units = seg.n // RING if seg else 0
    with ExitStack() as ctx:
        def sb(name, shape):
            return ctx.enter_context(nc.sbuf_tensor(f"{name}_{core.turn}", shape, BF16))

        hot2 = sb("hot2", [P, 2, KEYS, OH])
        hot1 = sb("hot1", [P, 2, keys, OH])
        parts = sb("hot1_parts", [P, 2, 3, keys, OH])
        iotas = sb("iotas", [P, KEYS, OH])
        row = ctx.enter_context(nc.sbuf_tensor(f"mod_row{core.turn}", [2, P], F32))
        with core.stage() as st:
            @st.block.vector
            def _(dve):
                dve.tensor_copy(iotas[:, :, :], core.iota.unsqueeze(2).broadcast_to([P, KEYS, OH]))
        with core.stage() as st:
            built, steps = st.sem(), st.sem()
            multiplied, taken = [st.sem(), st.sem()], [st.sem(), st.sem()]
            row_taken, row_turned = st.sem(), st.sem()

            def batches_of(eng, body):
                for a, b, units in ((0, with_units, True), (with_units, rounds, False)):
                    if b > a:
                        with eng.Fori(a, b, 1) as i:
                            for x in range(per_loop):
                                body(i, x, units)

            if seg:
                @st.block.sync
                def _(sp):
                    core.feed(sp, mod)

            @st.block.vector
            def _(dve):
                dve.sem_inc(multiplied[0], 1)
                dve.sem_inc(multiplied[1], 1)
                def batch(i, x, units):
                    b = x % 2
                    n0 = (i * per_loop + x) * OH
                    three = [P, 3, keys, OH]
                    dve.wait_ge(multiplied[b], i * (per_loop // 2) + x // 2 + 1)
                    dve.tensor_tensor(hot1[:, b, :, :], pair_keys[:, 0, bass.ds(n0, OH)].unsqueeze(1).broadcast_to([P, keys, OH]),
                                      iotas[:, first:first + keys, :], ALU.is_equal).then_inc(steps, 1)
                    dve.tensor_tensor(hot2[:, b, :, :], pair_keys[:, 1, bass.ds(n0, OH)].unsqueeze(1).broadcast_to([P, KEYS, OH]),
                                      iotas[:, :, :], ALU.is_equal).then_inc(built, 1)
                    dve.wait_ge(steps, i * per_loop + x + 1)
                    dve.tensor_tensor(parts[:, b, :, :, :], hot1[:, b, :, :].unsqueeze(1).broadcast_to(three),
                                      weight_parts[:, :, bass.ds(n0, OH)].unsqueeze(2).broadcast_to(three),
                                      ALU.mult).then_inc(built, 1)

                batches_of(dve, batch)
                if seg:
                    core.split_lo(dve, seg.start + seg.n, 0)

            @st.block.tensor
            def _(pe):
                def unit(i, y):
                    u = seg.start + y
                    pe.wait_ge(core.loaded[u % RING], i * 16 + 16 * (u // RING + 1))
                    for kt in range(KT):
                        last = pe.matmul(core.ps[0:2, 6, 0:P], core.silu_c[:, kt, :],
                                         core.ring[:, u % RING, kt * P:(kt + 1) * P],
                                         start=(kt == 0), stop=(kt == KT - 1))
                    last.then_inc(core.units_done, 1)

                def turn(i, y):
                    pe.wait_ge(row_taken, i * RING + y + 1)
                    pe.matmul(core.ps[:, 7, bass.ds((i * RING + y) * 2, 2)], row[:, :], core.ident[0:2, 0:2],
                              start=True, stop=True, skip_group_check=True).then_inc(row_turned, 1)

                def batch(i, x, units):
                    b = x % 2
                    pe.wait_ge(built, (i * per_loop + x) * 2 + 2)
                    pe.wait_ge(taken[b], i * (per_loop // 2) + x // 2 + 1)
                    for n in range(OH):
                        for w in range(3):
                            last = pe.matmul(core.ps[:, b, n * keys:(n + 1) * keys], hot2[:, b, :, n],
                                             parts[:, b, w, :, n], start=(w == 0), stop=(w == 2),
                                             skip_group_check=True)
                    last.then_inc(multiplied[b], 1)
                    if units and x % 4 < 2:
                        (unit, turn)[x % 4](i, x // 4)

                batches_of(pe, batch)

            @st.block.scalar
            def _(act):
                act.sem_inc(taken[0], 1)
                act.sem_inc(taken[1], 1)
                act.sem_inc(row_turned, 1)

                def batch(i, x, units):
                    b = x % 2
                    n0 = (i * per_loop + x) * OH
                    act.wait_ge(multiplied[b], i * (per_loop // 2) + x // 2 + 2)
                    act.activation(G[:, :, bass.ds(n0, OH)],
                                   core.ps[:, b, 0:OH * keys].rearrange("p (n k) -> p k n", n=OH),
                                   ACT.Copy).then_inc(taken[b], 1)
                    if units and x % 4 == 0:
                        y = x // 4
                        act.wait_ge(core.units_done, i * RING + seg.start + y + 3)
                        act.sem_inc(core.hi_done, 2)
                        act.sem_inc(core.split_done, 2)
                        act.wait_ge(row_turned, i * RING + y + 1)
                        act.activation(row[:, :], core.ps[0:2, 6, 0:P], ACT.Copy).then_inc(row_taken, 1)

                batches_of(act, batch)
                if seg:
                    act.wait_ge(row_turned, seg.n + 1)
                    act.activation(core.MOD[:, mod_first:mod_first + seg.n, :],
                                   core.ps[:, 7, 0:2 * seg.n].rearrange("p (f s) -> p f s", s=2), ACT.Copy)
                    core.split_hi(act, seg.start + seg.n, 0)


def expert_inputs(core, k, xs, G, tokens):
    seg = core.segments[k]
    with ExitStack() as ctx:
        act_out = ctx.enter_context(core.nc.sbuf_tensor(f"expert_act{core.turn}", [P, 2, tokens], F32))
        with core.stage() as st:
            raised, used = [st.sem(), st.sem()], [st.sem(), st.sem()]

            @st.block.sync
            def _(sp):
                core.feed(sp, k)

            @st.block.tensor
            def _(pe):
                def unit(it, j, last):
                    b = core.wait_split(pe, seg, it, j)
                    pe.wait_ge(raised[j % 2], it * (BODY // 2) + j // 2 + 1)
                    for kt in range(KT):
                        if kt == KT // 2:
                            core.wait_split(pe, seg, it, j, 1)
                        ins = three_passes(pe, core.ps[:, j % 2, 0:tokens],
                                           core.unit.parts(slice(None), b, slice(kt * P, (kt + 1) * P)),
                                           xs.parts(slice(None), kt, slice(0, tokens)), kt == 0, kt == KT - 1)
                    ins.then_inc(core.units_done, 1)

                run_units(pe, seg.n, unit)

            @st.block.scalar
            def _(act):
                for b in range(2):
                    act.sem_inc(raised[b], 1)
                    act.sem_inc(used[b], 1)

                def unit(it, j, last):
                    core.split_next(act, seg, it, j, last)
                    core.wait_done(act, seg, it, j)
                    act.wait_ge(used[j % 2], it * (BODY // 2) + j // 2 + 1)
                    act.activation(act_out[:, j % 2, :], core.ps[:, j % 2, 0:tokens],
                                   ACT.Gelu_apprx_tanh).then_inc(raised[j % 2], 1)

                run_units(act, seg.n, unit)

            @st.block.vector
            def _(dve):
                def unit(it, j, last):
                    core.split_next(dve, seg, it, j, last)
                    dve.wait_ge(raised[j % 2], it * (BODY // 2) + j // 2 + 2)
                    g = G[:, it * BODY + j, :]
                    dve.tensor_tensor(g, g, act_out[:, j % 2, :], ALU.mult).then_inc(used[j % 2], 1)

                run_units(dve, seg.n, unit)


def expert_outputs(core, k, G, tokens):
    seg = core.segments[k]
    with ExitStack() as ctx:
        g = Split(core.nc, ctx, f"expert_g{core.turn}", [P, 2, tokens])
        with core.stage() as st:
            g_hi, g_split = st.sem(), st.sem()

            @st.block.sync
            def _(sp):
                core.feed(sp, k)

            @st.block.scalar
            def _(act):
                def unit(it, j, last):
                    act.wait_ge(core.units_done, seg.start + j + 1 + it * BODY)
                    act.activation(g.hi[:, j % 2, :], G[:, it * BODY + j, :], ACT.Copy).then_inc(g_hi, 1)
                    core.split_next(act, seg, it, j, last)

                run_units(act, seg.n, unit)

            @st.block.vector
            def _(dve):
                def unit(it, j, last):
                    dve.wait_ge(g_hi, it * BODY + j + 1)
                    minus_hi(dve, g.lo[:, j % 2, :], G[:, it * BODY + j, :], g.hi[:, j % 2, :]).then_inc(g_split, 1)
                    core.split_next(dve, seg, it, j, last)

                run_units(dve, seg.n, unit)

            @st.block.tensor
            def _(pe):
                def unit(it, j, start, stop):
                    b = core.wait_split(pe, seg, it, j)
                    pe.wait_ge(g_split, it * BODY + j + 1)
                    for kt in range(KT):
                        if kt == KT // 2:
                            core.wait_split(pe, seg, it, j, 1)
                        last = three_passes(pe, core.ps[:, kt, 0:tokens],
                                            core.unit.parts(slice(None), b, slice(kt * P, (kt + 1) * P)),
                                            g.parts(slice(None), j % 2, slice(None)), start, stop)
                    last.then_inc(core.units_done, 1)

                rounds = seg.n // BODY
                for j in range(BODY):
                    unit(0, j, j == 0, False)
                with pe.Fori(1, rounds - 1, 1) as it:
                    for j in range(BODY):
                        unit(it, j, False, False)
                for j in range(BODY):
                    unit(rounds - 1, j, False, j == BODY - 1)

def add_outputs(core, YT, X, tokens):
    tiles = tokens // P
    parked = core.parked[:, 0:tiles, :]
    with core.stage() as st:
        scaled, turned, added, stored = (st.sem() for _ in range(4))
        core.dma_count += 16
        fetched = core.dma_count

        @st.block.sync
        def _(sp):
            sp.dma_start(X, parked).then_inc(core.dma_done, 16)
            for t in range(tiles):
                sp.wait_ge(added, t + 1)
                sp.dma_start(parked[:, t, :], X[:, t, :]).then_inc(stored, 16)
            sp.wait_ge(stored, 16 * tiles)

        def scale(eng, kt):
            for s in range(tokens // SEQ):
                to, src = YT[:, kt, s * SEQ:(s + 1) * SEQ], core.ps[:, kt, s * SEQ:(s + 1) * SEQ]
                gate = core.gate2[:, kt, s:s + 1]
                if eng is core.nc.scalar:
                    last = eng.activation(to, src, ACT.Copy, scale=gate)
                else:
                    last = eng.tensor_scalar(to, src, gate, None, ALU.mult)
            last.then_inc(scaled, 1)

        @st.block.scalar
        def _(act):
            for kt in range(0, KT, 2):
                scale(act, kt)

        @st.block.tensor
        def _(pe):
            pe.wait_ge(scaled, KT)
            for t in range(tiles):
                for kt in range(KT):
                    last = pe.transpose(core.ps[:, 2 * t + kt // 4, (kt % 4) * P:(kt % 4 + 1) * P],
                                        YT[:, kt, t * P:(t + 1) * P], core.ident)
                last.then_inc(turned, 1)

        @st.block.vector
        def _(dve):
            for kt in range(1, KT, 2):
                scale(dve, kt)
            dve.wait_ge(core.dma_done, fetched)
            for t in range(tiles):
                dve.wait_ge(turned, t + 1)
                x = X[:, t, :].rearrange("p (h n) -> p h n", h=2)
                dve.tensor_tensor(x, x, core.ps[:, 2 * t:2 * t + 2, :], ALU.add).then_inc(added, 1)


def park(core, store, X):
    parked = core.parked[:, 0:X.shape[1], :]
    small_loads(core, [(parked, X) if store else (X, parked)])


def peer(core, A, layer, k_first, sets):
    nc = core.nc
    tokens = sets * SEQ
    tiles = tokens // P
    with ExitStack() as scope:
        xs = Split(nc, scope, f"peer_xs{layer}", [P, KT, tokens])
        with ExitStack() as ctx:
            core.X = ctx.enter_context(nc.sbuf_tensor(f"peer_x{layer}", [P, tiles, D], F32))
            park(core, False, core.X[:, :, :])
            norm_transpose(core, [(t, t, t // NX) for t in range(tiles)],
                           lambda m, kt: core.gains[:, 1, kt, m:m + 1], lambda m, kt: core.MOD[:, 24 + kt, m:m + 1], xs)
        pair_keys = scope.enter_context(nc.sbuf_tensor(f"pair_keys{layer}", [P, 2, tokens], BF16))
        weight_parts = scope.enter_context(nc.sbuf_tensor(f"weight_parts{layer}", [P, 3, tokens], BF16))
        with ExitStack() as ctx:
            pair_weight = ctx.enter_context(nc.sbuf_tensor(f"pair_weight{layer}", [P, tokens], F32))
            keysT = ctx.enter_context(nc.sbuf_tensor(f"keys{layer}", [P, 32, KEYS], F32))
            core.beside = [(keysT[:, :, :], A[f"keys{layer}"])]
            choose_experts(core, k_first, xs, keysT, tiles, pair_keys, pair_weight)
            split_weights(core, pair_weight[:, :], weight_parts)
        keys = KEYS // PARTS[layer]
        G = scope.enter_context(nc.sbuf_tensor(f"routing{layer}", [P, keys, tokens], F32))
        YT = G[:, 0:KT, :]
        per = D // tokens
        for part in range(PARTS[layer]):
            if layer == 0:
                mod = k_first + 1 + 3 * part
                routing_weights(core, part * keys, keys, pair_keys, weight_parts, tokens, G, mod,
                                part * core.segments[mod].n)
                k = mod + 1
            else:
                routing_weights(core, part * keys, keys, pair_keys, weight_parts, tokens, G)
                k = k_first + 1
            expert_inputs(core, k, xs, G, tokens)
            expert_outputs(core, k + 1, G, tokens)
            X = G[:, KT:KT + per * tiles, :].rearrange("p (t a) b -> p t (a b)", t=tiles)
            add_outputs(core, YT, X, tokens)


def ssm_parameters(core, A, ctx):
    nc = core.nc

    def sb(name, shape):
        return ctx.enter_context(nc.sbuf_tensor(name, shape, F32))

    mag = sb("ssm_mag", [P, STILES])
    phases = sb("ssm_phases", [P, 2, SPAD, 1 << SEED])
    power = sb("ssm_power", [P, 3, LEVELS, SPAD])
    inject = sb("ssm_inject", [P, 16, 2, P])
    readout = sb("ssm_readout", [P, STILES, 2, 32])
    with ExitStack() as tmp:
        def t(name, shape):
            return tmp.enter_context(nc.sbuf_tensor(name, shape, F32))

        lam = t("ssm_lam", [P, 3, STILES])
        b = t("ssm_b", [P, 2, STILES, CG])
        c = t("ssm_c", [P, 2, STILES, CG])
        w = t("ssm_work", [P, 12, STILES])
        wide = t("ssm_wide", [P, 2, STILES, CG])
        small_loads(core, [(lam[:, :, :], A["ssm_lam"]), (b[:, :, :, :], A["ssm_b"]), (c[:, :, :, :], A["ssm_c"])])
        BD = t("ssm_blocks", [P, 2, STILES, 32])
        lr, li, ls = lam[:, 0, :], lam[:, 1, :], lam[:, 2, :]
        with core.stage() as st:
            steps, asteps, ready, sined = (st.sem() for _ in range(4))

            @st.block.scalar
            def _(act):
                step = Chain(act, asteps)
                step(act.activation(w[:, 0, :], ls, ACT.Exp))
                act.wait_ge(ready, 1)
                step(act.activation(mag[:, :], w[:, 1, :], ACT.Exp))
                act.activation(w[:, 4:6, :], w[:, 4:6, :], ACT.Sin).then_inc(sined, 1)

            @st.block.vector
            def _(dve):
                step = Chain(dve, steps)
                step.mark(dve.memset(BD[:, :, :, :], 0.0))
                step.mark(dve.memset(power[:, :, :, STILES:SPAD], 0.0))
                step.mark(dve.memset(phases[:, :, STILES:SPAD, :], 0.0))
                step(dve.memset(readout[:, :, :, :], 0.0))
                dve.wait_ge(asteps, 1)
                step.mark(dve.tensor_tensor(w[:, 1, :], lr, w[:, 0, :], ALU.mult))
                step(dve.tensor_tensor(w[:, 2, :], li, w[:, 0, :], ALU.mult))
                step.mark(dve.tensor_scalar(w[:, 4, :], w[:, 2, :], 0.25 * TWO_PI, None, ALU.add))
                step(dve.tensor_copy(w[:, 5, :], w[:, 2, :]))
                step(dve.tensor_scalar(w[:, 6:8, :], w[:, 4:6, :], 1.0 / TWO_PI, None, ALU.mult))
                step(dve.tensor_scalar(w[:, 6:8, :], w[:, 6:8, :], ROUND, -ROUND, ALU.add, ALU.add))
                for part in (6.28125, 0.0019350051879882812, 3.019916e-07):
                    step(dve.scalar_tensor_tensor(out=w[:, 4:6, :], in0=w[:, 6:8, :], scalar=-part,
                                                  in1=w[:, 4:6, :], op0=ALU.mult, op1=ALU.add))
                step(dve.tensor_scalar(w[:, 4:6, :], w[:, 4:6, :], 3.1415925, -3.1415925, ALU.min, ALU.max))
                dve.engine_nop().then_inc(ready, 1)
                dve.wait_ge(sined, 1)
                cos, sin, nsin = (power[:, i, 0, 0:STILES] for i in range(3))
                step.mark(dve.tensor_copy(cos, w[:, 4, :]))
                step(dve.tensor_copy(sin, w[:, 5, :]))
                step(dve.tensor_scalar(nsin, sin, -1.0, None, ALU.mult))
                for k in range(1, LEVELS):
                    c0, s0 = power[:, 0, k - 1, 0:STILES], power[:, 1, k - 1, 0:STILES]
                    step.mark(dve.tensor_tensor(w[:, 6, :], c0, c0, ALU.mult))
                    step.mark(dve.tensor_tensor(w[:, 7, :], s0, s0, ALU.mult))
                    step(dve.tensor_tensor(w[:, 8, :], c0, s0, ALU.mult))
                    step.mark(dve.tensor_tensor(power[:, 0, k, 0:STILES], w[:, 6, :], w[:, 7, :], ALU.subtract))
                    step.mark(dve.tensor_scalar(power[:, 1, k, 0:STILES], w[:, 8, :], 2.0, None, ALU.mult))
                    step(dve.tensor_scalar(power[:, 2, k, 0:STILES], w[:, 8, :], -2.0, None, ALU.mult))
                a_r, a_i, den, cr, ci, x = (w[:, i, :] for i in (1, 2, 3, 6, 7, 8))
                step.mark(dve.tensor_tensor(a_r, mag[:, :], cos, ALU.mult))
                step.mark(dve.tensor_tensor(a_i, mag[:, :], sin, ALU.mult))
                step.mark(dve.tensor_tensor(den, lr, lr, ALU.mult))
                step(dve.tensor_tensor(x, li, li, ALU.mult))
                step.mark(dve.tensor_scalar(a_r, a_r, -1.0, None, ALU.add))
                step(dve.tensor_tensor(den, den, x, ALU.add))
                step(dve.reciprocal(den, den))
                step.mark(dve.tensor_tensor(cr, a_r, lr, ALU.mult))
                step(dve.tensor_tensor(x, a_i, li, ALU.mult))
                step.mark(dve.tensor_tensor(cr, cr, x, ALU.add))
                step(dve.tensor_tensor(ci, a_i, lr, ALU.mult))
                step(dve.tensor_tensor(x, a_r, li, ALU.mult))
                step(dve.tensor_tensor(ci, ci, x, ALU.subtract))
                step.mark(dve.tensor_tensor(cr, cr, den, ALU.mult))
                step(dve.tensor_tensor(ci, ci, den, ALU.mult))

                def over(y):
                    return y.unsqueeze(2).broadcast_to([P, STILES, CG])

                for part, (p0, p1, op) in enumerate(((cr, ci, ALU.subtract), (ci, cr, ALU.add))):
                    step.mark(dve.tensor_tensor(wide[:, 0, :, :], b[:, 0, :, :], over(p0), ALU.mult))
                    step(dve.tensor_tensor(wide[:, 1, :, :], b[:, 1, :, :], over(p1), ALU.mult))
                    for g in range(2):
                        rows = slice(64 * g, 64 * g + 64)
                        step.mark(dve.tensor_tensor(BD[rows, part, :, g * CG:(g + 1) * CG], wide[rows, 0, :, :],
                                                    wide[rows, 1, :, :], op))
                    step.wait()
                for g in range(2):
                    rows = slice(64 * g, 64 * g + 64)
                    dve.tensor_copy(readout[rows, :, 0, g * CG:(g + 1) * CG], c[rows, 0, :, :])
                    dve.tensor_scalar(readout[rows, :, 1, g * CG:(g + 1) * CG], c[rows, 1, :, :], -1.0, None, ALU.mult)

        with core.stage() as st:
            turned, taken = st.sem(), st.sem()

            @st.block.tensor
            def _(pe):
                for i in range(16):
                    if i >= 2:
                        pe.wait_ge(taken, i - 1)
                    for part in range(2):
                        last = pe.transpose(core.ps[:, i % 2, part * P:(part + 1) * P],
                                            BD[:, part, 4 * i:4 * i + 4, :].rearrange("p q c -> p (q c)"), core.ident)
                    last.then_inc(turned, 1)

            @st.block.scalar
            def _(act):
                for i in range(16):
                    act.wait_ge(turned, i + 1)
                    act.activation(inject[:, i, :, :].rearrange("p r s -> p (r s)"), core.ps[:, i % 2, 0:2 * P],
                                   ACT.Copy).then_inc(taken, 1)
    with ExitStack() as tmp:
        prod = tmp.enter_context(nc.sbuf_tensor("ssm_phase_products", [P, 4, STILES, 1 << (SEED - 1)], F32))
        with core.stage() as st:
            steps = st.sem()

            @st.block.vector
            def _(dve):
                step = Chain(dve, steps)
                tiles = slice(0, STILES)
                step.mark(dve.memset(phases[:, 0, tiles, 0:1], 1.0))
                step(dve.memset(phases[:, 1, tiles, 0:1], 0.0))
                for k in range(SEED):
                    n = 1 << k
                    re, im = phases[:, 0, tiles, 0:n], phases[:, 1, tiles, 0:n]
                    c0, s0 = (power[:, x, k, tiles].unsqueeze(2).broadcast_to([P, STILES, n]) for x in range(2))
                    for x, (a, b) in enumerate(((re, c0), (im, s0), (im, c0), (re, s0))):
                        step.mark(dve.tensor_tensor(prod[:, x, :, 0:n], a, b, ALU.mult))
                    step.wait()
                    step.mark(dve.tensor_tensor(phases[:, 0, tiles, n:2 * n], prod[:, 0, :, 0:n], prod[:, 1, :, 0:n],
                                                ALU.subtract))
                    step(dve.tensor_tensor(phases[:, 1, tiles, n:2 * n], prod[:, 2, :, 0:n], prod[:, 3, :, 0:n], ALU.add))
    return mag, power, phases, inject, readout


def ssm_scan(core, U, mag, power, phases, inject, readout, YD):
    nc = core.nc
    T = 2 * SEQ
    GROUPS = STILES // 4
    with ExitStack() as ctx:
        def sb(name, shape):
            return ctx.enter_context(nc.sbuf_tensor(name, shape, F32))

        u = sb("scan_u", [P, 2, T])
        inj = sb("scan_inject", [P, 2, 2, P])
        rd = sb("scan_readout", [P, 2, 4, 2, 32])
        phase = sb("scan_phase", [P, 4, 2, T])
        part = sb("scan_part", [P, 2, T // 2])
        first_part = sb("scan_first_part", [P, 2, 1 << SEED])
        prod = sb("scan_prod", [P, 2, 4, T])
        turning = sb("scan_turning", [P, 2, 2, T])
        state = sb("scan_state", [P, 2, 2, T])
        back = sb("scan_back", [P, 4, SEQ])
        with core.stage() as st:
            (staged, driven, turned_dve, turned, scanned, back_dve, back_pool, read, kept, parted,
             doubled) = (st.sem() for _ in range(11))

            def pick(t):
                return slice(t, t + 1) if isinstance(t, int) else bass.ds(t, 1)

            def first_step(t, n):
                return isinstance(t, int) and t < n

            def bodies(eng, body):
                body(0, True, False)
                with eng.Fori(1, GROUPS // 2 - 1, 1) as i:
                    body(i, False, False)
                body(GROUPS // 2 - 1, False, True)

            @st.block.scalar
            def _(act):
                def stage(g, b):
                    act.activation(u[:, b, :], U[:, g, :], ACT.Copy)
                    act.activation(inj[:, b, :, :], inject[:, g, :, :], ACT.Copy)
                    act.activation(rd[:, b, :, :, :], readout[:, bass.ds(g * 4, 4), :, :] if not isinstance(g, int)
                                   else readout[:, g * 4:g * 4 + 4, :, :], ACT.Copy).then_inc(staged, 1)

                def start_table(t, b):
                    n = 1 << SEED
                    act.activation(phase[:, b, :, 0:n], phases[:, :, t, :], ACT.Copy).then_inc(parted, 1)
                    act.wait_ge(parted, t * 5 + 1)
                    shares(t, b, SEED, first_part)

                def shares(t, b, k, to):
                    n = 1 << k
                    act.activation(to[:, 0, 0:n], phase[:, b, 1, 0:n], ACT.Copy, scale=power[:, 2, k, pick(t)])
                    act.activation(to[:, 1, 0:n], phase[:, b, 0, 0:n], ACT.Copy,
                                   scale=power[:, 1, k, pick(t)]).then_inc(parted, 1)

                def table(t, b):
                    for k in range(SEED + 1, LEVELS):
                        act.wait_ge(doubled, t * 4 + (k - SEED))
                        shares(t, b, k, part)

                act.sem_inc(read, 2)
                act.sem_inc(kept, 1)
                act.sem_inc(turned_dve, 1)
                act.sem_inc(back_dve, 1)
                act.sem_inc(back_pool, 1)
                stage(0, 0)
                start_table(0, 0)
                table(0, 0)
                start_table(1, 1)

                def body(i, first, last):
                    for x in range(8):
                        t = i * 8 + x
                        if not (last and x == 7):
                            table(t + 1, (x + 1) % 4)
                        if not (last and x >= 6):
                            if not (first and x < 2):
                                act.wait_ge(back_dve, t)
                                act.wait_ge(back_pool, t)
                            start_table(t + 2, (x + 2) % 4)
                        if x % 4 == 1:
                            g, h = i * 2 + x // 4, x // 4
                            if not (first and x == 1):
                                act.wait_ge(read, g * 4 + 2)
                                act.activation(YD[:, g - 1, :], core.ps[:, 4 + (h + 1) % 2, 0:SEQ],
                                               ACT.Copy).then_inc(kept, 1)
                            if not (last and x == 5):
                                stage(g + 1, (h + 1) % 2)

                bodies(act, body)
                act.wait_ge(read, STILES + 2)
                act.activation(YD[:, GROUPS - 1, :], core.ps[:, 5, 0:SEQ], ACT.Copy)

            @st.block.tensor
            def _(pe):
                def drive(t, x):
                    q, b = x % 4, (x // 4) % 2
                    rows = slice(32 * q, 32 * q + 32)
                    for r in range(2):
                        last = pe.matmul(core.ps[:, 2 * (x % 2) + r, :], inj[rows, b, r, :], u[rows, b, :],
                                         start=True, stop=True)
                    last.then_inc(driven, 1)

                def readout_of(x):
                    q, b = x % 4, (x // 4) % 2
                    for n, r in enumerate((0, 0, 1, 1)):
                        last = pe.matmul(core.ps[32 * q:32 * q + 32, 4 + b, 0:SEQ], rd[:, b, q, r, :], back[:, n, :],
                                         start=(n == 0), stop=(n == 3), skip_group_check=True)
                    last.then_inc(read, 1)

                pe.wait_ge(staged, 1)
                drive(0, 0)

                def body(i, first, last):
                    for x in range(8):
                        t = i * 8 + x
                        if not (last and x == 7):
                            pe.wait_ge(turned_dve, t + 1)
                            if x % 4 == 3:
                                pe.wait_ge(staged, i * 2 + x // 4 + 2)
                            drive(t + 1, x + 1)
                        if not (first and x == 0):
                            pe.wait_ge(back_dve, t + 1)
                            pe.wait_ge(back_pool, t + 1)
                            if x % 4 == 1:
                                pe.wait_ge(kept, i * 2 + x // 4)
                            readout_of((x + 7) % 8)

                bodies(pe, body)
                pe.wait_ge(back_dve, STILES + 1)
                pe.wait_ge(back_pool, STILES + 1)
                readout_of(7)

            @st.block.vector
            def _(dve):
                def double(t, b, k):
                    n = 1 << k
                    dve.wait_ge(parted, t * 5 + (k - SEED) + 2)
                    if k > SEED:
                        dve.wait_ge(doubled, t * 4 + (k - SEED))
                    share = first_part if k == SEED else part
                    dve.scalar_tensor_tensor(out=phase[:, b, :, n:2 * n], in0=phase[:, b, :, 0:n],
                                             scalar=power[:, 0, k, pick(t)], in1=share[:, :, 0:n],
                                             op0=ALU.mult, op1=ALU.add).then_inc(doubled, 1)

                late = slice(SEQ, T)

                def scan(t, x, part):
                    dve.wait_ge(turned, t * 2 - 1 + part)
                    if part == 0 and not (first_step(t, 2)):
                        dve.wait_ge(back_dve, t - 1)
                        dve.wait_ge(back_pool, t - 1)
                    b = (x + 1) % 2
                    return dve.tensor_tensor_scan(state[:, b, part, :], mag[:, pick(t - 1)].broadcast_to([P, T]),
                                                  turning[:, b, part, :], 0.0, ALU.mult, ALU.add)

                def turn_back(t, x):
                    dve.wait_ge(scanned, t)
                    dve.wait_ge(read, t + 1)
                    b, p = (x + 1) % 2, (x + 3) % 4
                    dve.tensor_tensor(back[:, 0, :], state[:, b, 0, late], phase[:, p, 0, late], ALU.mult)
                    dve.scalar_tensor_tensor(out=back[:, 1, :], in0=state[:, b, 1, late], scalar=-1.0,
                                             in1=phase[:, p, 1, late], op0=ALU.mult, op1=ALU.mult).then_inc(back_dve, 1)

                for k in range(SEED, LEVELS):
                    double(0, 0, k)

                def body(i, first, last):
                    for x in range(8):
                        t, b = i * 8 + x, x % 2
                        nxt = not (last and x == 7)
                        before = not (first and x == 0)
                        if nxt:
                            double(t + 1, (x + 1) % 4, SEED)
                        dve.wait_ge(driven, t + 1)
                        dve.wait_ge(doubled, t * 4 + 4)
                        dve.tensor_tensor(prod[:, b, 0:2, :], core.ps[:, 2 * b:2 * b + 2, :], phase[:, x % 4, :, :],
                                          ALU.mult)
                        if nxt:
                            double(t + 1, (x + 1) % 4, SEED + 1)
                        dve.tensor_tensor(prod[:, b, 2:4, :], core.ps[:, 2 * b:2 * b + 2, :],
                                          phase[:, x % 4, ::-1, :], ALU.mult).then_inc(turned_dve, 1)
                        if nxt:
                            double(t + 1, (x + 1) % 4, SEED + 2)
                        if before:
                            scan(t, x, 0)
                            scan(t, x, 1).then_inc(scanned, 1)
                            turn_back(t, x)
                        if nxt:
                            double(t + 1, (x + 1) % 4, SEED + 3)

                bodies(dve, body)
                scan(STILES, 8, 0)
                scan(STILES, 8, 1).then_inc(scanned, 1)
                turn_back(STILES, 8)

            @st.block.gpsimd
            def _(pool):
                late = slice(SEQ, T)

                def turn_back(t, x):
                    pool.wait_ge(scanned, t)
                    pool.wait_ge(read, t + 1)
                    b, p = (x + 1) % 2, (x + 3) % 4
                    pool.tensor_tensor(back[:, 2, :], state[:, b, 0, late], phase[:, p, 1, late], ALU.mult)
                    pool.tensor_tensor(back[:, 3, :], state[:, b, 1, late], phase[:, p, 0, late],
                                       ALU.mult).then_inc(back_pool, 1)

                def body(i, first, last):
                    for x in range(8):
                        t, b = i * 8 + x, x % 2
                        pool.wait_ge(turned_dve, t + 2)
                        pool.tensor_tensor(turning[:, b, 0, :], prod[:, b, 0, :], prod[:, b, 1, :],
                                           ALU.add).then_inc(turned, 1)
                        pool.tensor_tensor(turning[:, b, 1, :], prod[:, b, 3, :], prod[:, b, 2, :],
                                           ALU.subtract).then_inc(turned, 1)
                        if not (first and x == 0):
                            turn_back(t, x)

                bodies(pool, body)
                turn_back(STILES, 8)


def ssm_mixer(core, A, k_in, k_out):
    nc = core.nc
    with ExitStack() as ctx:
        def sb(name, shape):
            return ctx.enter_context(nc.sbuf_tensor(name, shape, F32))

        gate_row = sb("ssm_gate_row", [P, 1, D])
        spread_rows(core, 16, 1, gate_row)
        U = sb("ssm_u", [P, 16, 2 * SEQ])
        before = ctx.enter_context(ExitStack())
        xs = Split(nc, before, "ssm_xs", [P, KT, 2 * SEQ])
        with ExitStack() as inner:
            core.X = inner.enter_context(nc.sbuf_tensor("X_second", [P, NT, D], F32))
            park(core, False, core.X[:, :, :])
            norm_transpose(core, [(t, (t + NX) % NT, t // NX) for t in range(NT)],
                           lambda m, kt: core.gains[:, 0, kt, m:m + 1], lambda m, kt: core.MOD[:, kt, m:m + 1], xs)

        def keep(eng, ps, f, slot):
            if eng is core.nc.scalar:
                return eng.activation(U[:, f, :], ps, ACT.Copy)
            return eng.tensor_copy(U[:, f, :], ps)

        product_by_feature(core, k_in, lambda kt: xs.parts(slice(None), kt, slice(None)), 2 * SEQ, keep)
        before.close()
        YD = sb("ssm_y", [P, 16, SEQ])
        with core.stage() as st:
            @st.block.vector
            def _(dve):
                for half in range(2):
                    fwd = U[:, 0:8, half * SEQ:(half + 1) * SEQ]
                    dve.tensor_copy(U[:, 8:16, half * SEQ:(half + 1) * SEQ], fwd[:, :, ::-1])
        with ExitStack() as inner:
            mag, power, phases, inject, readout = ssm_parameters(core, A, inner)
            ssm_scan(core, U, mag, power, phases, inject, readout, YD)
        with core.stage() as st:
            steps, summed = st.sem(), st.sem()

            @st.block.vector
            def _(dve):
                step = Chain(dve, steps)
                step(dve.tensor_tensor(YD[:, 0:8, :], YD[:, 0:8, :], YD[:, 8:16, ::-1], ALU.add))
                for f in range(KT):
                    last = dve.scalar_tensor_tensor(out=YD[:, f, :], in0=U[:, f, SEQ:2 * SEQ],
                                                    scalar=core.columns("ssm_d")[:, f:f + 1], in1=YD[:, f, :],
                                                    op0=ALU.mult, op1=ALU.add)
                last.then_inc(summed, 1)

            @st.block.scalar
            def _(act):
                act.wait_ge(summed, 1)
                act.activation(YD[:, 8:16, :], YD[:, 0:8, :], ACT.Gelu_apprx_tanh)
        X = sb("X_mixed", [P, NX, D])
        core.beside = [(X[:, :, :], core.parked[:, 0:NX, :])]
        ys = Split(nc, ctx, "ssm_ys", [P, KT, SEQ])
        split_tensor(core, YD[:, 8:16, :], ys, 4)
        out = U[:, :, :].rearrange("p (t s a) b -> p t s (a b)", t=NX, s=4)

        def take(eng, c, t, h, ps):
            return eng.activation(out[:, t, c, h * HALF:(h + 1) * HALF], ps, ACT.Sigmoid if c else ACT.Copy)

        product_by_token(core, k_out, lambda c, kt, t: ys.parts(slice(None), kt, slice(t * P, (t + 1) * P)), NX, KT, take,
                         ("scalar", "scalar"))
        with core.stage() as st:
            steps = st.sem()

            @st.block.vector
            def _(dve):
                step = Chain(dve, steps)
                step(dve.tensor_tensor(out[:, :, 0, :], out[:, :, 0, :], out[:, :, 1, :], ALU.mult))
                step(dve.tensor_tensor(out[:, :, 0, :], out[:, :, 0, :],
                                       gate_row[:, :, :].broadcast_to([P, NX, D]), ALU.mult))
                dve.tensor_tensor(X[:, :, :], X[:, :, :], out[:, :, 0, :], ALU.add)
        park(core, True, X[:, :, :])


def program(nc, A, out, stop=99):
    with ExitStack() as ctx:
        core = Core(nc, ctx)

        def sb(name, shape):
            return ctx.enter_context(nc.sbuf_tensor(name, shape, F32))

        core.ring = sb("ring", [P, RING, D])
        core.unit = Split(nc, ctx, "unit", [P, 2, D])
        core.parked = nc.dram_tensor("parked_x", (P, NT, D), F32, kind="Internal").ap()
        core.cols = sb("cols", [P, NCOLS])
        consts = sb("consts", [P, 2 * P])
        core.ident, core.iota = consts[:, 0:P], consts[:, P:2 * P]
        core.silu_c = sb("silu_c", [P, KT, 2])
        core.MOD = sb("mod", [P, 48, 2])
        core.gains = sb("mod_gains", [P, 2, KT, 2])
        core.gate2 = sb("mod_gate2", [P, KT, 2])
        core.ps = ctx.enter_context(nc.psum_tensor("banks", [P, BANKS, HALF], F32))
        start = 0
        for name in SEGMENTS:
            core.segments.append(Segment(A[name], start))
            core.segments[-1].whole = name.startswith("s_ada")
            start += core.segments[-1].n

        with core.stage() as st:
            @st.block.sync
            def _(sp):
                for v in range(RING):
                    sp.dma_start(core.ring[:, v, :], core.segments[0].ap[v]).then_inc(core.loaded[v], 16)

        def tokens_in(name, tiles, scope):
            core.X = scope.enter_context(nc.sbuf_tensor(name, [P, tiles, D], F32))

        with ExitStack() as scope:
            tokens_in("X_first", NT, scope)
            small_loads(core, [(core.X[:, 0:NX, :], A["x"].rearrange("b (t p) d -> p (b t) d", p=P)),
                               (core.cols[:, :], A["cols"]), (consts[:, :], A["k_consts"])])
            with core.stage() as st:
                @st.block.scalar
                def _(act):
                    act.sem_inc(core.units_done, 2)
                    core.split_hi(act, 0, 0)
                    act.activation(core.silu_c[:, :, 0], core.columns("c"), ACT.Silu)
                    act.activation(core.silu_c[:, :, 1], core.columns("cc"), ACT.Silu)

                @st.block.vector
                def _(dve):
                    core.split_lo(dve, 0, 0)
            first_block(core, A)
            finish_modulation(core, "ada_b0")
            chunk_mixer(core, A, 10, 11)
            park(core, True, core.X[:, :, :])
        if stop > 2:
            peer(core, A, 0, 12, 2)
        if stop > 3:
            finish_modulation(core, "ada_b1")
            ssm_mixer(core, A, 19, 20)
        if stop > 4:
            peer(core, A, 1, 21, 1)

        tokens_in("X_last", NT, ctx)
        final = sb("final", [P, NX, D])
        row = sb("final_row", [P, D])
        stat = sb("final_stat", [P, NX])
        small_loads(core, [(core.X[:, :, :], core.parked), (row[:, :], A["gain_rows"][4:5, :].broadcast_to([P, D]))])
        inverse_norms(core, [core.X[:, t, :] for t in range(NX)], stat)
        with core.stage() as st:
            normed, stored = st.sem(), st.sem()

            @st.block.vector
            def _(dve):
                for t in range(NX):
                    dve.scalar_tensor_tensor(out=final[:, t, :], in0=core.X[:, t, :], scalar=stat[:, t:t + 1],
                                             in1=row[:, :], op0=ALU.mult, op1=ALU.mult).then_inc(normed, 1)

            @st.block.sync
            def _(sp):
                sp.wait_ge(normed, NX)
                sp.dma_start(out.rearrange("b (t p) d -> p (b t) d", p=P),
                             final[:, :, :] if stop > 4 else core.X[:, 0:NX, :]).then_inc(stored, 16)
                sp.wait_ge(stored, 16)


SEGMENTS = ["s_features", "s_tokens", "s_ada0_a", "s_ada0_b", "s_w_mlstm", "s_w_diff", "s_w_ret", "s_w_out", "s_ffn_in", "s_ffn_out",
            "s_cm_in", "s_cm_out", "s_wq0", "s_ada1_a", "s_u00", "s_v00", "s_ada1_b", "s_u01",
            "s_v01", "s_ssm_in", "s_ssm_out", "s_wq1", "s_u10", "s_v10"]


def constants():
    f = np.float32
    ident = np.eye(P, dtype=f)
    iota = np.broadcast_to(np.arange(P, dtype=f), (P, P))
    sel = np.zeros((HEADS, HEADS, P), f)
    for h in range(HEADS):
        sel[h, h] = 1.0
    s = np.arange(P)[:, None]
    t = np.concatenate([np.arange(SEQ), np.arange(P)])[None, :]
    lag = (t - s).astype(f)
    scale = f(HD) ** f(-0.5)
    mask = np.where(lag >= 0, scale, 0).astype(f)
    log_gamma = np.log(1.0 - 2.0 ** (-5.0 - np.arange(HEADS, dtype=np.float64)))
    ret = np.where(lag[:, None] >= 0, np.exp(log_gamma[None, :, None] * np.maximum(lag, 0)[:, None]) * scale, 0)
    slopes = 2.0 ** (-8.0 * (np.arange(DH) + 1.0) / DH)
    tq = np.concatenate([np.broadcast_to(s, (P, P)), np.broadcast_to(s + P, (P, SEQ))], 1)
    tk = np.concatenate([np.arange(P), np.arange(SEQ)])[None, :]
    alibi = np.where((tk // 64 <= tq // 64)[:, None], -slopes[None, :, None] * np.abs(tq - tk)[:, None], NEG)

    def sincos(pos, dim):
        omega = (1.0 / (f(10000.0) ** (np.arange(dim // 2, dtype=f) / f(dim // 2)))).astype(f)
        ang = pos[:, None] * omega[None, :]
        return np.concatenate([np.sin(ang), np.cos(ang)], -1)

    grid = 64
    r = np.repeat(np.arange(SEQ // grid, dtype=f), grid)
    c = np.tile(np.arange(grid, dtype=f), SEQ // grid)
    pos = np.concatenate([sincos(r, D // 2), sincos(c, D // 2)], -1).astype(f)
    return {
        "k_consts": np.concatenate([ident, iota], 1),
        "k_sel": sel,
        "k_mask": mask,
        "k_retention": ret.astype(f),
        "k_alibi": alibi.astype(f),
        "k_positions": pos.reshape(NX, P, D).transpose(1, 0, 2),
    }


def layouts(i):
    def column(v):
        return np.reshape(v, (-1, P)).T

    def by_feature(w):
        k, n = w.shape
        return w.reshape(k // P, P, n // P, P).transpose(2, 1, 0, 3).reshape(n // P, P, k)

    def by_token(w):
        k, n = w.shape
        return w.reshape(k // P, P, n // D, D).transpose(2, 0, 1, 3).reshape(-1, P, D)

    w_in = i["w_in"][0]
    cut = dict(zip("mq mk mv mo mif dq dk dv rq rk rv rg gm gd gr".split(),
                   np.split(w_in, np.cumsum([D] * 4 + [8] + [D] * 9), axis=1)))
    g = i["norm_gains"][0]
    pad = np.zeros((P - HEADS,), np.float32)
    ffn = i["w_ffn_in"][0].reshape(D, 2, FT, P).transpose(0, 2, 1, 3).reshape(D, 2 * FFN)
    cols = [column(g[0]), column(g[2]), column(i["norm1_g_2"][0]), column(i["norm1_g_2"][1]),
            column(i["norm2_g_2"][0]), column(i["norm2_g_2"][1]), column(i["ssm_d_2"][0]),
            column(i["ada_b_2"][0]), column(i["ada_b_2"][1]), column(i["mlstm_conv"][0]),
            i["cm_b_s_2"][0].T,
            np.concatenate([i["mlstm_gate_bias"][0, 0], pad])[:, None],
            np.concatenate([i["mlstm_gate_bias"][0, 1], pad])[:, None],
            column(i["c_2"][0]), column(i["c_ctx_2"])]

    def states(v):
        rest = v.shape[3:]
        v = v.reshape(2, 32, 2, 64, *rest)
        v = np.moveaxis(v, (2, 3, 0, 1), (0, 1, 2, 3))
        return v.reshape(P, STILES, *rest)

    step = np.broadcast_to(i["ssm_log_step_2"][0][:, :, None], (2, 64, 64))
    a = {
        "x": i["x"], "ctx": i["ctx_2"],
        "cols": np.concatenate(cols, 1),
        "gain_rows": np.stack([g[1], g[3], i["cm_ln_g_2"][0], i["cm_ln_b_2"][0], i["final_g_2"]]),
        "diff_lambda": i["diff_lambda"].reshape(1, 256), "diff_subln": i["diff_subln"].reshape(1, P),
        "w_gate": cut["mif"].reshape(KT, P, 8).transpose(1, 0, 2),
        "cm_ws": i["cm_w_s_2"][0].transpose(2, 0, 1),
        "s_features": by_feature(np.concatenate([cut[n] for n in ("dq", "dk", "mq", "mk", "rq", "rk")], 1)),
        "s_tokens": by_token(np.concatenate([cut[n] for n in ("mv", "rv", "dv", "mo", "gm", "gd", "gr", "rg")], 1)),
        "s_w_mlstm": by_token(i["w_mlstm_out"][0]), "s_w_diff": by_token(i["w_diff_out"][0]),
        "s_w_ret": by_token(i["w_ret_out"][0]),
        "s_w_out": by_token(i["w_out"][0]),
        "s_ffn_in": by_feature(ffn),
        "s_ffn_out": by_token(i["w_ffn_out"][0]),
        "s_cm_in": by_token(i["cm_w_in_2"][0]),
        "s_cm_out": by_token(i["cm_w_out_2"][0]),
        "s_ssm_in": by_feature(i["ssm_w_in_2"][0]),
        "s_ssm_out": by_token(i["ssm_w_out_2"][0]),
        "ssm_lam": np.stack([states(i["ssm_lam_re_2"][0]), states(i["ssm_lam_im_2"][0]), states(step)], 1),
        "ssm_b": np.stack([states(i["ssm_b_re_2"][0]), states(i["ssm_b_im_2"][0])], 1),
        "ssm_c": np.stack([states(i[n][0].transpose(0, 1, 3, 2)) for n in ("ssm_c_re_2", "ssm_c_im_2")], 1),
    }
    for l in range(2):
        a[f"s_wq{l}"] = by_feature(i["peer_w_q_2"][l])
        a[f"keys{l}"] = i["peer_keys_2"][l].reshape(16, KEYS, 2, P).transpose(3, 0, 2, 1).reshape(P, 32, KEYS)
        u = i["peer_u_2"][l].reshape(KEYS, KEYS, KT, P).transpose(0, 3, 2, 1).reshape(KEYS, P, D)
        v = i["peer_v_2"][l].reshape(KEYS, KEYS, D)
        keys = KEYS // PARTS[l]
        for part in range(PARTS[l]):
            a[f"s_u{l}{part}"] = u[part * keys:(part + 1) * keys]
            a[f"s_v{l}{part}"] = v[part * keys:(part + 1) * keys]
    ada0 = by_token(i["ada_w_2"][0])
    ada1 = by_feature(i["ada_w_2"][1])
    a.update({"s_ada0_a": ada0[0:2 * KT], "s_ada0_b": ada0[2 * KT:], "s_ada1_a": ada1[0:3 * KT], "s_ada1_b": ada1[3 * KT:]})
    a.update(constants())
    return {n: np.ascontiguousarray(v) for n, v in a.items()}


def kernel(**inputs):
    import concourse.bacc as bacc
    from concourse.bass_utils import run_bass_kernel_spmd as run

    laid = layouts({n: np.asarray(v) for n, v in inputs.items()})
    nc = bacc.Bacc("TRN2", target_bir_lowering=False, num_devices=1)
    arrays = {f"in_{n}": v for n, v in laid.items()}
    aps = {n: nc.dram_tensor(f"in_{n}", v.shape, mybir.dt.from_np(v.dtype), kind="ExternalInput").ap()
           for n, v in laid.items()}
    out = nc.dram_tensor("out", (1, SEQ, D), F32, kind="ExternalOutput").ap()
    program(nc, aps, out)
    r = run(nc, [arrays], core_ids=[0])
    return r.results[0]["out"]
```
